# Optimizing a Trainium2 kernel written in Bass

```python
import math
import jax, jax.numpy as jnp
from jax import lax
import numpy as np

D_MODEL = 1024
BATCH = 1
SEQ = 1024
DEPTH = 1
DEC_BATCH = 8
DEC_SEQ = 1
PAST_LEN = 8192
PAGE_SIZE = 128

F32 = jnp.float32
EPS = 1e-6
CHUNK = 64
H_GLA = 6
DK_GLA = 32
DV_GLA = 64
GLA_RANK = 16
GLA_TAU = 16.0
H_DN = 6
DK_DN = 64
DV_DN = 64
CONV_W = 4
CONV_DIM = H_DN * (2 * DK_DN + DV_DN)
H_HG = 4
DK_HG = 64
DV_HG = 64
MIX = H_GLA * DV_GLA + H_DN * DV_DN + H_HG * DV_HG
IN_SIZES = (H_GLA * DK_GLA, H_GLA * DK_GLA, H_GLA * DV_GLA, GLA_RANK, H_GLA * DV_GLA,
            CONV_DIM, H_DN, H_DN, H_DN * DV_DN,
            H_HG * DK_HG, H_HG * DK_HG, H_HG * DV_HG, H_HG * DV_HG)
IN_COLS = 2 * H_GLA * DK_GLA + 2 * H_GLA * DV_GLA + GLA_RANK + CONV_DIM + 2 * H_DN + H_DN * DV_DN + 2 * H_HG * DK_HG + 2 * H_HG * DV_HG
N_GROUPS = 4
EXP_PER_GROUP = 8
N_EXPERTS = N_GROUPS * EXP_PER_GROUP
TOP_K = 2
D_FF_EXPERT = 256

kernel_name = 'hybrid_gla_gdn_hgrn2_hmoe_step'

def _rms_norm(x, g):
    xf = x.astype(F32)
    y = xf * lax.rsqrt(jnp.mean(xf * xf, axis=-1, keepdims=True) + EPS)
    return (y * g.astype(F32)).astype(x.dtype)

def _l2norm(x):
    return x * lax.rsqrt(jnp.sum(x * x, axis=-1, keepdims=True) + EPS)

def _heads(t, h):
    b, l, _ = t.shape
    return t.reshape(b, l, h, -1).transpose(0, 2, 1, 3)

def _unheads(t):
    b, h, l, d = t.shape
    return t.transpose(0, 2, 1, 3).reshape(b, l, h * d)

def _to_chunks(t, c, n):
    b, h, l = t.shape[:3]
    t = jnp.pad(t, [(0, 0), (0, 0), (0, n * c - l)] + [(0, 0)] * (t.ndim - 3))
    t = t.reshape((b, h, n, c) + t.shape[3:])
    return jnp.moveaxis(t, 2, 0)

def _from_chunks(o, l):
    n, b, h, c, d = o.shape
    return jnp.moveaxis(o, 0, 2).reshape(b, h, n * c, d)[:, :, :l]

def _chunk_gla(q, k, v, log_a, s0):
    l = q.shape[2]
    c = min(CHUNK, l)
    n = -(-l // c)
    mask = jnp.tril(jnp.ones((c, c), bool))
    xs = tuple(_to_chunks(t, c, n) for t in (q, k, v, log_a))

    def step(s, inp):
        qc, kc, vc, ac = inp
        bcum = jnp.cumsum(ac, axis=-2)
        o_inter = jnp.einsum('bhcd,bhde->bhce', qc * jnp.exp(bcum), s)
        diff = bcum[..., :, None, :] - bcum[..., None, :, :]
        m3 = mask[:, :, None]
        decay = jnp.where(m3, jnp.exp(jnp.where(m3, diff, 0.0)), 0.0)
        att = jnp.einsum('bhid,bhjd,bhijd->bhij', qc, kc, decay)
        o = o_inter + jnp.einsum('bhij,bhje->bhie', att, vc)
        b_last = bcum[..., -1:, :]
        s = s * jnp.exp(b_last)[..., 0, :, None] + jnp.einsum('bhcd,bhce->bhde', kc * jnp.exp(b_last - bcum), vc)
        return s, o

    s, o = lax.scan(step, s0, xs)
    return _from_chunks(o, l), s

def _chunk_gated_delta(q, k, v, g, beta, s0):
    l = q.shape[2]
    c = min(CHUNK, l)
    n = -(-l // c)
    mask = jnp.tril(jnp.ones((c, c), bool))
    strict = jnp.tril(jnp.ones((c, c), bool), -1)
    eye = jnp.eye(c, dtype=F32)
    xs = tuple(_to_chunks(t, c, n) for t in (q, k, v, g, beta))

    def step(s, inp):
        qc, kc, vc, gc, bc = inp
        gcum = jnp.cumsum(gc, axis=-1)
        gdiff = gcum[..., :, None] - gcum[..., None, :]
        gam = jnp.where(mask, jnp.exp(jnp.where(mask, gdiff, 0.0)), 0.0)
        kb = kc * bc[..., None]
        vb = vc * bc[..., None]
        m = jnp.where(strict, jnp.einsum('bhid,bhjd->bhij', kb, kc) * gam, 0.0)
        tmat = eye + m
        u = lax.linalg.triangular_solve(tmat, vb, left_side=True, lower=True, unit_diagonal=True)
        w = lax.linalg.triangular_solve(tmat, kb * jnp.exp(gcum)[..., None], left_side=True, lower=True, unit_diagonal=True)
        v_new = u - jnp.einsum('bhcd,bhde->bhce', w, s)
        att = jnp.einsum('bhid,bhjd->bhij', qc, kc) * gam
        o = jnp.einsum('bhcd,bhde->bhce', qc * jnp.exp(gcum)[..., None], s) + jnp.einsum('bhij,bhje->bhie', att, v_new)
        g_last = gcum[..., -1:]
        s = s * jnp.exp(g_last)[..., None] + jnp.einsum('bhcd,bhce->bhde', kc * jnp.exp(g_last - gcum)[..., None], v_new)
        return s, o

    s, o = lax.scan(step, s0, xs)
    return _from_chunks(o, l), s

def _gla_group(q, k, v, a_lr, g, wa2, ba, norm_g, s0):
    q = _heads(q, H_GLA).astype(F32) * DK_GLA ** -0.5
    k = _heads(k, H_GLA).astype(F32)
    v = _heads(v, H_GLA).astype(F32)
    log_a = jax.nn.log_sigmoid((a_lr @ wa2 + ba).astype(F32)) / GLA_TAU
    o, s = _chunk_gla(q, k, v, _heads(log_a, H_GLA), s0.astype(F32))
    o = _rms_norm(o, norm_g) * jax.nn.silu(_heads(g, H_GLA).astype(F32))
    return _unheads(o).astype(g.dtype), s

def _deltanet_group(qkv, a, b, g, conv_w, a_log, dt_bias, norm_g, s0, buf):
    l = qkv.shape[1]
    ext = jnp.concatenate([buf.astype(qkv.dtype), qkv], axis=1)
    conv = sum(ext[:, i:i + l] * conv_w[i] for i in range(CONV_W))
    new_buf = ext[:, l:]
    qkv_c = jax.nn.silu(conv.astype(F32))
    q, k, v = jnp.split(qkv_c, [H_DN * DK_DN, 2 * H_DN * DK_DN], axis=-1)
    q = _l2norm(_heads(q, H_DN)) * DK_DN ** -0.5
    k = _l2norm(_heads(k, H_DN))
    v = _heads(v, H_DN)
    beta = jax.nn.sigmoid(b.astype(F32)).transpose(0, 2, 1)
    gdec = (-jnp.exp(a_log.astype(F32)) * jax.nn.softplus(a.astype(F32) + dt_bias.astype(F32))).transpose(0, 2, 1)
    o, s = _chunk_gated_delta(q, k, v, gdec, beta, s0.astype(F32))
    o = _rms_norm(o, norm_g) * jax.nn.silu(_heads(g, H_DN).astype(F32))
    return _unheads(o).astype(g.dtype), s, new_buf

def _hgrn2_group(q, f_pre, i, g, lb, norm_g, s0):
    lbf = lb.astype(F32)
    x = f_pre.astype(F32)
    log_f = jax.nn.log_sigmoid(x) + jnp.log1p(lbf * jnp.exp(-x))
    k = (1.0 - lbf) * jax.nn.sigmoid(-x)
    q = jax.nn.silu(q.astype(F32))
    o, s = _chunk_gla(_heads(q, H_HG), _heads(k, H_HG), _heads(i.astype(F32), H_HG), _heads(log_f, H_HG), s0.astype(F32))
    o = _rms_norm(o * jax.nn.sigmoid(_heads(g, H_HG).astype(F32)), norm_g)
    return _unheads(o).astype(g.dtype), s

def _hier_moe(x, rg_w, rg_b, re_w, re_b, w1, w3, w2):
    t = x.shape[0]
    pg = jax.nn.softmax((x @ rg_w + rg_b).astype(F32), axis=-1)
    pg_top, g_idx = lax.top_k(pg, 1)
    le = (x @ re_w + re_b).astype(F32).reshape(t, N_GROUPS, EXP_PER_GROUP)
    le_sel = jnp.take_along_axis(le, g_idx[:, :, None], axis=1)[:, 0]
    pe = jax.nn.softmax(le_sel, axis=-1)
    v2, i2 = lax.top_k(pe, TOP_K)
    v2 = v2 / jnp.sum(v2, axis=-1, keepdims=True)
    w_in_grp = jnp.sum(jax.nn.one_hot(i2, EXP_PER_GROUP, dtype=F32) * v2[..., None], axis=-2)
    gate = jax.nn.one_hot(g_idx[:, 0], N_GROUPS, dtype=F32)[:, :, None] * (pg_top * w_in_grp)[:, None, :]
    y = jnp.zeros_like(x)
    for gi in range(N_GROUPS):
        e0 = gi * EXP_PER_GROUP
        e1 = e0 + EXP_PER_GROUP
        h = jax.nn.silu(jnp.einsum('td,edf->tef', x, w1[e0:e1])) * jnp.einsum('td,edf->tef', x, w3[e0:e1])
        h = h * gate[:, gi, :, None].astype(x.dtype)
        y = y + jnp.einsum('tef,efd->td', h, w2[e0:e1])
    return y

def _trunk(x, s_gla, s_dn, s_conv, s_hg,
           norm1_g, w_in, gla_wa2, gla_ba, gla_norm_g, dn_conv_w, dn_a_log, dn_dt_bias, dn_norm_g,
           hg_lb_logits, hg_norm_g, w_out, norm2_g, router_g_w, router_g_b, router_e_w, router_e_b,
           exp_w1, exp_w3, exp_w2, final_norm_g):
    b, l, _ = x.shape
    offs = np.cumsum(IN_SIZES)[:-1].tolist()
    sm = jax.nn.softmax(hg_lb_logits.astype(F32), axis=0)
    lb_all = jnp.maximum(jnp.cumsum(sm, axis=0) - sm[0:1], 0.0)
    out_gla, out_dn, out_conv, out_hg = [], [], [], []
    for li in range(DEPTH):
        h = _rms_norm(x, norm1_g[li])
        (g_q, g_k, g_v, g_a, g_g, d_qkv, d_a, d_b, d_g, h_q, h_f, h_i, h_g) = jnp.split(h @ w_in[li], offs, axis=-1)
        o_a, sa = _gla_group(g_q, g_k, g_v, g_a, g_g, gla_wa2[li], gla_ba[li], gla_norm_g[li], s_gla[li])
        o_b, sb, buf = _deltanet_group(d_qkv, d_a, d_b, d_g, dn_conv_w[li], dn_a_log[li], dn_dt_bias[li],
                                       dn_norm_g[li], s_dn[li], s_conv[li])
        o_c, sc = _hgrn2_group(h_q, h_f, h_i, h_g, lb_all[li], hg_norm_g[li], s_hg[li])
        x = x + jnp.concatenate([o_a, o_b, o_c], axis=-1) @ w_out[li]
        h2 = _rms_norm(x, norm2_g[li]).reshape(b * l, D_MODEL)
        x = x + _hier_moe(h2, router_g_w[li], router_g_b[li], router_e_w[li], router_e_b[li],
                          exp_w1[li], exp_w3[li], exp_w2[li]).reshape(b, l, D_MODEL)
        out_gla.append(sa)
        out_dn.append(sb)
        out_conv.append(buf)
        out_hg.append(sc)
    y = _rms_norm(x, final_norm_g)
    return (y, jnp.stack(out_gla).astype(s_gla.dtype), jnp.stack(out_dn).astype(s_dn.dtype),
            jnp.stack(out_conv).astype(s_conv.dtype), jnp.stack(out_hg).astype(s_hg.dtype))

def setup_inputs(seed: int = 0) -> dict:
    key = jax.random.key(seed)
    ks = iter(jax.random.split(key, 40))

    def nrm(shape, s):
        return jax.random.normal(next(ks), shape, F32) * s

    dt = jnp.exp(jax.random.uniform(next(ks), (DEPTH, H_DN), F32, math.log(1e-3), math.log(1e-1)))
    return {
        'x_prompt': nrm((BATCH, SEQ, D_MODEL), 1.0),
        'x_sample': nrm((DEC_BATCH, DEC_SEQ, D_MODEL), 1.0),
        'state_gla': nrm((DEPTH, DEC_BATCH, H_GLA, DK_GLA, DV_GLA), 0.5),
        'state_dn': nrm((DEPTH, DEC_BATCH, H_DN, DK_DN, DV_DN), 0.3),
        'state_conv': nrm((DEPTH, DEC_BATCH, CONV_W - 1, CONV_DIM), 1.0),
        'state_hgrn': nrm((DEPTH, DEC_BATCH, H_HG, DK_HG, DV_HG), 0.5),
        'norm1_g': 1.0 + nrm((DEPTH, D_MODEL), 0.01),
        'w_in': nrm((DEPTH, D_MODEL, IN_COLS), D_MODEL ** -0.5),
        'gla_wa2': nrm((DEPTH, GLA_RANK, H_GLA * DK_GLA), GLA_RANK ** -0.5),
        'gla_ba': nrm((DEPTH, H_GLA * DK_GLA), 0.1),
        'gla_norm_g': 1.0 + nrm((DEPTH, DV_GLA), 0.01),
        'dn_conv_w': nrm((DEPTH, CONV_W, CONV_DIM), CONV_W ** -0.5),
        'dn_a_log': jnp.log(jax.random.uniform(next(ks), (DEPTH, H_DN), F32, 1.0, 16.0)),
        'dn_dt_bias': dt + jnp.log(-jnp.expm1(-dt)),
        'dn_norm_g': 1.0 + nrm((DEPTH, DV_DN), 0.01),
        'hg_lb_logits': nrm((DEPTH, H_HG * DK_HG), 0.1),
        'hg_norm_g': 1.0 + nrm((DEPTH, DV_HG), 0.01),
        'w_out': nrm((DEPTH, MIX, D_MODEL), MIX ** -0.5),
        'norm2_g': 1.0 + nrm((DEPTH, D_MODEL), 0.01),
        'router_g_w': nrm((DEPTH, D_MODEL, N_GROUPS), D_MODEL ** -0.5),
        'router_g_b': nrm((DEPTH, N_GROUPS), 0.01),
        'router_e_w': nrm((DEPTH, D_MODEL, N_EXPERTS), D_MODEL ** -0.5),
        'router_e_b': nrm((DEPTH, N_EXPERTS), 0.01),
        'exp_w1': nrm((DEPTH, N_EXPERTS, D_MODEL, D_FF_EXPERT), D_MODEL ** -0.5),
        'exp_w3': nrm((DEPTH, N_EXPERTS, D_MODEL, D_FF_EXPERT), D_MODEL ** -0.5),
        'exp_w2': nrm((DEPTH, N_EXPERTS, D_FF_EXPERT, D_MODEL), D_FF_EXPERT ** -0.5),
        'final_norm_g': 1.0 + nrm((D_MODEL,), 0.01),
    }

def reference(x_prompt, x_sample, state_gla, state_dn, state_conv, state_hgrn,
              norm1_g, w_in, gla_wa2, gla_ba, gla_norm_g, dn_conv_w, dn_a_log, dn_dt_bias, dn_norm_g,
              hg_lb_logits, hg_norm_g, w_out, norm2_g, router_g_w, router_g_b, router_e_w, router_e_b,
              exp_w1, exp_w3, exp_w2, final_norm_g):
    weights = (norm1_g, w_in, gla_wa2, gla_ba, gla_norm_g, dn_conv_w, dn_a_log, dn_dt_bias, dn_norm_g,
               hg_lb_logits, hg_norm_g, w_out, norm2_g, router_g_w, router_g_b, router_e_w, router_e_b,
               exp_w1, exp_w3, exp_w2, final_norm_g)
    bp = x_prompt.shape[0]
    z_gla = jnp.zeros((DEPTH, bp) + state_gla.shape[2:], state_gla.dtype)
    z_dn = jnp.zeros((DEPTH, bp) + state_dn.shape[2:], state_dn.dtype)
    z_conv = jnp.zeros((DEPTH, bp) + state_conv.shape[2:], state_conv.dtype)
    z_hg = jnp.zeros((DEPTH, bp) + state_hgrn.shape[2:], state_hgrn.dtype)
    y_prompt, gla_p, dn_p, conv_p, hg_p = _trunk(x_prompt, z_gla, z_dn, z_conv, z_hg, *weights)
    y_sample, gla_s, dn_s, conv_s, hg_s = _trunk(x_sample, state_gla, state_dn, state_conv, state_hgrn, *weights)
    return (y_prompt, y_sample, gla_p, dn_p, conv_p, hg_p, gla_s, dn_s, conv_s, hg_s)


_drawn_inputs = setup_inputs


def setup_inputs(seed=0):
    import zlib

    import numpy as np

    out = dict(_drawn_inputs(seed))
    spreads = {}
    factors = {'norm1_g': 2.683,
     'gla_norm_g': 18.301,
     'dn_norm_g': 17.423,
     'hg_norm_g': 4.369,
     'norm2_g': 8.602,
     'router_g_b': 14.803,
     'router_e_b': 4.478,
     'final_norm_g': 31.425}
    for name, (base, spread) in spreads.items():
        noise = np.random.default_rng([zlib.crc32(name.encode()), seed]).standard_normal(out[name].shape)
        drawn = base * np.exp(spread * noise) if base else spread * noise
        out[name] = __import__('jax').numpy.asarray(drawn.astype(out[name].dtype))
    for name, factor in factors.items():
        out[name] = (out[name] * factor).astype(out[name].dtype)
    return out
```

```python
from contextlib import ExitStack
import math

import concourse.bass as bass
from concourse import mybir

ALU = mybir.AluOpType
ACT = mybir.ActivationFunctionType
AX = mybir.AxisListType.X
F32 = mybir.dt.float32
I32 = mybir.dt.int32

P = 128
D = 1024
KC = D // P
SEQ = 1024
NT = SEQ // P
NS = 8
NTT = NT + 1
EPS = 1e-6
H_GLA, DK_GLA, DV = 6, 32, 64
H_DN, DK_DN = 6, 64
H_HG, DK_HG = 4, 64
CONV = H_DN * 3 * 64
CT = CONV // P
IN_COLS = 3740
N_EXP, N_GRP, EPG, FF = 32, 4, 8, 256
LEVELS = 7
CAP = 128
OVER = (2 * (NT * P + NS)) // (CAP + 1) + 1
TILES = N_EXP + OVER
NONE = 4096
CLAMP = -40.0

GQ, GK, GV, GA, GG = 0, 192, 384, 768, 784
DA, DB, DG = 1168, 1174, 1180
HQ, HF, HI, HG = 1564, 1820, 2076, 2332
TOK = 2588
QKV0 = 1168
UNITS = [(0, 0, 512), (512, 512, 512), (1024, 1024, 144), (2320, 1168, 512), (2832, 1680, 512), (3344, 2192, 396)]
LG_H, LG_D, LG_B, LG = 192, 448, 454, 460
DT_ROWS = [128, 64, 128, 128]
DT_COLS = [0, 128, 192, 320]
DT_VALS = [0, 256, 384, 512]
DT_HEADS = [[0, 1, 2, 3], [4, 5], [6, 7], [8, 9]]


def head_place(n):
    if n < H_GLA:
        return n // 4, DK_GLA * (n % 4), DK_GLA, GV + DV * n
    n -= H_GLA
    return 2 + n // 2, DK_HG * (n % 2), DK_HG, HI + DV * n


def shape_constants():
    import numpy as np

    t = np.arange(P)
    j, i = t[:, None], t[None, :]
    f = [np.eye(P)]
    lower, upper = [], []
    for n in range(LEVELS):
        s = 1 << n
        second = (t // s) % 2 == 1
        same = (j // (2 * s)) == (i // (2 * s))
        mid = (t // (2 * s)) * 2 * s + s - 1
        q_part = second[None, :] & (j > mid[None, :]) & (j <= i)
        k_part = ~second[None, :] & (j > i) & (j <= mid[None, :])
        f.append((q_part | k_part).astype(float))
        upper.append(same & second[None, :] & ~second[:, None])
        lower.append(upper[-1].T)
    f += [j <= i, j > i, np.ones((P, P)), -(i > j).astype(float)]
    f.append(np.broadcast_to(np.arange(P)[None, :], (P, P)))
    f.append(np.arange(P)[:, None] // 32 == np.arange(4 * 64)[None, :] // 64)
    f.append(np.arange(P)[:, None] // 64 == np.arange(2 * 64)[None, :] // 64)
    m = lower + upper + [np.eye(P, dtype=bool)]
    m.append(2 * (t[:, None, None] + P * np.arange(NTT)[None, :, None]) + np.arange(2)[None, None, :])
    m[-1] = m[-1].reshape(P, 2 * NTT)
    return (np.ascontiguousarray(np.concatenate(f, 1), np.float32),
            np.ascontiguousarray(np.concatenate(m, 1), np.int32))


C_ID, C_LV = 0, P
C_SUF = P + (LEVELS + 1) * P
C_ONES, C_NST, C_IOTA = C_SUF + P, C_SUF + 2 * P, C_SUF + 3 * P
C_M32, C_M64 = C_IOTA + P, C_IOTA + 3 * P
NCONST = C_M64 + P
M_DST = (2 * LEVELS + 1) * P
NMASK = M_DST + 2 * NTT


def one_table(nc):
    nc.scalar.preload_act_table_set("natural_log_exp_and_others")


def dram_rows(ap, first, n):
    return ap[bass.ds(first, n), :]


def tiles(eng, body, n, unroll=2):
    for t in range(unroll):
        body(t, t % 2)
    with eng.Fori(1, n // unroll) as i:
        for t in range(unroll):
            body(i * unroll + t, t % 2)


def wait_earlier(eng, sem, tile, back, per=1, n=None):
    n = per if n is None else n
    if isinstance(tile, int):
        if tile >= back:
            eng.wait_ge(sem, (tile - back) * per + n)
    else:
        eng.wait_ge(sem, tile * per + (n - back * per))


class stage_semaphores:

    def __init__(self, nc):
        self.nc, self.made = nc, []

    def __enter__(self):
        return self

    def semaphore(self, name):
        self.made.append(self.nc.alloc_semaphore(name=name))
        return self.made[-1]

    def __exit__(self, kind, value, trace):
        if kind is None:
            self.nc.all_engine_barrier()
            self.nc.clear_and_free_semaphores(self.made)
            self.nc.all_engine_barrier()


def build(nc, A, O):
    with ExitStack() as ctx:
        arena = ctx.enter_context(nc.sbuf_tensor("arena", [P, 53200], F32))
        psum = ctx.enter_context(nc.psum_tensor("psum", [P, 8 * 512], F32))
        bank = [psum[:, 512 * n:512 * n + 512] for n in range(8)]
        tok_d = nc.dram_tensor("tok_d", (NT * P + NS, TOK), F32, kind="Internal").ap()
        qkv_d = nc.dram_tensor("qkv_d", (NT * P, CONV), F32, kind="Internal").ap()
        sqkv_d = nc.dram_tensor("sqkv_d", (NS, CONV), F32, kind="Internal").ap()

        x2_d = nc.dram_tensor("x2_d", (NT * P + NS, D), F32, kind="Internal").ap()
        h2_d = nc.dram_tensor("h2_d", (NT * P + NS, D), F32, kind="Internal").ap()
        lg_d = nc.dram_tensor("lg_d", (NT * P + NS, 36), F32, kind="Internal").ap()

        rows_d = nc.dram_tensor("rows_d", (NS * 3400,), F32, kind="Internal").ap()
        y2_d = nc.dram_tensor("y2_d", (2 * (NT * P + NS), D), F32, kind="Internal").ap()
        tab_d = nc.dram_tensor("tab_d", (P * TILES, 1), I32, kind="Internal").ap()
        so_d = nc.dram_tensor("so_d", (NS, D), F32, kind="Internal").ap()

        used = [0]

        def take(n):
            used[0] += n
            assert used[0] <= 53200, used[0]
            return arena[:, used[0] - n:used[0]]

        const = take(NCONST)
        masks = take(NMASK).bitcast(I32)
        consts_in = ctx.enter_context(nc.semaphore("consts_in"))
        mark = used[0]
        with stage_semaphores(nc) as stage:
            project(nc, stage, A, take, bank, const, masks, consts_in, tok_d, qkv_d, sqkv_d)
        used[0] = mark
        with stage_semaphores(nc) as stage:
            mix(nc, stage, A, O, lambda a, b: arena[:, a:b], lambda: used[0], take, psum, bank, const, masks, consts_in, tok_d, qkv_d, sqkv_d, x2_d, h2_d, lg_d, rows_d, so_d)
        used[0] = mark
        with stage_semaphores(nc) as stage:
            experts(nc, stage, A, O, take, bank, const, masks, x2_d, h2_d, lg_d, y2_d, tab_d)


def project(nc, ctx, A, take, bank, const, masks, consts_in, tok_d, qkv_d, sqkv_d):
    ident = const[:, C_ID:C_ID + P]
    w_in = take(KC * IN_COLS).rearrange("p (c n) -> p c n", c=KC)
    g1 = take(KC)
    x = [take(D) for _ in range(2)]
    xs = take(D)
    hT = [take(D).rearrange("p (c t) -> p c t", c=KC) for _ in range(2)]
    tok = [take(TOK) for _ in range(2)]
    qkv = [take(CONV) for _ in range(2)]
    junk = take(D)
    stat = take(8)
    units = [(w, o, n, None) for w, o, n in UNITS] + [(QKV0 + 384 * q, 384 * q, 384, q) for q in range(3)]
    NU = len(units)

    def sem(name):
        return ctx.semaphore(name)

    x_in = [sem(f"x_in{u}") for u in range(2)]
    w_in_in = [sem(f"w_in_in{k}") for k in range(NU)]
    g1_in = sem("g1_in")
    ss_done, lnss_done, rstd_done = sem("ss_done"), sem("lnss_done"), sem("rstd_done")
    xs_done, xsT_done, hT_done = sem("xs_done"), sem("xsT_done"), sem("hT_done")
    unit_done, act_out, dve_out = sem("unit_done"), sem("act_out"), sem("dve_out")
    stored = [sem(f"proj_stored{u}") for u in range(2)]
    eps_set = sem("eps_set")
    xp = A["x_prompt"].rearrange("b s d -> (b s) d")
    xsmp = A["x_sample"].rearrange("b s d -> (b s) d")
    win_v = A["w_in"].rearrange("l (p c) n -> p (l c) n", c=KC)
    ACT_PER, DVE_PER = (NU + 1) // 2, NU // 2

    def wait_unit_out(eng, tile, k, back=0):
        s, per = (act_out, ACT_PER) if k % 2 == 0 else (dve_out, DVE_PER)
        wait_earlier(eng, s, tile, back, per, k // 2 + 1)

    with nc.Block() as block:
        def wait_stored(eng, t, u):
            if isinstance(t, int):
                if t >= 2:
                    eng.wait_ge(stored[u], 32 * (t // 2))
            else:
                eng.wait_ge(stored[u], (t - u) * 16)

        @block.sync
        def _(sp):
            sp.dma_start(const, A["shape_consts"]).then_inc(consts_in, 16)
            sp.dma_start(g1, A["norm1_g"].rearrange("l (p c) -> p (l c)", c=KC)).then_inc(g1_in, 16)

            def load_x(t, u):
                wait_earlier(sp, xs_done, t, 2)
                sp.dma_start(x[u], dram_rows(xp, t * P, P)).then_inc(x_in[u], 16)

            load_x(0, 0)
            for k in (0, 1):
                w, _, n, _ = units[k]
                sp.dma_start(w_in[:, :, w:w + n], win_v[:, :, w:w + n]).then_inc(w_in_in[k], 16)
            load_x(1, 1)
            for k in range(2, NU):
                w, _, n, _ = units[k]
                sp.dma_start(w_in[:, :, w:w + n], win_v[:, :, w:w + n]).then_inc(w_in_in[k], 16)
            sp.dma_start(masks, A["shape_masks"]).then_inc(consts_in, 16)
            with sp.Fori(1, NT // 2) as i:
                load_x(i * 2, 0)
                load_x(i * 2 + 1, 1)
            sp.wait_ge(xs_done, NT - 1)
            sp.dma_start(x[0][0:NS, :], xsmp).then_inc(x_in[0], 16)

        def x_arrived(eng, t, u):
            if isinstance(t, int):
                eng.wait_ge(x_in[u], 16 * (t // 2 + 1))
            else:
                eng.wait_ge(x_in[u], (t - u) * 8 + 16)

        @block.scalar
        def _(act):
            one_table(nc)
            def norm(t, u):
                x_arrived(act, t, u)
                wait_earlier(act, lnss_done, t, 1)
                nc.scalar.activation(junk, x[u], ACT.Square, accum_out=stat[:, 0:1]).then_inc(ss_done, 1)
                act.wait_ge(ss_done, t + 1)
                nc.scalar.activation(stat[:, 1:2], stat[:, 0:1], ACT.Ln, scale=1.0 / D, bias=const_eps).then_inc(lnss_done, 1)
                act.wait_ge(lnss_done, t + 1)
                wait_earlier(act, xs_done, t, 1)
                nc.scalar.activation(stat[:, 2:3], stat[:, 1:2], ACT.Exp, scale=-0.5).then_inc(rstd_done, 1)

            def out(t, u, k):
                _, o, n, q = units[k]
                act.wait_ge(unit_done, t * NU + k + 1)
                if k in (0, 6):
                    wait_stored(act, t, u)
                dst = tok[u][:, o:o + n] if q is None else qkv[u][:, o:o + n]
                nc.scalar.activation(dst, bank[2 + k % 6][:, 0:n], ACT.Copy).then_inc(act_out, 1)

            def body(t, u, last=False):
                if not last:
                    norm(t + 1, 1 - u)
                for k in range(0, NU, 2):
                    out(t, u, k)

            const_eps = stat[:, 7:8]
            act.wait_ge(eps_set, 1)
            norm(0, 0)
            tiles(act, body, NT)
            body(NT, 0, True)

        @block.vector
        def _(dve):
            nc.vector.memset(stat[:, 7:8], EPS).then_inc(eps_set, 1)

            def scale(t, u):
                dve.wait_ge(rstd_done, t + 1)
                wait_earlier(dve, xsT_done, t, 1)
                nc.vector.tensor_scalar(xs, x[u], stat[:, 2:3], None, ALU.mult).then_inc(xs_done, 1)

            def put_hT(t, u):
                dve.wait_ge(xsT_done, t + 1)
                for b in range(2):
                    ins = nc.vector.tensor_tensor(
                        hT[u][:, 4 * b:4 * b + 4, :], bank[b][:, :].rearrange("p (c t) -> p c t", c=4),
                        g1[:, 4 * b:4 * b + 4].unsqueeze(2).to_broadcast([P, 4, P]), ALU.mult)
                ins.then_inc(hT_done, 1)

            def out(t, u, k):
                _, o, n, q = units[k]
                dve.wait_ge(unit_done, t * NU + k + 1)
                if k == 1:
                    wait_stored(dve, t, u)
                dst = tok[u][:, o:o + n] if q is None else qkv[u][:, o:o + n]
                nc.vector.tensor_copy(dst, bank[2 + k % 6][:, 0:n]).then_inc(dve_out, 1)

            def body(t, u, last=False):
                out(t, u, 1)
                if not last:
                    scale(t + 1, 1 - u)
                out(t, u, 3)
                if not last:
                    put_hT(t + 1, 1 - u)
                out(t, u, 5)
                out(t, u, 7)

            scale(0, 0)
            dve.wait_ge(g1_in, 16)
            put_hT(0, 0)
            tiles(dve, body, NT)
            body(NT, 0, True)

        @block.tensor
        def _(pe):
            def transposes(t, u):
                pe.wait_ge(xs_done, t + 1)
                wait_earlier(pe, hT_done, t, 1)
                v = xs.rearrange("p (t c) -> p c t", c=KC)
                for c in range(KC):
                    ins = nc.tensor.transpose(bank[c // 4][:, (c % 4) * P:(c % 4 + 1) * P], v[:, c, :], ident)
                ins.then_inc(xsT_done, 1)

            def unit(t, u, k, column_major=True):
                w, _, n, q = units[k]
                if isinstance(t, int) and t == 0:
                    pe.wait_ge(w_in_in[k], 16)
                if k >= 6:
                    wait_unit_out(pe, t, k - 6)
                else:
                    wait_unit_out(pe, t, k + 6 if k < 3 else k, back=1)
                b = bank[2 + k % 6]
                if q is None or not column_major:
                    for c in range(KC):
                        ins = nc.tensor.matmul(b[:, 0:n], hT[u][:, c, :], w_in[:, c, w:w + n],
                                               start=(c == 0), stop=(c == KC - 1))
                else:
                    for j in range(3):
                        for c in range(KC):
                            ins = nc.tensor.matmul(b[:, j * P:(j + 1) * P], w_in[:, c, w + j * P:w + (j + 1) * P],
                                                   hT[u][:, c, :], start=(c == 0), stop=(c == KC - 1))
                ins.then_inc(unit_done, 1)

            def body(t, u, last=False):
                pe.wait_ge(hT_done, t + 1)
                for k in range(4):
                    unit(t, u, k)
                if not last:
                    transposes(t + 1, 1 - u)
                for k in range(4, NU):
                    unit(t, u, k, not last)

            pe.wait_ge(consts_in, 16)
            transposes(0, 0)
            tiles(pe, body, NT)
            body(NT, 0, True)

        @block.gpsimd
        def _(pool):
            def store(t, u):
                pool.wait_ge(act_out, t * ACT_PER + ACT_PER)
                pool.wait_ge(dve_out, t * DVE_PER + DVE_PER)
                pool.dma_start(dram_rows(tok_d, t * P, P), tok[u]).then_inc(stored[u], 16)
                pool.dma_start(dram_rows(qkv_d, t * P, P), qkv[u]).then_inc(stored[u], 16)

            tiles(pool, store, NT)
            pool.wait_ge(act_out, (NT + 1) * ACT_PER)
            pool.wait_ge(dve_out, (NT + 1) * DVE_PER)
            pool.dma_start(tok_d[NT * P:NT * P + NS, :], tok[0][0:NS, :]).then_inc(stored[0], 16)
            pool.dma_start(sqkv_d, qkv[0][0:NS, :]).then_inc(stored[0], 16)
            pool.wait_ge(stored[0], 32 * (NT // 2 + 1))
            pool.wait_ge(stored[1], 32 * (NT // 2))


def mix(nc, ctx, A, O, arena_cols, used_now, take, psum, bank, const, masks, consts_in, tok_d, qkv_d, sqkv_d, x2_d, h2_d, lg_d, rows_d, so_d):
    ident = const[:, C_ID:C_ID + P]
    lv = const[:, C_LV:C_LV + 8 * P]
    cum = const[:, C_LV + 7 * P:C_LV + 8 * P]
    m32, m64 = const[:, C_M32:C_M32 + 2 * P], const[:, C_M64:C_M64 + P]
    suf = const[:, C_SUF:C_SUF + P]
    ones = const[:, C_ONES:C_ONES + P]
    nstrict = const[:, C_NST:C_NST + P]
    lower = [masks[:, n * P:(n + 1) * P] for n in range(LEVELS)]
    upper = [masks[:, (LEVELS + n) * P:(LEVELS + n + 1) * P] for n in range(LEVELS)]
    diag = masks[:, 2 * LEVELS * P:(2 * LEVELS + 1) * P]
    q_mask = upper + [diag]

    def b3(ap, a, b):
        return ap.unsqueeze(1).to_broadcast([ap.shape[0], a, b])

    def bl(ap, n):
        return ap.unsqueeze(2).to_broadcast([ap.shape[0], ap.shape[1], n])

    def h3(ap, n=64):
        return ap.rearrange("p (h e) -> p h e", e=n)

    w_out = take(KC * D).rearrange("p (c n) -> p c n", c=KC)
    g2, ng, ba = take(D), take(D), take(192)
    scl, ndtb, lb, oml = take(LG), take(6), take(256), take(256)
    wa2 = take(192)
    cw = take(4 * CT).rearrange("p (c i) -> p c i", i=4)
    rw, rb = take(KC * 36).rearrange("p (c n) -> p c n", c=KC), take(36)
    eps, ln8 = take(1), take(1)
    tok = [take(TOK) for _ in range(2)]
    xc = [take(CT * 131).rearrange("p (c t) -> p c t", c=CT) for _ in range(2)]
    z, ab, la, ex, beta = take(LG), take(LG), take(LG), take(466), take(6)
    xe, hk = take(256), take(256)
    sm = hk
    gc, ge = take(1280), take(1280)
    cv, ce = take(CONV), take(CONV)
    cv3 = cv.rearrange("p (c t) -> p c t", c=CT)
    qkv = take(CONV)
    ssd, rs = take(12), take(12)
    kb, vb, kd = take(384), take(384), take(384)
    dqT = take(CONV).rearrange("p (c t) -> p c t", c=CT)
    gt, gtm, gti, nm, atd = take(768), take(768), take(768), take(768), take(768)
    T, U, pm = take(768), take(768), take(768)
    gl = pm
    qk2 = take(1024).rearrange("p (c t) -> p c t", c=8)
    kdg = take(448)
    att = take(1280)
    E = [take(1024) for _ in range(2)]
    zq = [take(896) for _ in range(2)]
    sq_junk = arena_cols(used_now() - 2 * 896, used_now() - 2 * 896 + D)
    zk = [take(896) for _ in range(2)]
    qs, el = take(512), take(4)
    r, vn = take(384), take(384)
    alT = r[:, 0:P]
    oc, x2 = take(D), take(D)
    oT, h2T, sq2 = E[0], E[1], ce
    h2 = oc
    sso, rso, st2 = take(16), take(16), take(4)
    lg = take(36)
    s_lin, s_dn = take(640), take(384)
    masked = zk[0][:, 0:640]

    def region(first, last):
        a, b = first.offset % 53200, last.offset % 53200 + last.shape[-1]
        return arena_cols(a, b)

    big1, big2 = region(gt, pm), region(E[0], zk[1])
    big3 = arena_cols(tok[1].offset % 53200, tok[1].offset % 53200 + 4096)
    sconv, cwb = big2[0:NS, 0:3 * CONV], big1[0:NS, 0:4 * CONV]
    rows = region(r, vn)
    vg, vh, vd = rows[0:48, 0:160], rows[0:32, 160:416], rows[0:48, 416:610]
    sg, sd, sh = big1[0:48, 4096:6144], big1[0:48, 0:4096], big3[0:32, :]
    og, od, oh = ab[0:48, 0:64], ab[0:48, 64:128], ab[0:32, 128:192]
    ks, dn_u = ab[0:48, 192:256], ab[0:48, 256:320]

    sems = {}

    def step(name):
        if name not in sems:
            sems[name] = ctx.semaphore(name)
        return sems[name]

    def done(eng, name, t, n=1, per=1):
        eng.wait_ge(step(name), t * per + n)

    def freed(eng, name, t, back=1, per=1):
        wait_earlier(eng, step(name), t, back, per)

    def loaded(eng, name, t, u):
        eng.wait_ge(step(f"{name}{u}"), (t - u) * 8 + 16)

    params = step("params_in")
    held = {e: step(f"held_{n}") for e, n in ((nc.vector.engine, "dve"), (nc.gpsimd.engine, "pool"), (nc.sync.engine, "sp"))}

    def hold(eng):
        eng.sem_inc(held[eng.engine], 1)

    params_all = [0]
    x_flat = A["x_prompt"].rearrange("b s d -> (b s) d")
    LIN_STEPS = [(dt, pair, half) for dt in range(4) for pair in range(len(DT_HEADS[dt]) // 2) for half in range(2)]
    LIN = len(LIN_STEPS)
    fill = [(1, 1)] * 3 + [(1, 0)] * 4
    order = []
    n = 0
    for level, (a, b) in enumerate(fill):
        order.append(("P", level))
        for _ in range(a):
            order.append(("lin", n))
            n += 1
        order.append(("TU", level))
        for _ in range(b):
            order.append(("lin", n))
            n += 1
    assert n == LIN

    def pair_of(n):
        return psum[:, 512 * n:512 * n + 1024].rearrange("p (b c) -> p b c", b=2)

    def halves(ap):
        return ap.rearrange("p (b c) -> p b c", b=2)

    def by_parity(ap):
        return ap.rearrange("p (c b e) -> p b c e", b=2, e=DV)

    def slot(h):
        return 3 * (h % 2) + h // 2

    def q_of(dt, rows=slice(0, P)):
        return qk2[rows, dt, :]

    def k_of(dt, rows=slice(0, P)):
        return qk2[rows, 4 + dt, :]

    def tail_free(eng, t):
        if isinstance(t, int):
            if t:
                eng.wait_ge(step("tail_stored"), 48 * t)
        else:
            eng.wait_ge(step("tail_stored"), t * 48)

    with nc.Block() as block:
        @block.sync
        def _(sp):
            pb = lambda ap, n=P: ap.partition_broadcast(n)
            loads = [(g2, pb(A["norm2_g"][0])), (ba, pb(A["gla_ba"][0])), (ndtb, pb(A["dn_dt_bias"][0])),
                     (scl[:, LG_D:LG_B], pb(A["dn_a_log"][0])), (sm, pb(A["hg_lb_logits"][0])),
                     (wa2[0:16, :], A["gla_wa2"][0]), (rb[:, 0:4], pb(A["router_g_b"][0])),
                     (rb[:, 4:36], pb(A["router_e_b"][0])),
                     (rw[:, :, 0:4], A["router_g_w"].rearrange("l (p c) n -> p (l c) n", c=KC)),
                     (rw[:, :, 4:36], A["router_e_w"].rearrange("l (p c) n -> p (l c) n", c=KC))]
            loads += [(ng[:, DV * h:DV * (h + 1)], pb(A[n][0]))
                      for h, n in enumerate(["gla_norm_g"] * 6 + ["dn_norm_g"] * 6 + ["hg_norm_g"] * 4)]
            loads += [(cw[:, :, i], A["dn_conv_w"][0, i].rearrange("(c p) -> p c", p=P)) for i in range(4)]

            def load_tile(t, u):
                freed(sp, "slin_mm", t, 2)
                hold(sp)
                sp.dma_start(tok[u], dram_rows(tok_d, t * P, P)).then_inc(step(f"tok_in{u}"), 16)
                freed(sp, "halo", t, 1)
                freed(sp, "cv", t, 2)
                hold(sp)
                sp.dma_start(xc[u][:, :, 3:131], dram_rows(qkv_d, t * P, P).rearrange("p (c t) -> p c t", c=CT)
                             ).then_inc(step(f"xc_in{u}"), 16)

            load_tile(0, 0)
            for dst, src in loads:
                sp.dma_start(dst, src, allow_slow_non_contiguous=True).then_inc(params, 16)
            params_all[0] = 16 * len(loads)
            sp.dma_start(w_out, A["w_out"].rearrange("l (p c) n -> p (l c) n", c=KC)).then_inc(step("w_out_in"), 16)

            def body(t, u, last=False):
                if not last:
                    load_tile(t + 1, 1 - u)
                if not (isinstance(t, int) and t == 0):
                    store_tail(t - 1)
                load_x(t)

            def load_x(t):
                freed(sp, "h2", t)
                hold(sp)
                tail_free(sp, t)
                hold(sp)
                sp.dma_start(x2, dram_rows(x_flat, t * P, P)).then_inc(step("x_in"), 16)

            def store_tail(t):
                done(sp, "x2", t)
                hold(sp)
                sp.dma_start(dram_rows(x2_d, t * P, P), x2).then_inc(step("tail_stored"), 16)
                done(sp, "h2", t)
                hold(sp)
                sp.dma_start(dram_rows(h2_d, t * P, P), h2).then_inc(step("tail_stored"), 16)
                done(sp, "lg", t)
                hold(sp)
                sp.dma_start(dram_rows(lg_d, t * P, P), lg).then_inc(step("tail_stored"), 16)

            for t in range(2):
                body(t, t)
            with sp.Fori(1, NT // 2 - 1) as i:
                body(i * 2, 0)
                body(i * 2 + 1, 1)
            body(NT - 2, 0)
            body(NT - 1, 1, True)
            store_tail(NT - 1)
            done(sp, "s_lin", NT - 1)
            done(sp, "s_dn", NT - 1)
            st = step("states_stored")
            for head in range(10):
                dt, row, K, _ = head_place(head)
                c = DT_VALS[dt] + DV * DT_HEADS[dt].index(head)
                dst = O[2][0, 0, head] if head < H_GLA else O[5][0, 0, head - H_GLA]
                sp.dma_start(dst, s_lin[row:row + K, c:c + DV]).then_inc(st, 16)
            for h in range(H_DN):
                sp.dma_start(O[3][0, 0, h], s_dn[64 * (h % 2):64 * (h % 2) + 64, DV * h:DV * h + DV]).then_inc(st, 16)
            for c in range(CT):
                sp.dma_start(O[4][0, 0, :, c * P:(c + 1) * P].rearrange("r p -> p r"),
                             xc[1][:, c, P:P + 3], allow_slow_non_contiguous=True).then_inc(st, 16)
            freed(sp, "slin_mm", NT, 2)
            sp.dma_start(tok[0][0:NS, :], tok_d[NT * P:NT * P + NS, :]).then_inc(step("tok_in0"), 16)
            done(sp, "tu", NT - 1, 7, 7)
            done(sp, "o2_mm", NT - 1)
            done(sp, "sdn_mm", NT - 1)
            done(sp, "masked_dn", NT - 1)
            done(sp, "s_dn", NT - 1)
            done(sp, "h2T_mm", NT - 1)
            done(sp, "rt_mm", NT - 1)
            sp.wait_ge(st, 16 * (16 + CT))
            sin = step("sconv_in")
            sp.dma_start(cwb, A["dn_conv_w"][0].rearrange("i c -> (i c)").partition_broadcast(NS)).then_inc(sin, 16)
            sp.dma_start(sconv, A["state_conv"][0].rearrange("b r c -> b (r c)")).then_inc(sin, 16)
            sp.dma_start(qkv[0:NS, :], sqkv_d).then_inc(sin, 16)
            sp.dma_start(sh, A["state_hgrn"][0].rearrange("b h k e -> (b h) (k e)")).then_inc(step("sh_in"), 16)
            sp.wait_ge(sin, 48)
            sp.dma_start(O[8][0, :, 0:2, :].rearrange("b r c -> b (r c)"), sconv[:, CONV:3 * CONV]).then_inc(st, 16)
            sp.dma_start(O[8][0, :, 2, :], qkv[0:NS, :]).then_inc(st, 16)
            done(sp, "s_conv", 0)
            sp.dma_start(sg, A["state_gla"][0].rearrange("b h k e -> (b h) (k e)")).then_inc(step("sg_in"), 16)
            sp.dma_start(sd, A["state_dn"][0].rearrange("b h k e -> (b h) (k e)")).then_inc(step("sd_in"), 16)
            done(sp, "s_rows", 0)
            done(sp, "s_ex", 0)
            done(sp, "hk", NT)
            done(sp, "hqs", NT)
            done(sp, "beta", NT)
            R8 = slice(0, NS)
            moves = [(tok[0][R8, GQ:GQ + 192], 6, 32, vg[:, 0:32]), (tok[0][R8, GK:GK + 192], 6, 32, vg[:, 32:64]),
                     (ex[R8, 0:192], 6, 32, vg[:, 64:96]), (tok[0][R8, GV:GV + 384], 6, 64, vg[:, 96:160]),
                     (gc[R8, 1024:1280], 4, 64, vh[:, 0:64]), (hk[R8, :], 4, 64, vh[:, 64:128]),
                     (ex[R8, LG_H:LG_D], 4, 64, vh[:, 128:192]), (tok[0][R8, HI:HI + 256], 4, 64, vh[:, 192:256]),
                     (cv[R8, 0:384], 6, 64, vd[:, 0:64]), (cv[R8, 384:768], 6, 64, vd[:, 64:128]),
                     (cv[R8, 768:1152], 6, 64, vd[:, 128:192]), (ex[R8, LG_D:LG_B], 6, 1, vd[:, 192:193]),
                     (beta[R8, :], 6, 1, vd[:, 193:194])]
            out, back = step("rows_out"), step("rows_back")
            spots = []
            o = 0
            for src, h, d, _ in moves:
                spots.append(rows_d[o:o + NS * h * d])
                sp.dma_start(spots[-1].rearrange("(b c) -> b c", b=NS), src).then_inc(out, 16)
                o += NS * h * d
            sp.wait_ge(out, 16 * len(moves))
            for spot, (_, h, d, dst) in zip(spots, moves):
                sp.dma_start(dst, spot.rearrange("(r d) -> r d", d=d)).then_inc(back, 16)
            done(sp, "s_out", 0, 3)
            sp.dma_start(O[6][0].rearrange("b h k e -> (b h) (k e)"), sg).then_inc(st, 16)
            sp.dma_start(O[7][0].rearrange("b h k e -> (b h) (k e)"), sd).then_inc(st, 16)
            sp.dma_start(O[9][0].rearrange("b h k e -> (b h) (k e)"), sh).then_inc(st, 16)
            for n, (ap, h) in enumerate(((og, 6), (od, 6), (oh, 4))):
                sp.dma_start(so_d[:, 384 * n:384 * n + 64 * h].rearrange("b (h e) -> b h e", e=DV), ap).then_inc(step("o_out"), 16)
            sp.wait_ge(step("o_out"), 48)
            tail_free(sp, NT)
            sp.dma_start(oc[0:NS, :], so_d).then_inc(step("so_in"), 16)
            sp.dma_start(x2[0:NS, :], A["x_sample"].rearrange("b s d -> (b s) d")).then_inc(step("x_in"), 16)
            rows_s = slice(NT * P, NT * P + NS)
            for name, dst, src in (("x2", x2_d, x2), ("h2", h2_d, h2), ("lg", lg_d, lg)):
                done(sp, name, NT)
                sp.dma_start(dst[rows_s, :], src[0:NS, :]).then_inc(step("tail_stored"), 16)
            sp.wait_ge(st, 16 * (16 + CT + 5))
            sp.wait_ge(step("tail_stored"), 48 * (NT + 1))

        @block.gpsimd
        def _(pool):
            g = nc.gpsimd
            g.memset(xc[1][:, :, 128:131], 0.0).then_inc(step("pool_const"), 1)
            g.memset(att, 0.0).then_inc(step("pool_const"), 1)
            pool.wait_ge(step("pool_const"), 2)

            def body(t, u):
                loaded(pool, "tok_in", t, u)
                freed(pool, "ls", t)
                hold(pool)
                g.tensor_copy(z[:, LG_H:LG_D], tok[u][:, HF:HF + 256]).then_inc(step("zf"), 1)
                freed(pool, "cv", t)
                hold(pool)
                g.tensor_copy(xc[u][:, :, 0:3], xc[1 - u][:, :, 128:131]).then_inc(step("halo"), 1)
                done(pool, "la", t)
                freed(pool, "tu_mm", t, 1, 7)
                for b in range(2):
                    ins = g.tensor_tensor(h3(gl[:, 384 * b:384 * b + 384], P), bl(la[:, LG_D + b:LG_B:2], P),
                                          b3(suf, 3, P), ALU.mult)
                ins.then_inc(step("gl"), 1)
                done(pool, "ex", t)
                done(pool, "hk", t)
                freed(pool, "slin_mm", t)
                g.tensor_tensor(kdg[:, 0:192], tok[u][:, GK:GK + 192], ex[:, 0:192], ALU.mult)
                g.tensor_tensor(kdg[:, 192:448], hk, ex[:, LG_H:LG_D], ALU.mult).then_inc(step("kdg"), 1)
                done(pool, "gam_exp", t)
                freed(pool, "atd", t)
                g.tensor_tensor(h3(gtm, P), h3(gt, P), b3(nstrict, 6, P), ALU.mult).then_inc(step("gtm"), 1)
                g.tensor_tensor(h3(gti, P), h3(gt, P), b3(cum, 6, P), ALU.mult).then_inc(step("gti"), 1)
                done(pool, "qkn", t)
                done(pool, "beta", t)
                freed(pool, "r", t)
                g.tensor_tensor(h3(vb), h3(qkv[:, 768:1152]), bl(beta, DV), ALU.mult).then_inc(step("vb"), 1)
                freed(pool, "sdn_mm", t)
                g.tensor_tensor(h3(kd), h3(qkv[:, 384:768]), bl(ex[:, LG_D:LG_B], 64), ALU.mult).then_inc(step("kd"), 1)
                freed(pool, "vn_mm", t)
                hold(pool)
                g.tensor_copy(h3(T, P), b3(ident, 6, P))
                g.tensor_copy(h3(U, P), b3(ident, 6, P)).then_inc(step("tu_init"), 1)
                gates(t)

            def gates(t):
                done(pool, "hqs", t)
                g.tensor_tensor(gc[:, 0:768], gc[:, 0:768], ge[:, 0:768], ALU.mult).then_inc(step("gn1"), 1)
                done(pool, "gn1", t)
                g.tensor_tensor(gc[:, 0:768], gc[:, 0:768], ng[:, 0:768], ALU.mult).then_inc(step("gn"), 1)

            pool.wait_ge(params, params_all[0])
            tiles(pool, body, NT)
            loaded(pool, "tok_in", NT, 0)
            freed(pool, "ls", NT)
            g.tensor_copy(z[:, LG_H:LG_D], tok[0][:, HF:HF + 256]).then_inc(step("zf"), 1)
            gates(NT)

        @block.scalar
        def _(act):
            one_table(nc)
            a = nc.scalar.activation

            act.wait_ge(params, params_all[0])
            a(scl[:, LG_D:LG_B], scl[:, LG_D:LG_B], ACT.Exp).then_inc(step("setup"), 1)
            act.wait_ge(step("lb0"), 1)
            a(lb, lb, ACT.Exp).then_inc(step("lb1"), 1)

            def sigmoid(name, out, src, t, ready):
                done(act, ready, t)
                a(out, src, ACT.Exp, scale=-1.0).then_inc(step(name), 1)
                done(act, name, t, 1, 3)
                a(out, out, ACT.Ln, bias=1.0).then_inc(step(name), 1)
                done(act, name, t, 2, 3)
                a(out, out, ACT.Exp, scale=-1.0).then_inc(step(name), 1)

            def prep(t, late=True):
                done(act, "alT_mm", t)
                a(alT[0:16, :], bank[0][0:16, 0:P], ACT.Copy).then_inc(step("alT"), 1)
                if late:
                    put_oT(t - 1)
                done(act, "z", t)
                done(act, "zf", t)
                freed(act, "ls", t)
                a(ab, z, ACT.Abs).then_inc(step("ab"), 1)
                done(act, "ab", t, 1, 3)
                a(ab, ab, ACT.Exp, scale=-1.0).then_inc(step("ab"), 1)
                done(act, "ab", t, 2, 3)
                a(ab, ab, ACT.Ln, bias=1.0).then_inc(step("ab"), 1)
                done(act, "xe", t)
                a(xe, xe, ACT.Exp, scale=-1.0).then_inc(step("xe_exp"), 1)
                done(act, "xel", t)
                a(xe, xe, ACT.Ln, bias=1.0).then_inc(step("xe_ln"), 1)
                done(act, "hkarg", t)
                a(hk, hk, ACT.Exp).then_inc(step("hk_exp"), 1)
                freed(act, "gn", t)
                sigmoid("ge", ge, gc, t, "gc")
                done(act, "la", t)
                freed(act, "vb", t)
                a(beta, la[:, LG_B:LG], ACT.Exp).then_inc(step("beta"), 1)

            def body(t, u):
                late = not (isinstance(t, int) and t == 0)
                prep(t, late)
                done(act, "sums_mm", t)
                freed(act, "s_dn", t)
                a(ex, bank[0][:, 0:466], ACT.Exp).then_inc(step("ex"), 1)
                freed(act, "sso", t)
                sigmoid("ce", ce, cv, t, "cv")
                done(act, "linT_mm", t)
                freed(act, "lin_mm", t, 1, LIN)
                a(q_of(0), bank[1][:, 0:P], ACT.Copy, scale=DK_GLA ** -0.5)
                a(q_of(1, slice(0, 64)), bank[1][0:64, P:2 * P], ACT.Copy, scale=DK_GLA ** -0.5)
                a(qk2[:, 2:4, :], h3(bank[1][:, 256:512], P), ACT.Copy).then_inc(step("q2"), 1)
                if late:
                    norm2(t - 1)
                done(act, "cvT_mm", t)
                for c in range(3):
                    ins = a(qkv[:, 384 * c:384 * c + 384], bank[3 + c][:, 0:384], ACT.Copy)
                ins.then_inc(step("cvT_out"), 1)
                done(act, "cvT_out", t)
                done(act, "cs", t)
                a(ce[:, 0:768], qkv[:, 0:768], ACT.Square).then_inc(step("sqd"), 1)
                done(act, "gam_mm", t)
                a(halves(gt), pair_of(6)[:, :, 0:384], ACT.Exp).then_inc(step("gam_exp"), 1)
                done(act, "ssd", t)
                a(rs, ssd, ACT.Ln, bias=eps).then_inc(step("rs"), 1)
                done(act, "rs", t, 1, 2)
                a(rs[:, 0:6], rs[:, 0:6], ACT.Exp, scale=-0.5, bias=ln8)
                a(rs[:, 6:12], rs[:, 6:12], ACT.Exp, scale=-0.5).then_inc(step("rs"), 1)
                if late:
                    put_h2T(t - 1)
                done(act, "dqT_mm", t)
                for c in range(3):
                    ins = a(dqT[:, 3 * c:3 * c + 3, :], bank[3 + c][:, 0:384].rearrange("p (c t) -> p c t", c=3), ACT.Copy)
                ins.then_inc(step("dqT_out"), 1)

                def decays(dt):
                    done(act, "cum_mm", t, dt + 1, 4)
                    if dt >= 2:
                        done(act, "zs", t, dt - 1, 4)
                    for b in range(2):
                        ins = a(E[dt % 2][0:DT_ROWS[dt], 512 * b:512 * b + 512], bank[b][0:DT_ROWS[dt], :], ACT.Exp)
                    ins.then_inc(step("e_exp"), 1)

                decays(0)
                for what, n in order:
                    if what == "P":
                        done(act, "p_mm", t, n + 1, 7)
                        a(halves(pm), pair_of(2)[:, :, 0:384], ACT.Copy).then_inc(step("pm"), 1)
                    elif what == "lin" and LIN_STEPS[n][1:] == (0, 0) and LIN_STEPS[n][0] < 3:
                        decays(LIN_STEPS[n][0] + 1)
                done(act, "olin_mm", t)
                freed(act, "h2T_mm", t)
                tail_free(act, t)
                a(oc[:, 0:384], bank[0][:, 0:384], ACT.Copy).then_inc(step("oc_gla"), 1)
                done(act, "vn_mm", t)
                a(vn, bank[2][:, 0:384], ACT.Copy).then_inc(step("vn_out"), 1)
                done(act, "oc_gla", t)
                head_norm(t)

            def head_norm(t):
                done(act, "oc_pre", t)
                a(sq2[:, 0:D], oc, ACT.Square).then_inc(step("sqo"), 1)
                done(act, "sso", t)
                a(rso, sso, ACT.Ln, scale=1.0 / DV, bias=eps).then_inc(step("rso"), 1)
                done(act, "rso", t, 1, 2)
                a(rso, rso, ACT.Exp, scale=-0.5).then_inc(step("rso"), 1)

            def put_oT(t):
                done(act, "oT_mm", t)
                a(oT[:, 0:512], bank[4][:, :], ACT.Copy).then_inc(step("oT_a"), 1)

            def norm2(t):
                done(act, "x2", t)
                freed(act, "h2", t)
                a(sq_junk, x2, ACT.Square, accum_out=st2[:, 0:1]).then_inc(step("sqo_used"), 1)
                done(act, "sqo_used", t)
                a(st2[:, 1:2], st2[:, 0:1], ACT.Ln, scale=1.0 / D, bias=eps).then_inc(step("rs2"), 1)
                done(act, "rs2", t, 1, 2)
                a(st2[:, 2:3], st2[:, 1:2], ACT.Exp, scale=-0.5).then_inc(step("rs2"), 1)

            def put_h2T(t):
                done(act, "h2T_mm", t)
                a(h2T[:, 0:512], bank[1][:, :], ACT.Copy).then_inc(step("h2T_a"), 1)

            def tail(t):
                put_oT(t)
                norm2(t)
                put_h2T(t)

            act.wait_ge(step("setup"), 6)
            tiles(act, body, NT)
            tail(NT - 1)
            prep(NT, False)
            done(act, "la", NT)
            freed(act, "s_dn", NT)
            R8 = slice(0, NS)
            a(ex[R8, 0:LG_B], la[R8, 0:LG_B], ACT.Exp).then_inc(step("s_ex"), 1)
            sigmoid("s_ce", ce[R8, :], cv[R8, :], 0, "s_conv")
            done(act, "s_cs", 0)
            a(ce[R8, 0:768], cv[R8, 0:768], ACT.Square).then_inc(step("s_sq"), 1)
            done(act, "s_ss", 0)
            a(rs[R8, :], ssd[R8, :], ACT.Ln, bias=eps[R8, :]).then_inc(step("s_rs"), 1)
            done(act, "s_rs", 0, 1)
            a(rs[R8, 0:6], rs[R8, 0:6], ACT.Exp, scale=-0.5, bias=ln8[R8, :])
            a(rs[R8, 6:12], rs[R8, 6:12], ACT.Exp, scale=-0.5).then_inc(step("s_rs"), 1)
            head_norm(NT)
            tail(NT)

        @block.vector
        def _(dve):
            v = nc.vector
            tt, ts, cp = v.tensor_tensor, v.tensor_scalar, v.tensor_copy
            setup = step("setup")
            v.memset(eps, EPS)
            v.memset(ln8, math.log(DK_DN ** -0.5))
            v.memset(scl[:, 0:LG_H], 1.0 / 16.0)
            v.memset(scl[:, LG_H:LG_D], 1.0)
            v.memset(scl[:, LG_B:LG], 1.0)
            v.memset(s_lin, 0.0)
            v.memset(s_dn, 0.0).then_inc(setup, 1)
            dve.wait_ge(params, params_all[0])
            ts(ndtb, ndtb, -1.0, None, ALU.mult).then_inc(setup, 1)
            tt(lb, sm, sm, ALU.subtract).then_inc(step("lb0"), 1)
            dve.wait_ge(step("lb1"), 1)
            v.reciprocal(sm, lb).then_inc(step("lb0"), 1)
            dve.wait_ge(step("lb0"), 2)
            tt(sm, sm, lb, ALU.mult).then_inc(step("lb0"), 1)
            dve.wait_ge(step("lb0"), 3)
            tt(lb, sm, sm, ALU.subtract).then_inc(setup, 1)
            dve.wait_ge(setup, 4)
            ts(lb, lb, 0.0, None, ALU.max).then_inc(setup, 1)
            dve.wait_ge(setup, 5)
            ts(oml, lb, -1.0, 1.0, ALU.mult, ALU.add).then_inc(setup, 1)

            def convolve(t, u):
                loaded(dve, "xc_in", t, u)
                done(dve, "halo", t)
                freed(dve, "cvT_mm", t)
                for i in range(4):
                    if i:
                        done(dve, "tap", t, i, 3)
                    for c in range(CT):
                        if i == 0:
                            ins = ts(cv3[:, c, :], xc[u][:, c, 0:P], cw[:, c, 0:1], None, ALU.mult)
                        else:
                            ins = v.scalar_tensor_tensor(cv3[:, c, :], xc[u][:, c, i:i + P], cw[:, c, i:i + 1],
                                                         cv3[:, c, :], ALU.mult, ALU.add)
                    ins.then_inc(step("tap" if i < 3 else "conv"), 1)
                done(dve, "conv", t)
                ts(cv, cv, CLAMP, None, ALU.max).then_inc(step("cv"), 1)

            def prep(t, u):
                loaded(dve, "tok_in", t, u)
                freed(dve, "gn", t)
                freed(dve, "oc", t)
                freed(dve, "linT_mm", t)
                for n, c, w in ((0, GG, 384), (384, DG, 384), (768, HG, 256), (1024, HQ, 256)):
                    ins = ts(gc[:, n:n + w], tok[u][:, c:c + w], CLAMP, None, ALU.max)
                ins.then_inc(step("gc"), 1)
                ts(xe, tok[u][:, HF:HF + 256], CLAMP, None, ALU.max).then_inc(step("xe"), 1)
                v.scalar_tensor_tensor(z[:, LG_D:LG_B], tok[u][:, DA:DA + 6], -1.0, ndtb, ALU.mult, ALU.add)
                cp(z[:, LG_B:LG], tok[u][:, DB:DB + 6])
                done(dve, "z_mm", t)
                tt(z[:, 0:LG_H], bank[1][:, 0:192], ba, ALU.add).then_inc(step("z"), 1)
                if not (isinstance(t, int) and t == NT):
                    if not (isinstance(t, int) and t == 0):
                        put_oT(t - 1)
                    convolve(t, u)
                done(dve, "ab", t, 3, 3)
                freed(dve, "gl", t)
                v.scalar_tensor_tensor(la, z, 0.0, ab, ALU.min, ALU.subtract).then_inc(step("ls"), 1)
                done(dve, "xe_exp", t)
                tt(xe, xe, lb, ALU.mult).then_inc(step("xel"), 1)
                done(dve, "ls", t)
                freed(dve, "kdg", t)
                tt(hk, la[:, LG_H:LG_D], tok[u][:, HF:HF + 256], ALU.subtract).then_inc(step("hkarg"), 1)
                done(dve, "hkarg", t)
                tt(la, la, scl, ALU.mult).then_inc(step("la_scl"), 1)
                done(dve, "la_scl", t)
                done(dve, "xe_ln", t)
                tt(la[:, LG_H:LG_D], la[:, LG_H:LG_D], xe, ALU.add).then_inc(step("la"), 1)
                done(dve, "hk_exp", t)
                tt(hk, hk, oml, ALU.mult).then_inc(step("hk"), 1)
                done(dve, "ge", t, 3, 3)
                tt(gc[:, 1024:1280], gc[:, 1024:1280], ge[:, 1024:1280], ALU.mult).then_inc(step("hqs"), 1)

            def body(t, u):
                prep(t, u)
                done(dve, "ce", t, 3, 3)
                tt(cv, cv, ce, ALU.mult).then_inc(step("cs"), 1)
                late = not (isinstance(t, int) and t == 0)
                if late:
                    residual(t - 1)
                done(dve, "linT_mm", t)
                cp(k_of(0), bank[2][:, 0:P])
                cp(k_of(1, slice(0, 64)), bank[2][0:64, P:2 * P])
                cp(qk2[:, 6:8, :], h3(bank[2][:, 256:512], P)).then_inc(step("k2"), 1)
                if late:
                    norm2(t - 1)
                done(dve, "sqd", t)
                v.tensor_reduce(ssd, h3(ce[:, 0:768]), AX, ALU.add).then_inc(step("ssd"), 1)
                done(dve, "rs", t, 2, 2)
                tt(h3(qkv[:, 0:768]), h3(qkv[:, 0:768]), bl(rs, 64), ALU.mult).then_inc(step("qkn"), 1)
                done(dve, "qkn", t)
                done(dve, "beta", t)
                tt(h3(kb), h3(qkv[:, 384:768]), bl(beta, 64), ALU.mult).then_inc(step("kb"), 1)
                if late:
                    put_h2T(t - 1)
                    logits(t - 1)
                done(dve, "a_mm", t)
                done(dve, "gtm", t)
                tt(halves(nm), pair_of(6)[:, :, 0:384], halves(gtm), ALU.mult).then_inc(step("nm"), 1)
                done(dve, "att_mm", t)
                done(dve, "gti", t)
                tt(halves(atd), pair_of(3)[:, :, 0:384], halves(gti), ALU.mult).then_inc(step("atd"), 1)

                def scaled(dt):
                    R = slice(0, DT_ROWS[dt])
                    done(dve, "e_exp", t, dt + 1, 4)
                    done(dve, "q2", t)
                    done(dve, "k2", t)
                    e3 = h3(E[dt % 2][R, :], P)
                    freed(dve, "olin_mm", t)
                    tt(qs[R, dt * P:dt * P + P], e3[:, 7, :], q_of(dt, R), ALU.mult)
                    cp(el[R, dt:dt + 1], E[dt % 2][R, 1023:1024])
                    tt(h3(zq[dt % 2][R, :], P), e3[:, 0:7, :], b3(q_of(dt, R), 7, P), ALU.mult)
                    tt(h3(zk[dt % 2][R, :], P), e3[:, 0:7, :], b3(k_of(dt, R), 7, P), ALU.mult).then_inc(step("zs"), 1)

                scaled(0)
                for what, n in order:
                    if what == "lin":
                        dt, pair, half = LIN_STEPS[n]
                        done(dve, "lin_mm", t, n + 1, LIN)
                        hold(dve)
                        if n == 0:
                            dve.wait_ge(step("pool_const"), 2)
                        h = DT_HEADS[dt][2 * pair]
                        for j in range(4):
                            if j:
                                done(dve, "lin_put", t, 4 * n + j, 4 * LIN)
                                hold(dve)
                            v.copy_predicated(h3(att[:, h * P:(h + 2) * P], P), b3(q_mask[4 * half + j], 2, P),
                                              pair_of(6)[:, :, j * P:j * P + P]).then_inc(step("lin_put"), 1)
                        if (pair, half) == (0, 0) and dt < 3:
                            scaled(dt + 1)
                    elif what == "TU":
                        done(dve, "tu_mm", t, n + 1, 7)
                        if n == 0:
                            done(dve, "tu_init", t)
                        hold(dve)
                        if n < 6:
                            for b in range(2):
                                v.copy_predicated(h3(T[:, 384 * b:384 * b + 384], P), b3(lower[n], 3, P),
                                                  h3(bank[4 + b][:, 0:384], P))
                        for b in range(2):
                            ins = v.copy_predicated(h3(U[:, 384 * b:384 * b + 384], P), b3(upper[n], 3, P),
                                                    h3(bank[2 + b][:, 0:384], P))
                        ins.then_inc(step("tu"), 1)
                done(dve, "ks_mm", t)
                egc = bl(ex[:, 454:460], DV)
                tt(h3(r), h3(bank[4][:, 0:384]), egc, ALU.mult).then_inc(step("r0"), 1)
                done(dve, "r0", t)
                done(dve, "vb", t)
                tt(r, vb, r, ALU.subtract).then_inc(step("r"), 1)
                freed(dve, "h2T_mm", t)
                tail_free(dve, t)
                tt(h3(oc[:, 384:768]), h3(bank[5][:, 0:384]), egc, ALU.mult).then_inc(step("oc_dn"), 1)
                done(dve, "olin_mm", t)
                tt(oc[:, 768:1024], bank[1][:, 0:256], ge[:, 768:1024], ALU.mult)
                tt(h3(s_dn), h3(s_dn), bl(ex[:, 460:466], DV), ALU.mult).then_inc(step("s_dn0"), 1)
                done(dve, "slin_mm", t)
                tt(masked[:, 0:256], bank[6][:, 0:256], m32, ALU.mult)
                tt(masked[0:64, 256:384], bank[6][0:64, 256:384], m32[0:64, 0:P], ALU.mult)
                tt(masked[:, 384:512], bank[6][:, 384:512], m64, ALU.mult)
                tt(masked[:, 512:640], bank[7][:, 0:P], m64, ALU.mult).then_inc(step("masked"), 1)
                done(dve, "masked", t)
                for dt in range(4):
                    R, C = slice(0, DT_ROWS[dt]), slice(DT_VALS[dt], DT_VALS[dt] + DV * len(DT_HEADS[dt]))
                    ins = v.scalar_tensor_tensor(s_lin[R, C], s_lin[R, C], el[R, dt:dt + 1], masked[R, C],
                                                 ALU.mult, ALU.add)
                ins.then_inc(step("s_lin"), 1)
                done(dve, "o2_mm", t)
                done(dve, "oc_dn", t)
                tt(oc[:, 384:768], oc[:, 384:768], bank[3][:, 0:384], ALU.add).then_inc(step("oc_pre"), 1)
                done(dve, "sdn_mm", t)
                done(dve, "s_dn0", t)
                done(dve, "s_lin", t)
                tt(h3(masked[:, 0:384], P), h3(bank[5][:, 0:384], P), b3(m64, 3, P), ALU.mult).then_inc(step("masked_dn"), 1)
                done(dve, "masked_dn", t)
                tt(s_dn, s_dn, masked[:, 0:384], ALU.add).then_inc(step("s_dn"), 1)
                head_norm(t)

            def head_norm(t):
                done(dve, "sqo", t)
                v.tensor_reduce(sso, h3(sq2[:, 0:D]), AX, ALU.add).then_inc(step("sso"), 1)
                done(dve, "rso", t, 2, 2)
                tt(h3(oc), h3(oc), bl(rso, DV), ALU.mult).then_inc(step("oc_n"), 1)
                done(dve, "oc_n", t)
                done(dve, "gn", t)
                tt(oc[:, 0:768], oc[:, 0:768], gc[:, 0:768], ALU.mult)
                tt(oc[:, 768:1024], oc[:, 768:1024], ng[:, 768:1024], ALU.mult).then_inc(step("oc"), 1)

            def put_oT(t):
                done(dve, "oT_mm", t)
                cp(oT[:, 512:1024], bank[5][:, :]).then_inc(step("oT_b"), 1)

            def residual(t):
                done(dve, "wo_mm", t)
                dve.wait_ge(step("x_in"), t * 16 + 16)
                for b in range(2):
                    ins = tt(x2[:, 512 * b:512 * b + 512], x2[:, 512 * b:512 * b + 512], bank[6 + b][:, :], ALU.add)
                ins.then_inc(step("x2"), 1)

            def norm2(t):
                done(dve, "rs2", t, 2, 2)
                v.scalar_tensor_tensor(h2, x2, st2[:, 2:3], g2, ALU.mult, ALU.mult).then_inc(step("h2"), 1)

            def put_h2T(t):
                done(dve, "h2T_mm", t)
                cp(h2T[:, 512:1024], bank[2][:, :]).then_inc(step("h2T_b"), 1)

            def logits(t):
                done(dve, "rt_mm", t)
                tt(lg, bank[0][:, 0:36], rb, ALU.add).then_inc(step("lg"), 1)

            def tail(t):
                put_oT(t)
                residual(t)
                norm2(t)
                put_h2T(t)
                logits(t)

            dve.wait_ge(setup, 6)
            tiles(dve, body, NT)
            tail(NT - 1)
            prep(NT, 0)
            R8 = slice(0, NS)
            dve.wait_ge(step("sconv_in"), 48)
            n = [0]

            def then(ins):
                ins.then_inc(step("s_chain"), 1)
                n[0] += 1
                dve.wait_ge(step("s_chain"), n[0])

            def cw8(i):
                return cwb[:, i * CONV:(i + 1) * CONV]

            then(tt(cv[R8, :], sconv[:, 0:CONV], cw8(0), ALU.mult))
            for i in range(1, 4):
                src = sconv[:, i * CONV:(i + 1) * CONV] if i < 3 else qkv[R8, :]
                then(tt(ce[R8, :], src, cw8(i), ALU.mult))
                then(tt(cv[R8, :], cv[R8, :], ce[R8, :], ALU.add))
            ts(cv[R8, :], cv[R8, :], CLAMP, None, ALU.max).then_inc(step("s_conv"), 1)
            done(dve, "s_ce", 0, 3)
            tt(cv[R8, :], cv[R8, :], ce[R8, :], ALU.mult).then_inc(step("s_cs"), 1)
            done(dve, "s_sq", 0)
            v.tensor_reduce(ssd[R8, :], h3(ce[R8, 0:768]), AX, ALU.add).then_inc(step("s_ss"), 1)
            done(dve, "s_rs", 0, 2)
            ts(tok[0][R8, GQ:GQ + 192], tok[0][R8, GQ:GQ + 192], DK_GLA ** -0.5, None, ALU.mult)
            tt(h3(cv[R8, 0:768]), h3(cv[R8, 0:768]), bl(rs[R8, :], 64), ALU.mult).then_inc(step("s_rows"), 1)
            dve.wait_ge(step("rows_back"), 16 * 13)

            def over_v(ap, dk):
                return ap.unsqueeze(2).to_broadcast([ap.shape[0], dk, DV])

            def over_k(ap, dk):
                return ap.unsqueeze(1).to_broadcast([ap.shape[0], dk, DV])

            def dot(out, w, s3, tmp, dk):
                then(tt(tmp, s3, over_v(w, dk), ALU.mult))
                return v.tensor_reduce(out, tmp.rearrange("p k e -> p e k"), AX, ALU.add)

            for s2, vec, o, dk, name in ((sg, vg, og, 32, "sg_in"), (sh, vh, oh, 64, "sh_in")):
                n_rows = s2.shape[0]
                s3 = s2.rearrange("p (k e) -> p k e", e=DV)
                tmp = big2[0:n_rows, 0:dk * DV].rearrange("p (k e) -> p k e", e=DV)
                q, k, dec, val = vec[:, 0:dk], vec[:, dk:2 * dk], vec[:, 2 * dk:3 * dk], vec[:, 3 * dk:3 * dk + DV]
                dve.wait_ge(step(name), 16)
                then(tt(s3, s3, over_v(dec, dk), ALU.mult))
                then(tt(tmp, over_v(k, dk), over_k(val, dk), ALU.mult))
                then(tt(s3, s3, tmp, ALU.add))
                dot(o, q, s3, tmp, dk).then_inc(step("s_out"), 1)
                done(dve, "s_out", 0, 1 if dk == 32 else 2)
            s3 = sd.rearrange("p (k e) -> p k e", e=DV)
            tmp = big2[0:48, 0:4096].rearrange("p (k e) -> p k e", e=DV)
            dve.wait_ge(step("sd_in"), 16)
            then(ts(sd, sd, vd[:, 192:193], None, ALU.mult))
            then(dot(ks, vd[:, 64:128], s3, tmp, 64))
            then(tt(dn_u, vd[:, 128:192], ks, ALU.subtract))
            then(ts(dn_u, dn_u, vd[:, 193:194], None, ALU.mult))
            then(tt(tmp, over_v(vd[:, 64:128], 64), over_k(dn_u, 64), ALU.mult))
            then(tt(s3, s3, tmp, ALU.add))
            dot(od, vd[:, 0:64], s3, tmp, 64).then_inc(step("s_out"), 1)
            dve.wait_ge(step("so_in"), 16)
            tt(oc[R8, 768:1024], oc[R8, 768:1024], ge[R8, 768:1024], ALU.mult).then_inc(step("oc_pre"), 1)
            head_norm(NT)
            tail(NT)

        @block.tensor
        def _(pe):
            mm, tr = nc.tensor.matmul, nc.tensor.transpose

            def per_head(out, lhs, rhs):
                for h in (0, 2, 4, 1, 3, 5):
                    b, c = out[h % 2], h // 2
                    ins = mm(b[:, c * P:(c + 1) * P], lhs(h), rhs(h), start=True, stop=True)
                return ins

            def blk(ap, h):
                return ap[:, slot(h) * P:slot(h) * P + P]

            def dn(ap, h):
                return ap[64 * (h % 2):64 * (h % 2) + 64, h // 2, :]

            def low_rank(t, u):
                loaded(pe, "tok_in", t, u)
                freed(pe, "oc_gla", t)
                tr(bank[0][0:16, 0:P], tok[u][:, GA:GA + 16], ident).then_inc(step("alT_mm"), 1)
                freed(pe, "s_dn0", t)
                done(pe, "alT", t)
                mm(bank[1][:, 0:192], alT[0:16, :], wa2[0:16, :], start=True, stop=True).then_inc(step("z_mm"), 1)

            def body(t, u):
                low_rank(t, u)
                late = not (isinstance(t, int) and t == 0)
                if late:
                    turn_o(t - 1)
                    project_o(t - 1)
                done(pe, "la", t)
                mm(bank[0][:, 0:LG_B], suf, la[:, 0:LG_B], start=True, stop=True)
                mm(bank[0][:, 454:460], cum, la[:, LG_D:LG_B], start=True, stop=True)
                mm(bank[0][:, 460:466], ones, la[:, LG_D:LG_B], start=True, stop=True).then_inc(step("sums_mm"), 1)
                done(pe, "hqs", t)
                done(pe, "hk", t)
                freed(pe, "vn_out", t)
                for b, base in ((1, GQ), (2, GK)):
                    tr(bank[b][:, 0:P], tok[u][:, base:base + P], ident)
                    tr(bank[b][0:64, P:2 * P], tok[u][:, base + P:base + 192], ident)
                    src = gc[:, 1024:1280] if b == 1 else hk
                    for c in range(2):
                        ins = tr(bank[b][:, (2 + c) * P:(3 + c) * P], src[:, c * P:(c + 1) * P], ident)
                ins.then_inc(step("linT_mm"), 1)
                done(pe, "cs", t)
                for c in range(CT):
                    ins = tr(bank[3 + c // 3][:, (c % 3) * P:(c % 3 + 1) * P], cv3[:, c, :], ident)
                ins.then_inc(step("cvT_mm"), 1)
                done(pe, "gl", t)
                freed(pe, "x2", t)
                per_head(bank[6:8], lambda h: blk(gl, h), lambda h: cum).then_inc(step("gam_mm"), 1)
                if late:
                    done(pe, "q2", t)
                    done(pe, "k2", t)
                    turn_h2(t - 1)
                done(pe, "kb", t)
                for c in range(CT):
                    src = qkv[:, c * P:(c + 1) * P] if c < 6 else kb[:, (c - 6) * P:(c - 5) * P]
                    ins = tr(bank[3 + c // 3][:, (c % 3) * P:(c % 3 + 1) * P], src, ident)
                ins.then_inc(step("dqT_mm"), 1)
                if late:
                    done(pe, "ex", t)
                    route(t - 1)
                done(pe, "dqT_out", t)
                done(pe, "gam_exp", t)
                qT, kT, kbT = dqT[:, 0:3, :], dqT[:, 3:6, :], dqT[:, 6:9, :]
                per_head(bank[6:8], lambda h: dn(kT, h), lambda h: dn(kbT, h)).then_inc(step("a_mm"), 1)
                per_head(bank[3:5], lambda h: dn(kT, h), lambda h: dn(qT, h)).then_inc(step("att_mm"), 1)

                def sums(dt):
                    done(pe, "ex", t)
                    done(pe, "q2", t)
                    done(pe, "k2", t)
                    freed(pe, "lg", t)
                    if dt:
                        done(pe, "e_exp", t, dt, 4)
                    R = DT_ROWS[dt]
                    for b in range(2):
                        ins = mm(bank[b][0:R, :], la[:, DT_COLS[dt]:DT_COLS[dt] + R], lv[:, 512 * b:512 * b + 512],
                                 start=True, stop=True)
                    ins.then_inc(step("cum_mm"), 1)

                sums(0)
                done(pe, "nm", t)
                done(pe, "atd", t)
                for what, n in order:
                    if what == "P":
                        done(pe, "tu", t, n, 7) if n else done(pe, "tu_init", t)
                        per_head(bank[2:4], lambda h: blk(nm, h), lambda h: blk(T, h)).then_inc(step("p_mm"), 1)
                    elif what == "TU":
                        done(pe, "pm", t, n + 1, 7)
                        if n < 6:
                            per_head(bank[4:6], lambda h: blk(U, h), lambda h: blk(pm, h))
                        per_head(bank[2:4], lambda h: blk(pm, h), lambda h: blk(U, h)).then_inc(step("tu_mm"), 1)
                    else:
                        dt, pair, half = LIN_STEPS[n]
                        if (pair, half) == (0, 0):
                            if dt < 3:
                                sums(dt + 1)
                            done(pe, "zs", t, dt + 1, 4)
                        if n:
                            done(pe, "lin_put", t, 4 * n, 4 * LIN)
                        for m in range(2):
                            _, row, K, _ = head_place(DT_HEADS[dt][2 * pair + m])
                            R = slice(row, row + K)
                            for j in range(4):
                                lvl = 4 * half + j
                                if lvl < 7:
                                    lhs, rhs = zk[dt % 2][R, lvl * P:lvl * P + P], zq[dt % 2][R, lvl * P:lvl * P + P]
                                else:
                                    lhs, rhs = k_of(dt, R), q_of(dt, R)
                                ins = mm(bank[6 + m][:, j * P:j * P + P], lhs, rhs, start=True, stop=True)
                        ins.then_inc(step("lin_mm"), 1)
                freed(pe, "s_dn", t)
                for b, src in ((4, kbT), (5, qT)):
                    for c in range(3):
                        C = slice(c * P, c * P + P)
                        ins = mm(bank[b][:, C], src[:, c, :], s_dn[:, C], start=True, stop=True)
                ins.then_inc(step("ks_mm"), 1)
                done(pe, "e_exp", t, 4, 4)
                done(pe, "zs", t, 4, 4)
                done(pe, "lin_put", t, 4 * LIN, 4 * LIN)
                freed(pe, "s_lin", t)
                for dt in range(4):
                    w, c = DV * len(DT_HEADS[dt]), DT_VALS[dt]
                    b, c = (bank[0], c) if dt < 2 else (bank[1], c - 384)
                    R = slice(0, DT_ROWS[dt])
                    mm(b[:, c:c + w], qs[R, dt * P:dt * P + P], s_lin[R, DT_VALS[dt]:DT_VALS[dt] + w],
                       start=(dt % 2 == 0), stop=False, skip_group_check=True)
                    for m, head in enumerate(DT_HEADS[dt]):
                        vcol = head_place(head)[3]
                        ins = mm(b[:, c + DV * m:c + DV * m + DV], att[:, head * P:head * P + P],
                                 tok[u][:, vcol:vcol + DV], start=False,
                                 stop=(dt % 2 == 1 and m == 1), skip_group_check=True)
                ins.then_inc(step("olin_mm"), 1)
                done(pe, "r", t)
                done(pe, "tu", t, 7, 7)
                for h in range(6):
                    ins = mm(bank[2][:, DV * h:DV * h + DV], blk(U, h), r[:, DV * h:DV * h + DV],
                             start=True, stop=True)
                ins.then_inc(step("vn_mm"), 1)
                done(pe, "kdg", t)
                for dt in range(4):
                    R, w, vcol = DT_ROWS[dt], DV * len(DT_HEADS[dt]), head_place(DT_HEADS[dt][0])[3]
                    o = bank[6][0:R, DT_VALS[dt]:DT_VALS[dt] + w] if dt < 3 else bank[7][:, 0:w]
                    ins = mm(o, kdg[:, DT_COLS[dt]:DT_COLS[dt] + R], tok[u][:, vcol:vcol + w], start=True, stop=True)
                ins.then_inc(step("slin_mm"), 1)
                done(pe, "vn_out", t)
                for h in range(6):
                    ins = mm(bank[3][:, DV * h:DV * h + DV], blk(atd, h), vn[:, DV * h:DV * h + DV],
                             start=True, stop=True)
                ins.then_inc(step("o2_mm"), 1)
                done(pe, "kd", t)
                done(pe, "oc_dn", t)
                for c in range(3):
                    C = slice(c * P, c * P + P)
                    ins = mm(bank[5][:, C], kd[:, C], vn[:, C], start=True, stop=True)
                ins.then_inc(step("sdn_mm"), 1)

            def turn_o(t):
                done(pe, "oc", t)
                if not (isinstance(t, int) and t == NT):
                    done(pe, "s_dn", t)
                v = oc.rearrange("p (t c) -> p c t", c=KC)
                for c in range(KC):
                    ins = tr(bank[4 + c // 4][:, (c % 4) * P:(c % 4 + 1) * P], v[:, c, :], ident)
                ins.then_inc(step("oT_mm"), 1)

            def project_o(t):
                done(pe, "oT_a", t)
                done(pe, "oT_b", t)
                freed(pe, "x2", t)
                for b in range(2):
                    for c in range(KC):
                        ins = mm(bank[6 + b][:, :], oT[:, c * P:c * P + P], w_out[:, c, 512 * b:512 * b + 512],
                                 start=(c == 0), stop=(c == KC - 1))
                ins.then_inc(step("wo_mm"), 1)

            def turn_h2(t):
                done(pe, "h2", t)
                v = h2.rearrange("p (t c) -> p c t", c=KC)
                for c in range(KC):
                    ins = tr(bank[1 + c // 4][:, (c % 4) * P:(c % 4 + 1) * P], v[:, c, :], ident)
                ins.then_inc(step("h2T_mm"), 1)

            def route(t):
                done(pe, "h2T_a", t)
                done(pe, "h2T_b", t)
                for c in range(KC):
                    ins = mm(bank[0][:, 0:36], h2T[:, c * P:c * P + P], rw[:, c, :], start=(c == 0), stop=(c == KC - 1))
                ins.then_inc(step("rt_mm"), 1)

            def tail(t):
                turn_o(t)
                project_o(t)
                turn_h2(t)
                route(t)

            pe.wait_ge(params, params_all[0])
            pe.wait_ge(step("w_out_in"), 16)
            tiles(pe, body, NT)
            tail(NT - 1)
            low_rank(NT, 0)
            tail(NT)

def experts(nc, ctx, A, O, take, bank, const, masks, x2_d, h2_d, lg_d, y2_d, tab_d):
    ident = const[:, C_ID:C_ID + P]
    cum = const[:, C_LV + 7 * P:C_LV + 8 * P]
    ones = const[:, C_ONES:C_ONES + P]
    nbefore = const[:, C_NST:C_NST + P]
    iota = const[:, C_IOTA:C_IOTA + P]
    dst_row = masks[:, M_DST:M_DST + 2 * NTT]
    sems = {}

    def step(name):
        if name not in sems:
            sems[name] = ctx.semaphore(name)
        return sems[name]

    held = {e: step(f"held2_{n}") for e, n in ((nc.vector.engine, "dve"), (nc.gpsimd.engine, "pool"),
                                               (nc.sync.engine, "sp"), (nc.scalar.engine, "act"))}

    def hold(eng):
        eng.sem_inc(held[eng.engine], 1)

    NW = 4
    w13 = [take(KC * 512).rearrange("p (c n) -> p c n", c=KC) for _ in range(NW)]
    w2 = [take(2 * D).rearrange("p (c n) -> p c n", c=2) for _ in range(NW)]
    X = [take(D) for _ in range(NW)]
    xT = [take(D).rearrange("p (c t) -> p c t", c=KC) for _ in range(2)]
    Y = [take(D) for _ in range(NW)]
    h1, sg, hT = take(256), take(256), [take(256) for _ in range(2)]
    idx = [[take(1).bitcast(I32) for _ in range(2)] for _ in range(NW)]
    T2 = 2 * NTT
    lg = take(NTT * 36).rearrange("p (t n) -> p t n", n=36)
    oh, S = take(T2 * 32), take((NTT + 1) * 32)
    tmp = take(T2 * 32)
    d4, e4, sel, cand = take(NTT * 4), take(NTT * 4), take(NTT * 8), take(NTT * 8)
    ohg, ohk = take(NTT * 4), [take(NTT * 8) for _ in range(2)]
    mx, mi, m1, m2, pgt = take(NTT), take(NTT), take(NTT), take(NTT), take(NTT)
    gate = take(T2)
    gate_v = gate.rearrange("p (t k) -> p t k", k=2)
    pos, ex_id, lvl, off, tile_of, addr, cmp = (take(T2) for _ in range(7))
    addr_i = take(T2).bitcast(I32)
    nT, ovT, cmpT = take(1), take(P), take(P)
    over, ovb = take(64), take(OVER * 32)
    ov_exp, ov_exp_i = take(OVER + 1), take(OVER + 1).bitcast(I32)
    table, tokens = take(TILES).bitcast(I32), take(TILES).bitcast(I32)
    x2 = [take(D) for _ in range(2)]
    y2 = [w2[n].rearrange("p c n -> p (c n)") for n in range(2)]
    fg, fo, fs = take(D), [take(D) for _ in range(2)], take(8)
    eps = take(1)

    def load_w(eng, e, buf, sem):
        eng.dma_start(w13[buf][:, :, 0:256], A["exp_w1"][0, e].rearrange("(p c) n -> p c n", c=KC)).then_inc(sem, 16)
        eng.dma_start(w13[buf][:, :, 256:512], A["exp_w3"][0, e].rearrange("(p c) n -> p c n", c=KC)).then_inc(sem, 16)
        eng.dma_start(w2[buf], A["exp_w2"][0, e].rearrange("(c p) n -> p c n", c=2)).then_inc(sem, 16)

    def weights_in(b):
        return step(f"weights_in{b}")

    def bcast(ap, n, dim=2):
        return ap.unsqueeze(dim).to_broadcast([P] + list(ap.shape[1:dim]) + [n] + list(ap.shape[dim:]))

    with nc.Block() as block:
        @block.sync
        def _(sp):
            sp.wait_ge(step("lg_zero"), 2)
            sp.dma_start(lg[:, 0:NT, :], lg_d[0:NT * P, :].rearrange("(t p) n -> p t n", p=P)).then_inc(step("lg_in"), 16)
            sp.dma_start(lg[0:NS, NT, :], lg_d[NT * P:NT * P + NS, :]).then_inc(step("lg_in"), 16)
            sp.dma_start(tab_d.rearrange("(p t) o -> p (t o)", p=P), table).then_inc(step("table_empty"), 16)
            for e in range(NW):
                load_w(sp, e, e, weights_in(e))
            sp.dma_start(fg, A["final_norm_g"].partition_broadcast(P)).then_inc(step("fg_in"), 16)
            sp.wait_ge(step("table_put"), 16 * T2)
            sp.dma_start(table, tab_d.rearrange("(p t) o -> p (t o)", p=P)).then_inc(step("table_in"), 16)

        @block.gpsimd
        def _(pool):
            pool.wait_ge(step("addr"), 1)
            pool.wait_ge(step("table_empty"), 16)
            for n in range(T2):
                pool.indirect_dma_start(tab_d, bass.IndirectOffsetOnAxis(ap=addr_i[:, n:n + 1], axis=0),
                                        dst_row[:, n:n + 1], None, bounds_check=P * TILES - 1,
                                        oob_is_err=False).then_inc(step("table_put"), 16)

        @block.scalar
        def _(act):
            one_table(nc)
            act.wait_ge(step("d4"), 1)
            nc.scalar.activation(e4, d4, ACT.Exp).then_inc(step("e4"), 1)
            act.wait_ge(step("d12"), 1)
            nc.scalar.activation(m2, m2, ACT.Exp).then_inc(step("ed"), 1)

        @block.tensor
        def _(pe):
            mm = nc.tensor.matmul
            pe.wait_ge(step("S"), 1)
            mm(bank[0][:, 0:(NTT + 1) * 32], cum, S, start=True, stop=False, skip_group_check=True)
            for t in range(NTT):
                ins = mm(bank[0][:, (t + 1) * 32:(NTT + 1) * 32], ones,
                         S[:, t * 32:t * 32 + 32].unsqueeze(1).to_broadcast([P, NTT - t, 32]),
                         start=False, stop=(t == NTT - 1), skip_group_check=True)
            ins.then_inc(step("pos_mm"), 1)
            for t in range(NTT):
                ins = mm(bank[1][0:32, 0:P], S[:, t * 32:t * 32 + 32], ones, start=(t == 0), stop=(t == NTT - 1))
            ins.then_inc(step("n_mm"), 1)
            pe.wait_ge(step("ovT"), 1)
            mm(bank[2][:, 0:32], ovT[0:32, :], nbefore[0:32, 0:32], start=True, stop=True)
            mm(bank[2][:, 32:64], ovT[0:32, :], ident[0:32, 0:32], start=True, stop=True)
            mm(bank[2][:, 64:65], ovT[0:32, :], ones[0:32, 0:1], start=True, stop=True).then_inc(step("over_mm"), 1)

        @block.vector
        def _(dve):
            v = nc.vector
            tt, ts, red = v.tensor_tensor, v.tensor_scalar, v.tensor_reduce
            n = [0]

            def then(ins):
                ins.then_inc(step("r_chain"), 1)
                n[0] += 1
                dve.wait_ge(step("r_chain"), n[0])

            v.memset(lg[:, NT, :], 0.0).then_inc(step("lg_zero"), 1)
            v.memset(S[:, NTT * 32:], 0.0)
            for b in range(NW):
                v.memset(X[b], 0.0)
            v.memset(eps, EPS)
            v.memset(table, NONE).then_inc(step("lg_zero"), 1)
            dve.wait_ge(step("lg_in"), 32)

            def t3(ap, k):
                return ap.rearrange("p (t k) -> p t k", k=k)

            def first_max(out, ap, k, mx):
                then(red(mx, ap, AX, ALU.max))
                then(tt(t3(cand[:, 0:NTT * k], k), ap, bcast(mx, k), ALU.is_ge))
                then(v.scalar_tensor_tensor(t3(cand[:, 0:NTT * k], k), t3(cand[:, 0:NTT * k], k), -64.0,
                                            bcast(iota[:, 0:k], NTT, 1), ALU.mult, ALU.add))
                then(red(mi, t3(cand[:, 0:NTT * k], k), AX, ALU.min))
                then(tt(t3(out, k), t3(cand[:, 0:NTT * k], k), bcast(mi, k), ALU.is_equal))

            first_max(ohg, lg[:, :, 0:4], 4, mx)
            then(tt(t3(d4, 4), lg[:, :, 0:4], bcast(mx, 4), ALU.subtract))
            dve.sem_inc(step("d4"), 1)
            for gi in range(4):
                o = t3(tmp[:, 0:NTT * 32], 32)[:, :, 8 * gi:8 * gi + 8]
                then(tt(o, lg[:, :, 4 + 8 * gi:12 + 8 * gi], bcast(ohg[:, gi::4], 8), ALU.mult))
            for gi in range(4):
                o = t3(tmp[:, 0:NTT * 32], 32)[:, :, 8 * gi:8 * gi + 8]
                if gi == 1:
                    then(tt(t3(sel, 8), t3(tmp[:, 0:NTT * 32], 32)[:, :, 0:8], o, ALU.add))
                elif gi:
                    then(tt(t3(sel, 8), t3(sel, 8), o, ALU.add))
            first_max(ohk[0], t3(sel, 8), 8, m1)
            then(v.scalar_tensor_tensor(sel, ohk[0], -1e30, sel, ALU.mult, ALU.add))
            first_max(ohk[1], t3(sel, 8), 8, m2)
            tt(m2, m2, m1, ALU.subtract).then_inc(step("d12"), 1)
            dve.wait_ge(step("e4"), 1)
            then(red(pgt, t3(e4, 4), AX, ALU.add))
            dve.wait_ge(step("ed"), 1)
            then(v.scalar_tensor_tensor(m1, m2, 1.0, pgt, ALU.add, ALU.mult))
            then(v.reciprocal(mx, m1))
            v.tensor_copy(gate_v[:, :, 0], mx)
            tt(gate_v[:, :, 1], mx, m2, ALU.mult)
            oh4 = oh.rearrange("p (t k e) -> p t k e", k=2, e=32)
            for k in range(2):
                for gi in range(4):
                    then(tt(oh4[:, :, k, 8 * gi:8 * gi + 8], t3(ohk[k], 8), bcast(ohg[:, gi::4], 8), ALU.mult))
            then(ts(oh4[:, NT, :, :], oh4[:, NT, :, :], cum[:, NS - 1:NS], None, ALU.mult))
            tt(t3(S[:, 0:NTT * 32], 32), oh4[:, :, 0, :], oh4[:, :, 1, :], ALU.add).then_inc(step("S"), 1)
            oh3, tmp3 = t3(oh, 32), t3(tmp, 32)
            then(tt(tmp3, oh3, bcast(iota[:, 0:32], T2, 1), ALU.mult))
            then(red(ex_id, tmp3, AX, ALU.add))
            dve.wait_ge(step("pos_mm"), 1)
            for k in range(2):
                then(tt(tmp.rearrange("p (t k e) -> p t k e", k=2, e=32)[:, :, k, :], oh4[:, :, k, :],
                        t3(bank[0][:, 0:NTT * 32], 32), ALU.mult))
            then(red(pos, tmp3, AX, ALU.add))

            def level(out, src, scratch):
                for k in range(1, (NT * P + NS - 1) // CAP + 1):
                    if k == 1:
                        then(ts(out, src, float(CAP * k), None, ALU.is_gt))
                    else:
                        then(ts(scratch, src, float(CAP * k), None, ALU.is_gt))
                        then(tt(out, out, scratch, ALU.add))

            dve.wait_ge(step("n_mm"), 1)
            then(v.tensor_copy(cmpT[0:32, :], bank[1][0:32, 0:P]))
            level(ovT[0:32, :], cmpT[0:32, :], tmp[0:32, 0:P])
            dve.sem_inc(step("ovT"), 1)
            level(lvl, pos, cmp)
            dve.wait_ge(step("over_mm"), 1)
            then(ts(over[:, 0:32], bank[2][:, 0:32], -1.0, None, ALU.mult))
            then(tt(tmp3, oh3, bcast(over[:, 0:32], T2, 1), ALU.mult))
            then(red(off, tmp3, AX, ALU.add))
            then(tt(off, off, lvl, ALU.add))
            then(tt(off, off, ex_id, ALU.subtract))
            then(ts(off, off, float(N_EXP - 1), None, ALU.add))
            then(ts(cmp, lvl, 0.0, None, ALU.is_gt))
            then(tt(off, off, cmp, ALU.mult))
            then(tt(tile_of, off, ex_id, ALU.add))
            then(v.scalar_tensor_tensor(addr, lvl, -float(CAP), pos, ALU.mult, ALU.add))
            then(ts(addr, addr, -1.0, float(TILES), ALU.add, ALU.mult))
            then(tt(addr, addr, tile_of, ALU.add))
            then(ts(cmp, pos, 0.0, 1e6, ALU.is_le, ALU.mult))
            then(tt(addr, addr, cmp, ALU.add))
            v.tensor_copy(addr_i, addr).then_inc(step("addr"), 1)
            then(tt(over[:, 32:64], over[:, 0:32], bank[2][:, 32:64], ALU.add))
            ov3 = ovb.rearrange("p (j e) -> p j e", e=32)
            then(tt(ov3, bcast(over[:, 32:64], OVER, 1), bcast(iota[:, 0:OVER], 32), ALU.is_le))
            then(red(ov_exp[:, 0:OVER], ov3, AX, ALU.add))
            then(v.tensor_copy(ov_exp[:, OVER:OVER + 1], bank[2][:, 64:65]))
            then(v.tensor_copy(ov_exp_i, ov_exp))
            dve.wait_ge(step("table_in"), 16)
            then(ts(tokens, table, 1, None, ALU.logical_shift_right))

    with nc.Block() as block:
        def loop(eng, body, first=4, last=4):
            for e in range(first):
                body(e, e)
            with eng.Fori(1, N_EXP // NW - 1) as i:
                for u in range(NW):
                    body(i * NW + u, u)
            for e in range(N_EXP - last, N_EXP):
                body(e, e % NW)

        AHEAD = 3

        def after(eng, name, e, back=0, per=1, n=None):
            wait_earlier(eng, step(name), e, back, per, n)

        def in_buffer(eng, name, e, u):
            eng.wait_ge(step(f"{name}{u}"), (e - u) * (16 // NW) + 16)

        def out_of_buffer(eng, name, e, u):
            if not isinstance(e, int):
                eng.wait_ge(step(f"{name}{u}"), (e - u) * (16 // NW))
            elif e >= NW:
                eng.wait_ge(step(f"{name}{u}"), (e - u) * (16 // NW))

        @block.sync
        def _(sp):
            def body(e, u):
                after(sp, "mm2", e)
                hold(sp)
                load_w(sp, e + NW, u, weights_in(u))

            for e in range(NW):
                body(e, e)
            with sp.Fori(1, N_EXP // NW - 1) as i:
                for u in range(NW):
                    body(i * NW + u, u)

        @block.gpsimd
        def _(pool):
            g = nc.gpsimd

            def gather(e, u):
                after(pool, "idx", e)
                after(pool, "xT_mm", e, NW)
                hold(pool)
                pool.indirect_dma_start(X[u], None, h2_d, bass.IndirectOffsetOnAxis(ap=idx[u][0], axis=0),
                                        bounds_check=NT * P + NS - 1, oob_is_err=False
                                        ).then_inc(step(f"xg_in{u}"), 16)

            def scatter(e, u):
                after(pool, "odx", e)
                after(pool, "y_a", e)
                after(pool, "y_b", e)
                hold(pool)
                pool.indirect_dma_start(y2_d, bass.IndirectOffsetOnAxis(ap=idx[u][1], axis=0), Y[u], None,
                                        bounds_check=2 * (NT * P + NS) - 1, oob_is_err=False
                                        ).then_inc(step(f"y_out{u}"), 16)

            def body(e, u):
                if not (isinstance(e, int) and e >= N_EXP - AHEAD):
                    gather(e + AHEAD, (u + AHEAD) % NW)
                if not (isinstance(e, int) and e == 0):
                    scatter(e - 1, (u - 1) % NW)

            for e in range(AHEAD):
                gather(e, e)
            loop(pool, body)
            scatter(N_EXP - 1, NW - 1)
            for b in range(NW):
                pool.wait_ge(step(f"y_out{b}"), 16 * (N_EXP // NW))

        @block.scalar
        def _(act):
            one_table(nc)
            a = nc.scalar.activation

            def put_xT(e, u):
                after(act, "xT_mm", e)
                after(act, "mm1", e, 2)
                a(xT[u % 2][:, 0:4, :], bank[0][:, :].rearrange("p (c t) -> p c t", c=4), ACT.Copy
                  ).then_inc(step("xT_a"), 1)

            def put_y(e, u):
                after(act, "mm2", e)
                out_of_buffer(act, "y_out", e, u)
                a(Y[u][:, 0:512], bank[4 + 2 * (u % 2)][:, :], ACT.Copy).then_inc(step("y_a"), 1)

            def silu(e, u):
                after(act, "h_clamp", e)
                a(sg, h1, ACT.Exp, scale=-1.0).then_inc(step("sig"), 1)
                after(act, "sig", e, 0, 3, 1)
                a(sg, sg, ACT.Ln, bias=1.0).then_inc(step("sig"), 1)
                after(act, "sig", e, 0, 3, 2)
                a(sg, sg, ACT.Exp, scale=-1.0).then_inc(step("sig"), 1)

            def body(e, u):
                if not (isinstance(e, int) and e == N_EXP - 1):
                    put_xT(e + 1, u + 1)
                silu(e, u)
                if not (isinstance(e, int) and e == 0):
                    put_y(e - 1, u - 1 if u else NW - 1)

            put_xT(0, 0)
            loop(act, body)
            put_y(N_EXP - 1, NW - 1)

        @block.vector
        def _(dve):
            v = nc.vector

            def indices(e, u):
                out_of_buffer(dve, "xg_in", e, u)
                hold(dve)
                v.tensor_copy(idx[u][0], tokens[:, bass.ds(e, 1)]).then_inc(step("idx"), 1)

            def out_rows(e, u):
                out_of_buffer(dve, "y_out", e, u)
                hold(dve)
                v.tensor_copy(idx[u][1], table[:, bass.ds(e, 1)]).then_inc(step("odx"), 1)

            def put_xT(e, u):
                after(dve, "xT_mm", e)
                after(dve, "mm1", e, 2)
                v.tensor_copy(xT[u % 2][:, 4:8, :], bank[1][:, :].rearrange("p (c t) -> p c t", c=4)
                              ).then_inc(step("xT_b"), 1)

            def put_y(e, u):
                after(dve, "mm2", e)
                out_of_buffer(dve, "y_out", e, u)
                v.tensor_copy(Y[u][:, 512:1024], bank[5 + 2 * (u % 2)][:, :]).then_inc(step("y_b"), 1)

            def silu(e, u):
                h = bank[2 + u % 2]
                after(dve, "mm1", e)
                after(dve, "h", e, 1)
                v.tensor_scalar(h1, h[:, 0:256], CLAMP, None, ALU.max).then_inc(step("h_clamp"), 1)
                after(dve, "sig", e, 0, 3, 3)
                after(dve, "h_clamp", e)
                after(dve, "mm2", e, 2)
                v.tensor_tensor(h1, h1, h[:, 256:512], ALU.mult).then_inc(step("h13"), 1)
                after(dve, "h13", e)
                v.tensor_tensor(hT[u % 2], h1, sg, ALU.mult).then_inc(step("h"), 1)

            def body(e, u):
                if not (isinstance(e, int) and e >= N_EXP - AHEAD):
                    indices(e + AHEAD, (u + AHEAD) % NW)
                if not (isinstance(e, int) and e == N_EXP - 1):
                    put_xT(e + 1, u + 1)
                silu(e, u)
                out_rows(e, u)
                if not (isinstance(e, int) and e == 0):
                    put_y(e - 1, u - 1 if u else NW - 1)

            for e in range(AHEAD):
                indices(e, e)
            put_xT(0, 0)
            loop(dve, body)
            put_y(N_EXP - 1, NW - 1)

        @block.tensor
        def _(pe):
            mm, tr = nc.tensor.matmul, nc.tensor.transpose

            def transposes(e, u):
                in_buffer(pe, "xg_in", e, u % NW)
                after(pe, "xT_a", e, 1)
                after(pe, "xT_b", e, 1)
                x = X[u % NW].rearrange("p (t c) -> p c t", c=KC)
                for c in range(KC):
                    ins = tr(bank[c // 4][:, (c % 4) * P:(c % 4 + 1) * P], x[:, c, :], ident)
                ins.then_inc(step("xT_mm"), 1)

            def mm1(e, u):
                after(pe, "xT_a", e)
                after(pe, "xT_b", e)
                pe.wait_ge(weights_in(u % NW), (e - u) * (48 // NW) + 48)
                after(pe, "h13", e, 2)
                for j in range(4):
                    for c in range(KC):
                        ins = mm(bank[2 + u % 2][:, j * P:(j + 1) * P], w13[u][:, c, j * P:(j + 1) * P],
                                 xT[u % 2][:, c, :], start=(c == 0), stop=(c == KC - 1))
                ins.then_inc(step("mm1"), 1)

            def mm2(e, u):
                after(pe, "h", e)
                after(pe, "y_a", e, 2)
                after(pe, "y_b", e, 2)
                for b in range(2):
                    for c in range(2):
                        ins = mm(bank[4 + 2 * (u % 2) + b][:, :], hT[u % 2][:, c * P:(c + 1) * P],
                                 w2[u][:, c, 512 * b:512 * b + 512], start=(c == 0), stop=(c == 1))
                ins.then_inc(step("mm2"), 1)

            def body(e, u):
                if not (isinstance(e, int) and e == N_EXP - 1):
                    transposes(e + 1, u + 1)
                mm1(e, u)
                if not (isinstance(e, int) and e == 0):
                    mm2(e - 1, u - 1 if u else NW - 1)

            transposes(0, 0)
            loop(pe, body)
            mm2(N_EXP - 1, NW - 1)

    with nc.Block() as block:
        def further(eng, body):
            count = eng.value_load(ov_exp_i[0:1, OVER:OVER + 1], min_val=0, max_val=OVER)
            with eng.If(count > 0):
                with eng.Fori(0, count) as i:
                    body(i)

        @block.sync
        def _(sp):
            def body(i):
                sp.wait_ge(step("o_free"), i + 1)
                hold(sp)
                e = sp.value_load(ov_exp_i[0:1, bass.ds(i, 1)], min_val=0, max_val=N_EXP - 1)
                s = step("o_weights")
                w1v = A["exp_w1"][0].rearrange("e (p c) n -> e p c n", c=KC)
                w3v = A["exp_w3"][0].rearrange("e (p c) n -> e p c n", c=KC)
                w2v = A["exp_w2"][0].rearrange("e (c p) n -> e p c n", c=2)
                sp.dma_start(w13[0][:, :, 0:256], w1v[bass.ds(e, 1)]).then_inc(s, 16)
                sp.dma_start(w13[0][:, :, 256:512], w3v[bass.ds(e, 1)]).then_inc(s, 16)
                sp.dma_start(w2[0], w2v[bass.ds(e, 1)]).then_inc(s, 16)

            further(sp, body)

        @block.gpsimd
        def _(pool):
            def body(i):
                pool.wait_ge(step("o_idx"), i + 1)
                hold(pool)
                pool.indirect_dma_start(X[0], None, h2_d, bass.IndirectOffsetOnAxis(ap=idx[0][0], axis=0),
                                        bounds_check=NT * P + NS - 1, oob_is_err=False).then_inc(step("o_x"), 16)
                pool.wait_ge(step("o_y"), i + 1)
                hold(pool)
                pool.indirect_dma_start(y2_d, bass.IndirectOffsetOnAxis(ap=idx[0][1], axis=0), Y[0], None,
                                        bounds_check=2 * (NT * P + NS) - 1, oob_is_err=False
                                        ).then_inc(step("o_stored"), 16)
                pool.wait_ge(step("o_stored"), i * 16 + 16)
                pool.sem_inc(step("o_done"), 1)

            pool.sem_inc(step("o_done"), 1)
            further(pool, body)

        @block.scalar
        def _(act):
            one_table(nc)
            a = nc.scalar.activation

            def body(i):
                act.wait_ge(step("o_clamp"), i + 1)
                a(sg, h1, ACT.Exp, scale=-1.0).then_inc(step("o_sig"), 1)
                act.wait_ge(step("o_sig"), i * 3 + 1)
                a(sg, sg, ACT.Ln, bias=1.0).then_inc(step("o_sig"), 1)
                act.wait_ge(step("o_sig"), i * 3 + 2)
                a(sg, sg, ACT.Exp, scale=-1.0).then_inc(step("o_sig"), 1)

            further(act, body)

        @block.vector
        def _(dve):
            v = nc.vector

            def body(i):
                dve.wait_ge(step("o_done"), i + 1)
                hold(dve)
                v.tensor_copy(idx[0][0], tokens[:, bass.ds(i + N_EXP, 1)])
                v.tensor_copy(idx[0][1], table[:, bass.ds(i + N_EXP, 1)]).then_inc(step("o_idx"), 1)
                dve.wait_ge(step("o_xT_mm"), i + 1)
                for b in range(2):
                    ins = v.tensor_copy(xT[0][:, 4 * b:4 * b + 4, :], bank[b][:, :].rearrange("p (c t) -> p c t", c=4))
                ins.then_inc(step("o_xT"), 1)
                dve.wait_ge(step("o_mm1"), i + 1)
                v.tensor_scalar(h1, bank[2][:, 0:256], CLAMP, None, ALU.max).then_inc(step("o_clamp"), 1)
                dve.wait_ge(step("o_sig"), i * 3 + 3)
                v.tensor_tensor(h1, h1, bank[2][:, 256:512], ALU.mult).then_inc(step("o_h13"), 1)
                dve.wait_ge(step("o_h13"), i + 1)
                v.tensor_tensor(hT[0], h1, sg, ALU.mult).then_inc(step("o_h"), 1)
                dve.wait_ge(step("o_mm2"), i + 1)
                for b in range(2):
                    ins = v.tensor_copy(Y[0][:, 512 * b:512 * b + 512], bank[4 + b][:, :])
                ins.then_inc(step("o_y"), 1)

            further(dve, body)

        @block.tensor
        def _(pe):
            mm, tr = nc.tensor.matmul, nc.tensor.transpose

            def body(i):
                pe.wait_ge(step("o_x"), i * 16 + 16)
                x = X[0].rearrange("p (t c) -> p c t", c=KC)
                for c in range(KC):
                    ins = tr(bank[c // 4][:, (c % 4) * P:(c % 4 + 1) * P], x[:, c, :], ident)
                ins.then_inc(step("o_xT_mm"), 1)
                pe.wait_ge(step("o_xT"), i + 1)
                pe.wait_ge(step("o_weights"), i * 48 + 48)
                for j in range(4):
                    for c in range(KC):
                        ins = mm(bank[2][:, j * P:(j + 1) * P], w13[0][:, c, j * P:(j + 1) * P],
                                 xT[0][:, c, :], start=(c == 0), stop=(c == KC - 1))
                ins.then_inc(step("o_mm1"), 1)
                pe.wait_ge(step("o_h"), i + 1)
                for b in range(2):
                    for c in range(2):
                        ins = mm(bank[4 + b][:, :], hT[0][:, c * P:(c + 1) * P],
                                 w2[0][:, c, 512 * b:512 * b + 512], start=(c == 0), stop=(c == 1))
                ins.then_inc(step("o_mm2"), 1)
                pe.sem_inc(step("o_free"), 1)

            pe.sem_inc(step("o_free"), 1)
            further(pe, body)

    with nc.Block() as block:
        out = O[0].rearrange("b s d -> (b s) d")
        out_s = O[1].rearrange("b s d -> (b s) d")

        @block.sync
        def _(sp):
            for t in range(NTT):
                u, rows = t % 2, slice(t * P, t * P + P) if t < NT else slice(NT * P, NT * P + NS)
                n = rows.stop - rows.start
                wait_earlier(sp, step("f_sum"), t, 2)
                sp.dma_start(x2[u][0:n, :], x2_d[rows, :]).then_inc(step(f"f_in{u}"), 16)
                sp.dma_start(y2[u][0:n, :], y2_d[2 * rows.start:2 * rows.stop, :].rearrange("(p k) d -> p (k d)", k=2)
                             ).then_inc(step(f"f_in{u}"), 16)

        @block.gpsimd
        def _(pool):
            for t in range(NTT):
                u = t % 2
                pool.wait_ge(step("f_out"), t + 1)
                if t < NT:
                    pool.dma_start(out[t * P:(t + 1) * P, :], fo[u]).then_inc(step(f"f_stored{u}"), 16)
                else:
                    pool.dma_start(out_s, fo[u][0:NS, :]).then_inc(step(f"f_stored{u}"), 16)
            pool.wait_ge(step("f_stored0"), 16 * (NT // 2 + 1))
            pool.wait_ge(step("f_stored1"), 16 * (NT // 2))

        @block.scalar
        def _(act):
            one_table(nc)
            a = nc.scalar.activation
            for t in range(NTT):
                R = slice(0, P if t < NT else NS)
                u = t % 2
                act.wait_ge(step("f_sum"), t + 1)
                if t:
                    act.wait_ge(step("f_rs"), 3 * t)
                    act.wait_ge(step("f_out"), t)
                a(X[0][R, :], Y[u][R, :], ACT.Square, accum_out=fs[R, 0:1]).then_inc(step("f_rs"), 1)
                act.wait_ge(step("f_rs"), 3 * t + 1)
                a(fs[R, 1:2], fs[R, 0:1], ACT.Ln, scale=1.0 / D, bias=eps[R, :]).then_inc(step("f_rs"), 1)
                act.wait_ge(step("f_rs"), 3 * t + 2)
                a(fs[R, 2:3], fs[R, 1:2], ACT.Exp, scale=-0.5).then_inc(step("f_rs"), 1)

        @block.vector
        def _(dve):
            v = nc.vector
            dve.wait_ge(step("fg_in"), 16)
            for t in range(NTT):
                R, u = slice(0, P if t < NT else NS), t % 2
                dve.wait_ge(step(f"f_in{u}"), 32 * (t // 2 + 1))
                if t >= 2:
                    dve.wait_ge(step("f_out"), t - 1)
                v.scalar_tensor_tensor(X[1][R, :], y2[u][R, 0:D], gate[R, 2 * t:2 * t + 1], x2[u][R, :],
                                       ALU.mult, ALU.add).then_inc(step("f_half"), 1)
                dve.wait_ge(step("f_half"), t + 1)
                v.scalar_tensor_tensor(Y[u][R, :], y2[u][R, D:2 * D], gate[R, 2 * t + 1:2 * t + 2], X[1][R, :],
                                       ALU.mult, ALU.add).then_inc(step("f_sum"), 1)
                dve.wait_ge(step("f_rs"), 3 * t + 3)
                dve.wait_ge(step("f_sum"), t + 1)
                if t >= 2:
                    dve.wait_ge(step(f"f_stored{u}"), 16 * (t // 2))
                v.scalar_tensor_tensor(fo[u][R, :], Y[u][R, :], fs[R, 2:3], fg[R, :], ALU.mult, ALU.mult
                                       ).then_inc(step("f_out"), 1)


_INS = ['x_prompt', 'x_sample', 'state_gla', 'state_dn', 'state_conv', 'state_hgrn', 'norm1_g', 'w_in', 'gla_wa2',
        'gla_ba', 'gla_norm_g', 'dn_conv_w', 'dn_a_log', 'dn_dt_bias', 'dn_norm_g', 'hg_lb_logits', 'hg_norm_g',
        'w_out', 'norm2_g', 'router_g_w', 'router_g_b', 'router_e_w', 'router_e_b', 'exp_w1', 'exp_w3', 'exp_w2',
        'final_norm_g']
_OUTS = [(1, SEQ, D), (NS, 1, D), (1, 1, H_GLA, DK_GLA, DV), (1, 1, H_DN, DK_DN, DV), (1, 1, 3, CONV),
         (1, 1, H_HG, DK_HG, DV), (1, NS, H_GLA, DK_GLA, DV), (1, NS, H_DN, DK_DN, DV), (1, NS, 3, CONV),
         (1, NS, H_HG, DK_HG, DV)]


def kernel(**inputs):
    import numpy as _np
    import concourse.bacc as _bacc
    from concourse.bass_utils import run_bass_kernel_spmd as _run

    nc = _bacc.Bacc("TRN2", target_bir_lowering=False, num_devices=1)
    arrays, ins = {}, {}
    given = {name: _np.ascontiguousarray(inputs[name]) for name in _INS}
    given["shape_consts"], given["shape_masks"] = shape_constants()
    for name, a in given.items():
        arrays[f"in_{name}"] = a
        ins[name] = nc.dram_tensor(f"in_{name}", a.shape, mybir.dt.from_np(a.dtype), kind="ExternalInput").ap()
    outs = [nc.dram_tensor(f"out_{i}", s, F32, kind="ExternalOutput").ap() for i, s in enumerate(_OUTS)]
    build(nc, ins, outs)
    r = _run(nc, [arrays], core_ids=[0])
    return tuple(r.results[0][f"out_{i}"] for i in range(len(_OUTS)))
```

```python
from contextlib import ExitStack
import math

import concourse.bass as bass
from concourse import mybir

ALU = mybir.AluOpType
ACT = mybir.ActivationFunctionType
AX = mybir.AxisListType.X
F32 = mybir.dt.float32
I32 = mybir.dt.int32

P = 128
D = 1024
KC = D // P
SEQ = 1024
NT = SEQ // P
NS = 8
NTT = NT + 1
EPS = 1e-6
H_GLA, DK_GLA, DV = 6, 32, 64
H_DN, DK_DN = 6, 64
H_HG, DK_HG = 4, 64
CONV = H_DN * 3 * 64
CT = CONV // P
IN_COLS = 3740
N_EXP, N_GRP, EPG, FF = 32, 4, 8, 256
LEVELS = 7
CAP = 128
OVER = (2 * (NT * P + NS)) // (CAP + 1) + 1
TILES = N_EXP + OVER
LEVEL_MAX = (NT * P + NS - 1) // CAP
NONE = 4096
CLAMP = -40.0

GQ, GK, GV, GA, GG = 0, 192, 384, 768, 784
DA, DB, DG = 1168, 1174, 1180
HQ, HF, HI, HG = 1564, 1820, 2076, 2332
TOK = 2588
QKV0 = 1168
UNITS = [(0, 0, 512), (512, 512, 512), (1024, 1024, 144), (2320, 1168, 512), (2832, 1680, 512), (3344, 2192, 396)]
LG_H, LG_D, LG_B, LG = 192, 448, 454, 460
DT_ROWS = [128, 64, 128, 128]
DT_COLS = [0, 128, 192, 320]
DT_VALS = [0, 256, 384, 512]
DT_HEADS = [[0, 1, 2, 3], [4, 5], [6, 7], [8, 9]]


def head_place(n):
    if n < H_GLA:
        return n // 4, DK_GLA * (n % 4), DK_GLA, GV + DV * n
    n -= H_GLA
    return 2 + n // 2, DK_HG * (n % 2), DK_HG, HI + DV * n


def shape_constants():
    import numpy as np

    t = np.arange(P)
    j, i = t[:, None], t[None, :]
    f = [np.eye(P)]
    lower, upper = [], []
    for n in range(LEVELS):
        s = 1 << n
        second = (t // s) % 2 == 1
        same = (j // (2 * s)) == (i // (2 * s))
        mid = (t // (2 * s)) * 2 * s + s - 1
        q_part = second[None, :] & (j > mid[None, :]) & (j <= i)
        k_part = ~second[None, :] & (j > i) & (j <= mid[None, :])
        f.append((q_part | k_part).astype(float))
        upper.append(same & second[None, :] & ~second[:, None])
        lower.append(upper[-1].T)
    f += [j <= i, j > i, np.ones((P, P)), -(i > j).astype(float)]
    f.append(np.broadcast_to(np.arange(P)[None, :], (P, P)))
    f.append(np.arange(P)[:, None] // 32 == np.arange(4 * 64)[None, :] // 64)
    f.append(np.arange(P)[:, None] // 64 == np.arange(2 * 64)[None, :] // 64)
    m = lower + upper + [np.eye(P, dtype=bool)]
    m.append(2 * (t[:, None, None] + P * np.arange(NTT)[None, :, None]) + np.arange(2)[None, None, :])
    m[-1] = m[-1].reshape(P, 2 * NTT)
    return (np.ascontiguousarray(np.concatenate(f, 1), np.float32),
            np.ascontiguousarray(np.concatenate(m, 1), np.int32))


C_ID, C_LV = 0, P
C_SUF = P + (LEVELS + 1) * P
C_ONES, C_NST, C_IOTA = C_SUF + P, C_SUF + 2 * P, C_SUF + 3 * P
C_M32, C_M64 = C_IOTA + P, C_IOTA + 3 * P
NCONST = C_M64 + P
M_DST = (2 * LEVELS + 1) * P
NMASK = M_DST + 2 * NTT


def one_table(nc):
    nc.scalar.preload_act_table_set("natural_log_exp_and_others")


def dram_rows(ap, first, n):
    return ap[bass.ds(first, n), :]


def tiles(eng, body, n, unroll=2):
    for t in range(unroll):
        body(t, t % 2)
    with eng.Fori(1, n // unroll) as i:
        for t in range(unroll):
            body(i * unroll + t, t % 2)


def wait_earlier(eng, sem, tile, back, per=1, n=None):
    n = per if n is None else n
    if isinstance(tile, int):
        if tile >= back:
            eng.wait_ge(sem, (tile - back) * per + n)
    else:
        eng.wait_ge(sem, tile * per + (n - back * per))


class stage_semaphores:

    def __init__(self, nc):
        self.nc, self.made = nc, []

    def __enter__(self):
        return self

    def semaphore(self, name):
        self.made.append(self.nc.alloc_semaphore(name=name))
        return self.made[-1]

    def __exit__(self, kind, value, trace):
        if kind is None:
            self.nc.all_engine_barrier()
            self.nc.clear_and_free_semaphores(self.made)
            self.nc.all_engine_barrier()


def build(nc, A, O):
    with ExitStack() as ctx:
        arena = ctx.enter_context(nc.sbuf_tensor("arena", [P, 53200], F32))
        psum = ctx.enter_context(nc.psum_tensor("psum", [P, 8 * 512], F32))
        bank = [psum[:, 512 * n:512 * n + 512] for n in range(8)]
        tok_d = nc.dram_tensor("tok_d", (NT * P + NS, TOK), F32, kind="Internal").ap()
        qkv_d = nc.dram_tensor("qkv_d", (NT * P, CONV), F32, kind="Internal").ap()
        sqkv_d = nc.dram_tensor("sqkv_d", (NS, CONV), F32, kind="Internal").ap()

        x2_d = nc.dram_tensor("x2_d", (NT * P + NS, D), F32, kind="Internal").ap()
        h2_d = nc.dram_tensor("h2_d", (NT * P + NS, D), F32, kind="Internal").ap()
        lg_d = nc.dram_tensor("lg_d", (NT * P + NS, 36), F32, kind="Internal").ap()

        rows_d = nc.dram_tensor("rows_d", (NS * 3400,), F32, kind="Internal").ap()
        y2_d = nc.dram_tensor("y2_d", (2 * (NT * P + NS), D), F32, kind="Internal").ap()
        so_d = nc.dram_tensor("so_d", (NS, D), F32, kind="Internal").ap()

        used = [0]

        def take(n):
            used[0] += n
            assert used[0] <= 53200, used[0]
            return arena[:, used[0] - n:used[0]]

        const = take(NCONST)
        masks = take(NMASK).bitcast(I32)
        consts_in = ctx.enter_context(nc.semaphore("consts_in"))
        mark = used[0]
        with stage_semaphores(nc) as stage:
            project(nc, stage, A, take, bank, const, masks, consts_in, tok_d, qkv_d, sqkv_d)
        used[0] = mark
        with stage_semaphores(nc) as stage:
            mix(nc, stage, A, O, lambda a, b: arena[:, a:b], lambda: used[0], take, psum, bank, const, masks, consts_in, tok_d, qkv_d, sqkv_d, x2_d, h2_d, lg_d, rows_d, so_d)
        used[0] = mark
        with stage_semaphores(nc) as stage:
            experts(nc, stage, A, O, take, bank, const, masks, x2_d, h2_d, lg_d, y2_d)


def project(nc, ctx, A, take, bank, const, masks, consts_in, tok_d, qkv_d, sqkv_d):
    ident = const[:, C_ID:C_ID + P]
    w_in = take(KC * IN_COLS).rearrange("p (c n) -> p c n", c=KC)
    g1 = take(KC)
    x = [take(D) for _ in range(2)]
    xs = take(D)
    hT = [take(D).rearrange("p (c t) -> p c t", c=KC) for _ in range(2)]
    tok = [take(TOK) for _ in range(2)]
    qkv = [take(CONV) for _ in range(2)]
    junk = take(D)
    stat = take(8)
    units = [(w, o, n, None) for w, o, n in UNITS] + [(QKV0 + 384 * q, 384 * q, 384, q) for q in range(3)]
    NU = len(units)

    def sem(name):
        return ctx.semaphore(name)

    x_in = [sem(f"x_in{u}") for u in range(2)]
    w_in_in = [sem(f"w_in_in{k}") for k in range(NU)]
    g1_in = sem("g1_in")
    ss_done, lnss_done, rstd_done = sem("ss_done"), sem("lnss_done"), sem("rstd_done")
    xs_done, xsT_done, hT_done = sem("xs_done"), sem("xsT_done"), sem("hT_done")
    unit_done, act_out, dve_out = sem("unit_done"), sem("act_out"), sem("dve_out")
    stored = [sem(f"proj_stored{u}") for u in range(2)]
    eps_set, ident_in = sem("eps_set"), sem("ident_in")
    xp = A["x_prompt"].rearrange("b s d -> (b s) d")
    xsmp = A["x_sample"].rearrange("b s d -> (b s) d")
    win_v = A["w_in"].rearrange("l (p c) n -> p (l c) n", c=KC)
    ACT_PER, DVE_PER = (NU + 1) // 2, NU // 2

    def wait_unit_out(eng, tile, k, back=0):
        s, per = (act_out, ACT_PER) if k % 2 == 0 else (dve_out, DVE_PER)
        wait_earlier(eng, s, tile, back, per, k // 2 + 1)

    with nc.Block() as block:
        def wait_stored(eng, t, u):
            if isinstance(t, int):
                if t >= 2:
                    eng.wait_ge(stored[u], 32 * (t // 2))
            else:
                eng.wait_ge(stored[u], (t - u) * 16)

        @block.sync
        def _(sp):
            sp.dma_start(ident, A["shape_consts"][:, C_ID:C_ID + P]).then_inc(ident_in, 16)
            sp.dma_start(g1, A["norm1_g"].rearrange("l (p c) -> p (l c)", c=KC)).then_inc(g1_in, 16)

            def load_x(t, u):
                wait_earlier(sp, xs_done, t, 2)
                sp.dma_start(x[u], dram_rows(xp, t * P, P)).then_inc(x_in[u], 16)

            load_x(0, 0)
            for k in (0, 1):
                w, _, n, _ = units[k]
                sp.dma_start(w_in[:, :, w:w + n], win_v[:, :, w:w + n]).then_inc(w_in_in[k], 16)
            load_x(1, 1)
            for k in range(2, NU):
                w, _, n, _ = units[k]
                sp.dma_start(w_in[:, :, w:w + n], win_v[:, :, w:w + n]).then_inc(w_in_in[k], 16)
            sp.dma_start(const[:, P:], A["shape_consts"][:, P:]).then_inc(consts_in, 16)
            sp.dma_start(masks, A["shape_masks"]).then_inc(consts_in, 16)
            with sp.Fori(1, NT // 2) as i:
                load_x(i * 2, 0)
                load_x(i * 2 + 1, 1)
            sp.wait_ge(xs_done, NT - 1)
            sp.dma_start(x[0][0:NS, :], xsmp).then_inc(x_in[0], 16)

        def x_arrived(eng, t, u):
            if isinstance(t, int):
                eng.wait_ge(x_in[u], 16 * (t // 2 + 1))
            else:
                eng.wait_ge(x_in[u], (t - u) * 8 + 16)

        @block.scalar
        def _(act):
            one_table(nc)
            def norm(t, u):
                x_arrived(act, t, u)
                wait_earlier(act, lnss_done, t, 1)
                nc.scalar.activation(junk, x[u], ACT.Square, accum_out=stat[:, 0:1]).then_inc(ss_done, 1)
                act.wait_ge(ss_done, t + 1)
                nc.scalar.activation(stat[:, 1:2], stat[:, 0:1], ACT.Ln, scale=1.0 / D, bias=const_eps).then_inc(lnss_done, 1)
                act.wait_ge(lnss_done, t + 1)
                wait_earlier(act, xs_done, t, 1)
                nc.scalar.activation(stat[:, 2:3], stat[:, 1:2], ACT.Exp, scale=-0.5).then_inc(rstd_done, 1)

            def out(t, u, k):
                _, o, n, q = units[k]
                act.wait_ge(unit_done, t * NU + k + 1)
                if k in (0, 6):
                    wait_stored(act, t, u)
                dst = tok[u][:, o:o + n] if q is None else qkv[u][:, o:o + n]
                nc.scalar.activation(dst, bank[2 + k % 6][:, 0:n], ACT.Copy).then_inc(act_out, 1)

            def body(t, u, last=False):
                if not last:
                    norm(t + 1, 1 - u)
                for k in range(0, NU, 2):
                    out(t, u, k)

            const_eps = stat[:, 7:8]
            act.wait_ge(eps_set, 1)
            norm(0, 0)
            tiles(act, body, NT)
            body(NT, 0, True)

        @block.vector
        def _(dve):
            nc.vector.memset(stat[:, 7:8], EPS).then_inc(eps_set, 1)

            def scale(t, u):
                dve.wait_ge(rstd_done, t + 1)
                wait_earlier(dve, xsT_done, t, 1)
                nc.vector.tensor_scalar(xs, x[u], stat[:, 2:3], None, ALU.mult).then_inc(xs_done, 1)

            def put_hT(t, u):
                dve.wait_ge(xsT_done, t + 1)
                for b in range(2):
                    ins = nc.vector.tensor_tensor(
                        hT[u][:, 4 * b:4 * b + 4, :], bank[b][:, :].rearrange("p (c t) -> p c t", c=4),
                        g1[:, 4 * b:4 * b + 4].unsqueeze(2).to_broadcast([P, 4, P]), ALU.mult)
                ins.then_inc(hT_done, 1)

            def out(t, u, k):
                _, o, n, q = units[k]
                dve.wait_ge(unit_done, t * NU + k + 1)
                if k == 1:
                    wait_stored(dve, t, u)
                dst = tok[u][:, o:o + n] if q is None else qkv[u][:, o:o + n]
                nc.vector.tensor_copy(dst, bank[2 + k % 6][:, 0:n]).then_inc(dve_out, 1)

            def body(t, u, last=False):
                out(t, u, 1)
                if not last:
                    scale(t + 1, 1 - u)
                out(t, u, 3)
                if not last:
                    put_hT(t + 1, 1 - u)
                out(t, u, 5)
                out(t, u, 7)

            scale(0, 0)
            dve.wait_ge(g1_in, 16)
            put_hT(0, 0)
            tiles(dve, body, NT)
            body(NT, 0, True)

        @block.tensor
        def _(pe):
            def transposes(t, u):
                pe.wait_ge(xs_done, t + 1)
                wait_earlier(pe, hT_done, t, 1)
                v = xs.rearrange("p (t c) -> p c t", c=KC)
                for c in range(KC):
                    ins = nc.tensor.transpose(bank[c // 4][:, (c % 4) * P:(c % 4 + 1) * P], v[:, c, :], ident)
                ins.then_inc(xsT_done, 1)

            def unit(t, u, k, column_major=True):
                w, _, n, q = units[k]
                if isinstance(t, int) and t == 0:
                    pe.wait_ge(w_in_in[k], 16)
                if k >= 6:
                    wait_unit_out(pe, t, k - 6)
                else:
                    wait_unit_out(pe, t, k + 6 if k < 3 else k, back=1)
                b = bank[2 + k % 6]
                if q is None or not column_major:
                    for c in range(KC):
                        ins = nc.tensor.matmul(b[:, 0:n], hT[u][:, c, :], w_in[:, c, w:w + n],
                                               start=(c == 0), stop=(c == KC - 1))
                else:
                    for j in range(3):
                        for c in range(KC):
                            ins = nc.tensor.matmul(b[:, j * P:(j + 1) * P], w_in[:, c, w + j * P:w + (j + 1) * P],
                                                   hT[u][:, c, :], start=(c == 0), stop=(c == KC - 1))
                ins.then_inc(unit_done, 1)

            def body(t, u, last=False):
                pe.wait_ge(hT_done, t + 1)
                for k in range(4):
                    unit(t, u, k)
                if not last:
                    transposes(t + 1, 1 - u)
                for k in range(4, NU):
                    unit(t, u, k, not last)

            pe.wait_ge(ident_in, 16)
            transposes(0, 0)
            tiles(pe, body, NT)
            body(NT, 0, True)

        @block.gpsimd
        def _(pool):
            def store(t, u):
                pool.wait_ge(act_out, t * ACT_PER + ACT_PER)
                pool.wait_ge(dve_out, t * DVE_PER + DVE_PER)
                pool.dma_start(dram_rows(tok_d, t * P, P), tok[u]).then_inc(stored[u], 16)
                pool.dma_start(dram_rows(qkv_d, t * P, P), qkv[u]).then_inc(stored[u], 16)

            tiles(pool, store, NT)
            pool.wait_ge(act_out, (NT + 1) * ACT_PER)
            pool.wait_ge(dve_out, (NT + 1) * DVE_PER)
            pool.dma_start(tok_d[NT * P:NT * P + NS, :], tok[0][0:NS, :]).then_inc(stored[0], 16)
            pool.dma_start(sqkv_d, qkv[0][0:NS, :]).then_inc(stored[0], 16)
            pool.wait_ge(stored[0], 32 * (NT // 2 + 1))
            pool.wait_ge(stored[1], 32 * (NT // 2))


def mix(nc, ctx, A, O, arena_cols, used_now, take, psum, bank, const, masks, consts_in, tok_d, qkv_d, sqkv_d, x2_d, h2_d, lg_d, rows_d, so_d):
    ident = const[:, C_ID:C_ID + P]
    lv = const[:, C_LV:C_LV + 8 * P]
    cum = const[:, C_LV + 7 * P:C_LV + 8 * P]
    m32, m64 = const[:, C_M32:C_M32 + 2 * P], const[:, C_M64:C_M64 + P]
    suf = const[:, C_SUF:C_SUF + P]
    ones = const[:, C_ONES:C_ONES + P]
    nstrict = const[:, C_NST:C_NST + P]
    lower = [masks[:, n * P:(n + 1) * P] for n in range(LEVELS)]
    upper = [masks[:, (LEVELS + n) * P:(LEVELS + n + 1) * P] for n in range(LEVELS)]
    diag = masks[:, 2 * LEVELS * P:(2 * LEVELS + 1) * P]
    q_mask = upper + [diag]

    def b3(ap, a, b):
        return ap.unsqueeze(1).to_broadcast([ap.shape[0], a, b])

    def bl(ap, n):
        return ap.unsqueeze(2).to_broadcast([ap.shape[0], ap.shape[1], n])

    def h3(ap, n=64):
        return ap.rearrange("p (h e) -> p h e", e=n)

    w_out = take(KC * D).rearrange("p (c n) -> p c n", c=KC)
    g2, ng, ba = take(D), take(D), take(192)
    scl, ndtb, lb, oml = take(LG), take(6), take(256), take(256)
    wa2 = take(192)
    cw = take(4 * CT).rearrange("p (c i) -> p c i", i=4)
    rw, rb = take(KC * 36).rearrange("p (c n) -> p c n", c=KC), take(36)
    eps, ln8 = take(1), take(1)
    tok = [take(TOK) for _ in range(2)]
    xc = [take(CT * 131).rearrange("p (c t) -> p c t", c=CT) for _ in range(2)]
    z, ab, la, ex, beta = take(LG), take(LG), take(LG), take(466), take(6)
    xe, hk = take(256), take(256)
    sm = hk
    gc, ge = take(1280), take(1280)
    cv, ce = take(CONV), take(CONV)
    cv3 = cv.rearrange("p (c t) -> p c t", c=CT)
    qkv = take(CONV)
    ssd, rs = take(12), take(12)
    kb, vb, kd = take(384), take(384), take(384)
    dqT = take(CONV).rearrange("p (c t) -> p c t", c=CT)
    gt, gtm, gti, nm, atd = take(768), take(768), take(768), take(768), take(768)
    T, U, pm = take(768), take(768), take(768)
    gl = pm
    qk2 = take(1024).rearrange("p (c t) -> p c t", c=8)
    kdg = take(448)
    att = take(1280)
    E = [take(1024) for _ in range(2)]
    zq = [take(896) for _ in range(2)]
    sq_junk = arena_cols(used_now() - 2 * 896, used_now() - 2 * 896 + D)
    zk = [take(896) for _ in range(2)]
    qs, el = take(512), take(4)
    r, vn = take(384), take(384)
    alT = r[:, 0:P]
    oc, x2 = take(D), take(D)
    oT, h2T, sq2 = E[0], E[1], ce
    h2 = oc
    sso, rso, st2 = take(16), take(16), take(4)
    lg = take(36)
    s_lin, s_dn = take(640), take(384)
    masked = zk[0][:, 0:640]

    def region(first, last):
        a, b = first.offset % 53200, last.offset % 53200 + last.shape[-1]
        return arena_cols(a, b)

    big1, big2 = region(kb, pm), region(E[0], zk[1])
    big3 = arena_cols(tok[1].offset % 53200, tok[1].offset % 53200 + 4096)
    sconv, cwb = big1[0:NS, 4 * CONV:7 * CONV], big1[0:NS, 0:4 * CONV]
    R_DN, R_GLA, R_HG = slice(0, 48), slice(48, 96), slice(96, 128)
    vec, sstate = kdg[:, 0:258], big3
    s_q, s_k, s_dec, s_val = vec[:, 0:64], vec[:, 64:128], vec[:, 128:192], vec[:, 192:256]
    s_beta, s_decay = vec[R_DN, 256:257], vec[R_DN, 257:258]
    so, ks = ab[:, 0:64], ab[0:48, 64:128]

    conv_part = region(gtm, gti)[:, 0:CONV].rearrange("p (c t) -> p c t", c=CT)
    sems = {}

    def step(name):
        if name not in sems:
            sems[name] = ctx.semaphore(name)
        return sems[name]

    def done(eng, name, t, n=1, per=1):
        eng.wait_ge(step(name), t * per + n)

    def freed(eng, name, t, back=1, per=1):
        wait_earlier(eng, step(name), t, back, per)

    def loaded(eng, name, t, u):
        eng.wait_ge(step(f"{name}{u}"), (t - u) * 8 + 16)

    params = step("params_in")
    held = {e: step(f"held_{n}") for e, n in ((nc.vector.engine, "dve"), (nc.gpsimd.engine, "pool"), (nc.sync.engine, "sp"))}

    def hold(eng):
        eng.sem_inc(held[eng.engine], 1)

    params_all = [0]
    x_flat = A["x_prompt"].rearrange("b s d -> (b s) d")
    LIN_STEPS = [(dt, pair, half) for dt in range(4) for pair in range(len(DT_HEADS[dt]) // 2) for half in range(2)]
    LIN = len(LIN_STEPS)
    fill = [(1, 1)] * 3 + [(1, 0)] * 4
    order = []
    n = 0
    for level, (a, b) in enumerate(fill):
        order.append(("P", level))
        for _ in range(a):
            order.append(("lin", n))
            n += 1
        order.append(("TU", level))
        for _ in range(b):
            order.append(("lin", n))
            n += 1
    assert n == LIN

    def pair_of(n):
        return psum[:, 512 * n:512 * n + 1024].rearrange("p (b c) -> p b c", b=2)

    def halves(ap):
        return ap.rearrange("p (b c) -> p b c", b=2)

    def by_parity(ap):
        return ap.rearrange("p (c b e) -> p b c e", b=2, e=DV)

    def slot(h):
        return 3 * (h % 2) + h // 2

    def q_of(dt, rows=slice(0, P)):
        return qk2[rows, dt, :]

    def k_of(dt, rows=slice(0, P)):
        return qk2[rows, 4 + dt, :]

    def tail_free(eng, t):
        if isinstance(t, int):
            if t:
                eng.wait_ge(step("tail_stored"), 48 * t)
        else:
            eng.wait_ge(step("tail_stored"), t * 48)

    with nc.Block() as block:
        @block.sync
        def _(sp):
            pb = lambda ap, n=P: ap.partition_broadcast(n)
            loads = [(g2, pb(A["norm2_g"][0])), (ba, pb(A["gla_ba"][0])), (ndtb, pb(A["dn_dt_bias"][0])),
                     (scl[:, LG_D:LG_B], pb(A["dn_a_log"][0])), (sm, pb(A["hg_lb_logits"][0])),
                     (wa2[0:16, :], A["gla_wa2"][0]), (rb[:, 0:4], pb(A["router_g_b"][0])),
                     (rb[:, 4:36], pb(A["router_e_b"][0])),
                     (rw[:, :, 0:4], A["router_g_w"].rearrange("l (p c) n -> p (l c) n", c=KC)),
                     (rw[:, :, 4:36], A["router_e_w"].rearrange("l (p c) n -> p (l c) n", c=KC))]
            loads += [(h3(ng[:, DV * h:DV * (h + n)]), pb(A[name][0]).unsqueeze(1).to_broadcast([P, n, DV]))
                      for h, n, name in ((0, 6, "gla_norm_g"), (6, 6, "dn_norm_g"), (12, 4, "hg_norm_g"))]
            loads += [(cw[:, :, i], A["dn_conv_w"][0, i].rearrange("(c p) -> p c", p=P)) for i in range(4)]

            def load_tile(t, u):
                freed(sp, "slin_mm", t, 2)
                hold(sp)
                sp.dma_start(tok[u], dram_rows(tok_d, t * P, P)).then_inc(step(f"tok_in{u}"), 16)
                freed(sp, "halo", t, 1)
                freed(sp, "conv", t, 2)
                hold(sp)
                sp.dma_start(xc[u][:, :, 3:131], dram_rows(qkv_d, t * P, P).rearrange("p (c t) -> p c t", c=CT)
                             ).then_inc(step(f"xc_in{u}"), 16)

            load_tile(0, 0)
            for dst, src in loads:
                sp.dma_start(dst, src, allow_slow_non_contiguous=True).then_inc(params, 16)
            params_all[0] = 16 * len(loads)
            def body(t, u, last=False):
                if not last:
                    load_tile(t + 1, 1 - u)
                if isinstance(t, int) and t == 0:
                    sp.dma_start(w_out, A["w_out"].rearrange("l (p c) n -> p (l c) n", c=KC)).then_inc(step("w_out_in"), 16)
                if not (isinstance(t, int) and t == 0):
                    store_tail(t - 1)
                load_x(t)

            def load_x(t):
                freed(sp, "h2", t)
                hold(sp)
                tail_free(sp, t)
                hold(sp)
                sp.dma_start(x2, dram_rows(x_flat, t * P, P)).then_inc(step("x_in"), 16)

            def store_tail(t):
                done(sp, "x2", t)
                hold(sp)
                sp.dma_start(dram_rows(x2_d, t * P, P), x2).then_inc(step("tail_stored"), 16)
                done(sp, "h2", t)
                hold(sp)
                sp.dma_start(dram_rows(h2_d, t * P, P), h2).then_inc(step("tail_stored"), 16)
                done(sp, "lg", t)
                hold(sp)
                sp.dma_start(dram_rows(lg_d, t * P, P), lg).then_inc(step("tail_stored"), 16)

            for t in range(2):
                body(t, t)
            with sp.Fori(1, NT // 2 - 1) as i:
                body(i * 2, 0)
                body(i * 2 + 1, 1)
            body(NT - 2, 0)
            body(NT - 1, 1, True)
            freed(sp, "slin_mm", NT, 2)
            sp.dma_start(tok[0][0:NS, :], tok_d[NT * P:NT * P + NS, :]).then_inc(step("tok_in0"), 16)
            done(sp, "tU", NT - 1, 7, 7)
            done(sp, "o2_mm", NT - 1)
            done(sp, "sdn_mm", NT - 1)
            sin = step("sconv_in")
            sp.dma_start(cwb, A["dn_conv_w"][0].rearrange("i c -> (i c)").partition_broadcast(NS)).then_inc(sin, 16)
            sp.dma_start(sconv, A["state_conv"][0].rearrange("b r c -> b (r c)")).then_inc(sin, 16)
            sp.dma_start(qkv[0:NS, :], sqkv_d).then_inc(sin, 16)
            done(sp, "s_lin", NT - 1)
            done(sp, "s_dn", NT - 1)
            st = step("states_stored")
            for head in range(10):
                dt, row, K, _ = head_place(head)
                c = DT_VALS[dt] + DV * DT_HEADS[dt].index(head)
                dst = O[2][0, 0, head] if head < H_GLA else O[5][0, 0, head - H_GLA]
                sp.dma_start(dst, s_lin[row:row + K, c:c + DV]).then_inc(st, 16)
            for h in range(H_DN):
                sp.dma_start(O[3][0, 0, h], s_dn[64 * (h % 2):64 * (h % 2) + 64, DV * h:DV * h + DV]).then_inc(st, 16)
            for c in range(CT):
                sp.dma_start(O[4][0, 0, :, c * P:(c + 1) * P].rearrange("r p -> p r"),
                             xc[1][:, c, P:P + 3], allow_slow_non_contiguous=True).then_inc(st, 16)
            done(sp, "masked_dn", NT - 1)
            sp.wait_ge(st, 16 * (16 + CT))
            sp.sem_inc(step("s_space"), 1)
            sp.wait_ge(step("s_zero"), 2)
            sd_in = step("s_states_in")
            sp.dma_start(sstate[R_HG, :], A["state_hgrn"][0].rearrange("b h k e -> (b h) (k e)")).then_inc(sd_in, 16)
            sp.dma_start(sstate[R_GLA, 0:2048], A["state_gla"][0].rearrange("b h k e -> (b h) (k e)")).then_inc(sd_in, 16)
            sp.dma_start(sstate[R_DN, :], A["state_dn"][0].rearrange("b h k e -> (b h) (k e)")).then_inc(sd_in, 16)
            sp.wait_ge(sin, 48)
            sp.dma_start(O[8][0, :, 0:2, :].rearrange("b r c -> b (r c)"), sconv[:, CONV:3 * CONV]).then_inc(st, 16)
            sp.dma_start(O[8][0, :, 2, :], qkv[0:NS, :]).then_inc(st, 16)
            done(sp, "s_gq", 0)
            done(sp, "s_ex", 0)
            done(sp, "hk", NT)
            done(sp, "hqs", NT)
            done(sp, "beta", NT)
            R8 = slice(0, NS)
            q, k, dec, val = 0, 64, 128, 192
            moves = [(tok[0][R8, GQ:GQ + 192], 6, 32, vec[R_GLA, q:q + 32]),
                     (tok[0][R8, GK:GK + 192], 6, 32, vec[R_GLA, k:k + 32]),
                     (ex[R8, 0:192], 6, 32, vec[R_GLA, dec:dec + 32]),
                     (tok[0][R8, GV:GV + 384], 6, 64, vec[R_GLA, val:val + 64]),
                     (gc[R8, 1024:1280], 4, 64, vec[R_HG, q:q + 64]), (hk[R8, :], 4, 64, vec[R_HG, k:k + 64]),
                     (ex[R8, LG_H:LG_D], 4, 64, vec[R_HG, dec:dec + 64]),
                     (tok[0][R8, HI:HI + 256], 4, 64, vec[R_HG, val:val + 64]),
                     (ex[R8, LG_D:LG_B], 6, 1, s_decay),
                     (beta[R8, :], 6, 1, s_beta)]
            late_moves = [(cv[R8, 384 * n:384 * n + 384], 6, 64, vec[R_DN, c:c + 64]) for n, c in enumerate((q, k, val))]
            place = [0]

            def relay(moves, out, back):
                spots = []
                for src, h, d, _ in moves:
                    spots.append(rows_d[place[0]:place[0] + NS * h * d])
                    sp.dma_start(spots[-1].rearrange("(b c) -> b c", b=NS), src).then_inc(out, 16)
                    place[0] += NS * h * d
                sp.wait_ge(out, 16 * len(moves))
                for spot, (_, h, d, dst) in zip(spots, moves):
                    sp.dma_start(dst, spot.rearrange("(r d) -> r d", d=d)).then_inc(back, 16)

            relay(moves, step("rows_out"), step("rows_back"))
            done(sp, "s_rows", 0)
            relay(late_moves, step("late_out"), step("late_back"))
            store_tail(NT - 1)
            done(sp, "s_out", 0)
            for n, (ap, h) in enumerate(((so[R_GLA, :], 6), (so[R_DN, :], 6), (so[R_HG, :], 4))):
                sp.dma_start(so_d[:, 384 * n:384 * n + 64 * h].rearrange("b (h e) -> b h e", e=DV), ap).then_inc(step("o_out"), 16)
            sp.dma_start(O[6][0].rearrange("b h k e -> (b h) (k e)"), sstate[R_GLA, 0:2048]).then_inc(st, 16)
            sp.dma_start(O[7][0].rearrange("b h k e -> (b h) (k e)"), sstate[R_DN, :]).then_inc(st, 16)
            sp.dma_start(O[9][0].rearrange("b h k e -> (b h) (k e)"), sstate[R_HG, :]).then_inc(st, 16)
            sp.wait_ge(step("o_out"), 48)
            tail_free(sp, NT)
            sp.dma_start(oc[0:NS, :], so_d).then_inc(step("so_in"), 16)
            sp.dma_start(x2[0:NS, :], A["x_sample"].rearrange("b s d -> (b s) d")).then_inc(step("x_in"), 16)
            rows_s = slice(NT * P, NT * P + NS)
            for name, dst, src in (("x2", x2_d, x2), ("h2", h2_d, h2), ("lg", lg_d, lg)):
                done(sp, name, NT)
                sp.dma_start(dst[rows_s, :], src[0:NS, :]).then_inc(step("tail_stored"), 16)
            sp.wait_ge(st, 16 * (16 + CT + 5))
            sp.wait_ge(step("tail_stored"), 48 * (NT + 1))

        @block.gpsimd
        def _(pool):
            g = nc.gpsimd
            g.memset(xc[1][:, :, 128:131], 0.0).then_inc(step("pool_const"), 1)
            g.memset(att, 0.0).then_inc(step("pool_const"), 1)
            pool.wait_ge(step("pool_const"), 2)

            def convolve(t, u):
                loaded(pool, "xc_in", t, u)
                hold(pool)
                g.tensor_copy(xc[u][:, :, 0:3], xc[1 - u][:, :, 128:131]).then_inc(step("halo"), 1)
                done(pool, "halo", t)
                freed(pool, "cvT_mm", t)
                if not (isinstance(t, int) and t == 0):
                    freed(pool, "atd", t)
                hold(pool)

                def tap(i):
                    return xc[u][:, :, i:i + P], cw[:, :, i:i + 1].to_broadcast([P, CT, P])

                g.tensor_tensor(cv3, *tap(0), ALU.mult).then_inc(step("tap"), 1)
                for i in range(1, 4):
                    done(pool, "tap", t, 2 * i - 1, 6)
                    hold(pool)
                    g.tensor_tensor(conv_part, *tap(i), ALU.mult).then_inc(step("tap"), 1)
                    done(pool, "tap", t, 2 * i, 6)
                    hold(pool)
                    g.tensor_tensor(cv3, cv3, conv_part, ALU.add).then_inc(step("tap" if i < 3 else "conv"), 1)

            def body(t, u, last=False):
                if not (isinstance(t, int) and t == 0):
                    forget_input(t, u)
                freed(pool, "vn_mm", t)
                hold(pool)
                g.tensor_copy(h3(T, P), b3(ident, 6, P))
                g.tensor_copy(h3(U, P), b3(ident, 6, P)).then_inc(step("tu_init"), 1)
                done(pool, "la", t)
                freed(pool, "tU_mm", t, 1, 6)
                for b in range(2):
                    ins = g.tensor_tensor(h3(gl[:, 384 * b:384 * b + 384], P), bl(la[:, LG_D + b:LG_B:2], P),
                                          b3(suf, 3, P), ALU.mult)
                ins.then_inc(step("gl"), 1)
                done(pool, "ex", t)
                done(pool, "hk", t)
                freed(pool, "slin_mm", t)
                g.tensor_tensor(kdg[:, 0:192], tok[u][:, GK:GK + 192], ex[:, 0:192], ALU.mult)
                g.tensor_tensor(kdg[:, 192:448], hk, ex[:, LG_H:LG_D], ALU.mult).then_inc(step("kdg"), 1)
                gates(t)
                done(pool, "gam_exp", t)
                freed(pool, "atd", t)
                g.tensor_tensor(h3(gtm, P), h3(gt, P), b3(nstrict, 6, P), ALU.mult).then_inc(step("gtm"), 1)
                g.tensor_tensor(h3(gti, P), h3(gt, P), b3(cum, 6, P), ALU.mult).then_inc(step("gti"), 1)
                done(pool, "qkn", t)
                done(pool, "beta", t)
                freed(pool, "r", t)
                g.tensor_tensor(h3(vb), h3(qkv[:, 768:1152]), bl(beta, DV), ALU.mult).then_inc(step("vb"), 1)
                freed(pool, "sdn_mm", t)
                g.tensor_tensor(h3(kd), h3(qkv[:, 384:768]), bl(ex[:, LG_D:LG_B], 64), ALU.mult).then_inc(step("kd"), 1)
                for dt in range(4):
                    R = slice(0, DT_ROWS[dt])
                    done(pool, "e_exp", t, dt + 1, 4)
                    done(pool, "k2", t)
                    if dt == 0:
                        freed(pool, "s_dn", t)
                    ins = g.tensor_tensor(h3(zk[dt % 2][R, :], P), h3(E[dt % 2][R, :], P)[:, 0:7, :],
                                          b3(k_of(dt, R), 7, P), ALU.mult)
                    if dt:
                        done(pool, "q2", t)
                        ins = g.tensor_tensor(h3(zq[dt % 2][R, :], P), h3(E[dt % 2][R, :], P)[:, 0:7, :],
                                              b3(q_of(dt, R), 7, P), ALU.mult)
                    ins.then_inc(step("zks"), 1)
                if not last:
                    convolve(t + 1, 1 - u)

            def forget_input(t, u):
                loaded(pool, "tok_in", t, u)
                freed(pool, "ls", t)
                hold(pool)
                g.tensor_copy(z[:, LG_H:LG_D], tok[u][:, HF:HF + 256]).then_inc(step("zf"), 1)

            def gates(t):
                done(pool, "hqs", t)
                g.tensor_tensor(gc[:, 0:768], gc[:, 0:768], ge[:, 0:768], ALU.mult).then_inc(step("gn1"), 1)
                done(pool, "gn1", t)
                g.tensor_tensor(gc[:, 0:768], gc[:, 0:768], ng[:, 0:768], ALU.mult).then_inc(step("gn"), 1)

            pool.wait_ge(params, params_all[0])
            pool.wait_ge(consts_in, 32)
            forget_input(0, 0)
            convolve(0, 0)
            for t in range(2):
                body(t, t)
            with pool.Fori(1, NT // 2 - 1) as i:
                for u in range(2):
                    body(i * 2 + u, u)
            body(NT - 2, 0)
            body(NT - 1, 1, True)
            loaded(pool, "tok_in", NT, 0)
            freed(pool, "ls", NT)
            g.tensor_copy(z[:, LG_H:LG_D], tok[0][:, HF:HF + 256]).then_inc(step("zf"), 1)
            pool.wait_ge(step("s_space"), 1)
            done(pool, "sdn_mm", NT - 1)
            g.memset(sstate, 0.0).then_inc(step("s_zero"), 1)
            g.memset(vec, 0.0).then_inc(step("s_zero"), 1)
            gates(NT)

        @block.scalar
        def _(act):
            one_table(nc)
            a = nc.scalar.activation

            act.wait_ge(params, params_all[0])
            a(scl[:, LG_D:LG_B], scl[:, LG_D:LG_B], ACT.Exp).then_inc(step("setup"), 1)
            act.wait_ge(step("lb0"), 1)
            a(lb, lb, ACT.Exp).then_inc(step("lb1"), 1)

            def sigmoid(name, out, src, t, ready):
                done(act, ready, t)
                a(out, src, ACT.Exp, scale=-1.0).then_inc(step(name), 1)
                done(act, name, t, 1, 3)
                a(out, out, ACT.Ln, bias=1.0).then_inc(step(name), 1)
                done(act, name, t, 2, 3)
                a(out, out, ACT.Exp, scale=-1.0).then_inc(step(name), 1)

            def prep(t, late=True):
                done(act, "alT_mm", t)
                a(alT[0:16, :], bank[0][0:16, 0:P], ACT.Copy).then_inc(step("alT"), 1)
                if late:
                    put_oT(t - 1)
                done(act, "z", t)
                done(act, "zf", t)
                freed(act, "ls", t)
                a(ab, z, ACT.Abs).then_inc(step("ab"), 1)
                done(act, "ab", t, 1, 3)
                a(ab, ab, ACT.Exp, scale=-1.0).then_inc(step("ab"), 1)
                done(act, "xe", t)
                a(xe, xe, ACT.Exp, scale=-1.0).then_inc(step("xe_exp"), 1)
                done(act, "ab", t, 2, 3)
                a(ab, ab, ACT.Ln, bias=1.0).then_inc(step("ab"), 1)
                freed(act, "gn", t)
                done(act, "gc", t)
                a(ge, gc, ACT.Exp, scale=-1.0).then_inc(step("ge"), 1)
                done(act, "ge", t, 1, 3)
                a(ge, ge, ACT.Ln, bias=1.0).then_inc(step("ge"), 1)
                done(act, "xel", t)
                a(xe, xe, ACT.Ln, bias=1.0).then_inc(step("xe_ln"), 1)
                done(act, "hkarg", t)
                a(hk, hk, ACT.Exp).then_inc(step("hk_exp"), 1)
                done(act, "ge", t, 2, 3)
                a(ge, ge, ACT.Exp, scale=-1.0).then_inc(step("ge"), 1)
                done(act, "la", t)
                freed(act, "vb", t)
                a(beta, la[:, LG_B:LG], ACT.Exp).then_inc(step("beta"), 1)

            def body(t, u):
                late = not (isinstance(t, int) and t == 0)
                prep(t, late)
                freed(act, "sso", t)
                sigmoid("ce", ce, cv, t, "cv")
                done(act, "sums_mm", t)
                freed(act, "s_dn", t)
                a(ex, bank[0][:, 0:466], ACT.Exp).then_inc(step("ex"), 1)
                done(act, "linT_mm", t)
                freed(act, "lin_mm", t, 1, LIN)
                a(q_of(0), bank[1][:, 0:P], ACT.Copy, scale=DK_GLA ** -0.5)
                a(q_of(1, slice(0, 64)), bank[1][0:64, P:2 * P], ACT.Copy, scale=DK_GLA ** -0.5)
                a(qk2[:, 2:4, :], h3(bank[1][:, 256:512], P), ACT.Copy).then_inc(step("q2"), 1)
                done(act, "cvT_mm", t)
                for c in range(3):
                    ins = a(qkv[:, 384 * c:384 * c + 384], bank[3 + c][:, 0:384], ACT.Copy)
                ins.then_inc(step("cvT_out"), 1)
                done(act, "cvT_out", t)
                done(act, "cs", t)
                a(ce[:, 0:768], qkv[:, 0:768], ACT.Square).then_inc(step("sqd"), 1)
                done(act, "gam_mm", t)
                a(halves(gt), pair_of(6)[:, :, 0:384], ACT.Exp).then_inc(step("gam_exp"), 1)
                done(act, "ssd", t)
                a(rs, ssd, ACT.Ln, bias=eps).then_inc(step("rs"), 1)
                done(act, "rs", t, 1, 2)
                a(rs[:, 0:6], rs[:, 0:6], ACT.Exp, scale=-0.5, bias=ln8)
                a(rs[:, 6:12], rs[:, 6:12], ACT.Exp, scale=-0.5).then_inc(step("rs"), 1)
                done(act, "dqT_mm", t)
                for c in range(3):
                    ins = a(dqT[:, 3 * c:3 * c + 3, :], bank[3 + c][:, 0:384].rearrange("p (c t) -> p c t", c=3), ACT.Copy)
                ins.then_inc(step("dqT_out"), 1)
                if late:
                    norm2(t - 1)
                    put_h2T(t - 1)

                def decays(dt):
                    done(act, "cum_mm", t, dt + 1, 4)
                    if dt >= 2:
                        done(act, "zs", t, dt - 1, 4)
                        done(act, "zks", t, dt - 1, 4)
                    for b in range(2):
                        ins = a(E[dt % 2][0:DT_ROWS[dt], 512 * b:512 * b + 512], bank[b][0:DT_ROWS[dt], :], ACT.Exp)
                    ins.then_inc(step("e_exp"), 1)

                decays(0)
                for what, n in order:
                    if what == "P" and n:
                        done(act, "p_mm", t, n + 1, 7)
                        a(halves(pm), pair_of(2)[:, :, 0:384], ACT.Copy).then_inc(step("pm"), 1)
                    elif what == "lin" and LIN_STEPS[n][1:] == (0, 0) and LIN_STEPS[n][0] < 3:
                        decays(LIN_STEPS[n][0] + 1)
                done(act, "olin_mm", t)
                freed(act, "h2T_mm", t)
                tail_free(act, t)
                a(oc[:, 0:384], bank[0][:, 0:384], ACT.Copy).then_inc(step("oc_gla"), 1)
                done(act, "vn_mm", t)
                a(vn, bank[2][:, 0:384], ACT.Copy).then_inc(step("vn_out"), 1)
                done(act, "oc_gla", t)
                head_norm(t)

            def head_norm(t):
                done(act, "oc_pre", t)
                a(sq2[:, 0:D], oc, ACT.Square).then_inc(step("sqo"), 1)
                done(act, "sso", t)
                a(rso, sso, ACT.Ln, scale=1.0 / DV, bias=eps).then_inc(step("rso"), 1)
                done(act, "rso", t, 1, 2)
                a(rso, rso, ACT.Exp, scale=-0.5).then_inc(step("rso"), 1)

            def put_oT(t):
                done(act, "oT_mm", t)
                a(oT[:, 0:512], bank[4][:, :], ACT.Copy).then_inc(step("oT_a"), 1)

            def norm2(t):
                done(act, "x2", t)
                freed(act, "h2", t)
                a(sq_junk, x2, ACT.Square, accum_out=st2[:, 0:1]).then_inc(step("sqo_used"), 1)
                done(act, "sqo_used", t)
                a(st2[:, 1:2], st2[:, 0:1], ACT.Ln, scale=1.0 / D, bias=eps).then_inc(step("rs2"), 1)
                done(act, "rs2", t, 1, 2)
                a(st2[:, 2:3], st2[:, 1:2], ACT.Exp, scale=-0.5).then_inc(step("rs2"), 1)

            def put_h2T(t):
                done(act, "h2T_mm", t)
                a(h2T[:, 0:512], bank[1][:, :], ACT.Copy).then_inc(step("h2T_a"), 1)

            def tail(t):
                put_oT(t)
                norm2(t)
                put_h2T(t)

            act.wait_ge(step("setup"), 6)
            tiles(act, body, NT)
            prep(NT)
            done(act, "la", NT)
            freed(act, "s_dn", NT)
            R8 = slice(0, NS)
            a(ex[R8, 0:LG_B], la[R8, 0:LG_B], ACT.Exp).then_inc(step("s_ex"), 1)
            freed(act, "sso", NT)
            sigmoid("s_ce", ce[R8, :], cv[R8, :], 0, "s_conv")
            norm2(NT - 1)
            done(act, "s_cs", 0)
            a(ce[R8, 0:768], cv[R8, 0:768], ACT.Square).then_inc(step("s_sq"), 1)
            done(act, "s_ss", 0)
            a(rs[R8, :], ssd[R8, :], ACT.Ln, bias=eps[R8, :]).then_inc(step("s_rs"), 1)
            done(act, "s_rs", 0, 1)
            a(rs[R8, 0:6], rs[R8, 0:6], ACT.Exp, scale=-0.5, bias=ln8[R8, :])
            a(rs[R8, 6:12], rs[R8, 6:12], ACT.Exp, scale=-0.5).then_inc(step("s_rs"), 1)
            put_h2T(NT - 1)
            head_norm(NT)
            tail(NT)

        @block.vector
        def _(dve):
            v = nc.vector
            tt, ts, cp = v.tensor_tensor, v.tensor_scalar, v.tensor_copy
            setup = step("setup")
            v.memset(eps, EPS)
            v.memset(ln8, math.log(DK_DN ** -0.5))
            v.memset(scl[:, 0:LG_H], 1.0 / 16.0)
            v.memset(scl[:, LG_H:LG_D], 1.0)
            v.memset(scl[:, LG_B:LG], 1.0)
            v.memset(s_lin, 0.0)
            v.memset(s_dn, 0.0).then_inc(setup, 1)
            dve.wait_ge(params, params_all[0])
            dve.wait_ge(consts_in, 32)
            ts(ndtb, ndtb, -1.0, None, ALU.mult).then_inc(setup, 1)
            tt(lb, sm, sm, ALU.subtract).then_inc(step("lb0"), 1)
            dve.wait_ge(step("lb1"), 1)
            v.reciprocal(sm, lb).then_inc(step("lb0"), 1)
            dve.wait_ge(step("lb0"), 2)
            tt(sm, sm, lb, ALU.mult).then_inc(step("lb0"), 1)
            dve.wait_ge(step("lb0"), 3)
            tt(lb, sm, sm, ALU.subtract).then_inc(setup, 1)
            dve.wait_ge(setup, 4)
            ts(lb, lb, 0.0, None, ALU.max).then_inc(setup, 1)
            dve.wait_ge(setup, 5)
            ts(oml, lb, -1.0, 1.0, ALU.mult, ALU.add).then_inc(setup, 1)

            def prep(t, u):
                loaded(dve, "tok_in", t, u)
                freed(dve, "gn", t)
                freed(dve, "oc", t)
                freed(dve, "linT_mm", t)
                for n, c, w in ((0, GG, 384), (384, DG, 384), (768, HG, 256), (1024, HQ, 256)):
                    ins = ts(gc[:, n:n + w], tok[u][:, c:c + w], CLAMP, None, ALU.max)
                ins.then_inc(step("gc"), 1)
                ts(xe, tok[u][:, HF:HF + 256], CLAMP, None, ALU.max).then_inc(step("xe"), 1)
                v.scalar_tensor_tensor(z[:, LG_D:LG_B], tok[u][:, DA:DA + 6], -1.0, ndtb, ALU.mult, ALU.add)
                cp(z[:, LG_B:LG], tok[u][:, DB:DB + 6])
                done(dve, "z_mm", t)
                tt(z[:, 0:LG_H], bank[1][:, 0:192], ba, ALU.add).then_inc(step("z"), 1)
                if not (isinstance(t, int) and t == 0):
                    put_oT(t - 1)
                done(dve, "ab", t, 3, 3)
                freed(dve, "gl", t)
                v.scalar_tensor_tensor(la, z, 0.0, ab, ALU.min, ALU.subtract).then_inc(step("ls"), 1)
                done(dve, "xe_exp", t)
                tt(xe, xe, lb, ALU.mult).then_inc(step("xel"), 1)
                done(dve, "ls", t)
                freed(dve, "kdg", t)
                tt(hk, la[:, LG_H:LG_D], tok[u][:, HF:HF + 256], ALU.subtract).then_inc(step("hkarg"), 1)
                done(dve, "hkarg", t)
                tt(la, la, scl, ALU.mult).then_inc(step("la_scl"), 1)
                done(dve, "la_scl", t)
                done(dve, "xe_ln", t)
                tt(la[:, LG_H:LG_D], la[:, LG_H:LG_D], xe, ALU.add).then_inc(step("la"), 1)
                done(dve, "hk_exp", t)
                tt(hk, hk, oml, ALU.mult).then_inc(step("hk"), 1)
                if not (isinstance(t, int) and t == NT):
                    done(dve, "conv", t)
                    ts(cv, cv, CLAMP, None, ALU.max).then_inc(step("cv"), 1)
                done(dve, "ge", t, 3, 3)
                tt(gc[:, 1024:1280], gc[:, 1024:1280], ge[:, 1024:1280], ALU.mult).then_inc(step("hqs"), 1)

            def body(t, u):
                prep(t, u)
                late = not (isinstance(t, int) and t == 0)
                done(dve, "ce", t, 3, 3)
                tt(cv, cv, ce, ALU.mult).then_inc(step("cs"), 1)
                if late:
                    residual_a(t - 1)
                done(dve, "linT_mm", t)
                cp(k_of(0), bank[2][:, 0:P])
                cp(k_of(1, slice(0, 64)), bank[2][0:64, P:2 * P])
                cp(qk2[:, 6:8, :], h3(bank[2][:, 256:512], P)).then_inc(step("k2"), 1)
                done(dve, "sqd", t)
                v.tensor_reduce(ssd, h3(ce[:, 0:768]), AX, ALU.add).then_inc(step("ssd"), 1)
                done(dve, "rs", t, 2, 2)
                tt(h3(qkv[:, 0:768]), h3(qkv[:, 0:768]), bl(rs, 64), ALU.mult).then_inc(step("qkn"), 1)
                done(dve, "qkn", t)
                done(dve, "beta", t)
                tt(h3(kb), h3(qkv[:, 384:768]), bl(beta, 64), ALU.mult).then_inc(step("kb"), 1)
                if late:
                    residual_b(t - 1)
                    norm2(t - 1)
                done(dve, "a_mm", t)
                done(dve, "gtm", t)
                tt(halves(nm), pair_of(6)[:, :, 0:384], halves(gtm), ALU.mult).then_inc(step("nm"), 1)
                done(dve, "att_mm", t)
                done(dve, "gti", t)
                tt(halves(atd), pair_of(3)[:, :, 0:384], halves(gti), ALU.mult).then_inc(step("atd"), 1)
                if late:
                    put_h2T(t - 1)

                def scaled(dt):
                    R = slice(0, DT_ROWS[dt])
                    done(dve, "e_exp", t, dt + 1, 4)
                    done(dve, "q2", t)
                    e3 = h3(E[dt % 2][R, :], P)
                    freed(dve, "olin_mm", t)
                    tt(qs[R, dt * P:dt * P + P], e3[:, 7, :], q_of(dt, R), ALU.mult)
                    ins = cp(el[R, dt:dt + 1], E[dt % 2][R, 1023:1024])
                    if dt == 0:
                        ins = tt(h3(zq[0][R, :], P), e3[:, 0:7, :], b3(q_of(0, R), 7, P), ALU.mult)
                    ins.then_inc(step("zs"), 1)

                scaled(0)
                if late:
                    logits(t - 1)
                for what, n in order:
                    if what == "lin":
                        dt, pair, half = LIN_STEPS[n]
                        done(dve, "lin_mm", t, n + 1, LIN)
                        hold(dve)
                        if n == 0:
                            dve.wait_ge(step("pool_const"), 2)
                        h = DT_HEADS[dt][2 * pair]
                        for j in range(4):
                            if j:
                                done(dve, "lin_put", t, 4 * n + j, 4 * LIN)
                                hold(dve)
                            v.copy_predicated(h3(att[:, h * P:(h + 2) * P], P), b3(q_mask[4 * half + j], 2, P),
                                              pair_of(6)[:, :, j * P:j * P + P]).then_inc(step("lin_put"), 1)
                        if (pair, half) == (0, 0) and dt < 3:
                            scaled(dt + 1)
                    elif what == "TU":
                        if n < 6:
                            if n:
                                done(dve, "tT_mm", t, n, 5)
                            else:
                                done(dve, "p_mm", t, 1, 7)
                                done(dve, "tu_init", t)
                                done(dve, "nm", t)
                            hold(dve)
                            for b in range(2):
                                ins = v.copy_predicated(h3(T[:, 384 * b:384 * b + 384], P), b3(lower[n], 3, P),
                                                        h3(bank[(4 if n else 2) + b][:, 0:384], P))
                            ins.then_inc(step("tT"), 1)
                        if n:
                            done(dve, "tU_mm", t, n, 6)
                            hold(dve)
                        for b in range(2):
                            src = bank[(0 if n < 6 else 2) + b][:, 0:384] if n else nm[:, 384 * b:384 * b + 384]
                            ins = v.copy_predicated(h3(U[:, 384 * b:384 * b + 384], P), b3(upper[n], 3, P), h3(src, P))
                        ins.then_inc(step("tU"), 1)
                done(dve, "ks_mm", t)
                egc = bl(ex[:, 454:460], DV)
                tt(h3(r), h3(bank[4][:, 0:384]), egc, ALU.mult).then_inc(step("r0"), 1)
                done(dve, "r0", t)
                done(dve, "vb", t)
                tt(r, vb, r, ALU.subtract).then_inc(step("r"), 1)
                freed(dve, "h2T_mm", t)
                tail_free(dve, t)
                tt(h3(oc[:, 384:768]), h3(bank[5][:, 0:384]), egc, ALU.mult).then_inc(step("oc_dn"), 1)
                done(dve, "olin_mm", t)
                tt(oc[:, 768:1024], bank[1][:, 0:256], ge[:, 768:1024], ALU.mult)
                tt(h3(s_dn), h3(s_dn), bl(ex[:, 460:466], DV), ALU.mult).then_inc(step("s_dn0"), 1)
                done(dve, "o2_mm", t)
                done(dve, "oc_dn", t)
                tt(oc[:, 384:768], oc[:, 384:768], bank[3][:, 0:384], ALU.add).then_inc(step("oc_pre"), 1)
                done(dve, "slin_mm", t)
                tt(masked[:, 0:256], bank[6][:, 0:256], m32, ALU.mult)
                tt(masked[0:64, 256:384], bank[6][0:64, 256:384], m32[0:64, 0:P], ALU.mult)
                tt(masked[:, 384:512], bank[6][:, 384:512], m64, ALU.mult)
                tt(masked[:, 512:640], bank[7][:, 0:P], m64, ALU.mult).then_inc(step("masked"), 1)
                head_sums(t)
                done(dve, "masked", t)
                for dt in range(4):
                    R, C = slice(0, DT_ROWS[dt]), slice(DT_VALS[dt], DT_VALS[dt] + DV * len(DT_HEADS[dt]))
                    ins = v.scalar_tensor_tensor(s_lin[R, C], s_lin[R, C], el[R, dt:dt + 1], masked[R, C],
                                                 ALU.mult, ALU.add)
                ins.then_inc(step("s_lin"), 1)
                head_scale(t)
                done(dve, "sdn_mm", t)
                done(dve, "s_dn0", t)
                done(dve, "s_lin", t)
                tt(h3(masked[:, 0:384], P), h3(bank[2][:, 0:384], P), b3(m64, 3, P), ALU.mult).then_inc(step("masked_dn"), 1)
                done(dve, "masked_dn", t)
                tt(s_dn, s_dn, masked[:, 0:384], ALU.add).then_inc(step("s_dn"), 1)

            def head_sums(t):
                done(dve, "sqo", t)
                v.tensor_reduce(sso, h3(sq2[:, 0:D]), AX, ALU.add).then_inc(step("sso"), 1)

            def head_scale(t):
                done(dve, "rso", t, 2, 2)
                tt(h3(oc), h3(oc), bl(rso, DV), ALU.mult).then_inc(step("oc_n"), 1)
                done(dve, "oc_n", t)
                done(dve, "gn", t)
                tt(oc[:, 0:768], oc[:, 0:768], gc[:, 0:768], ALU.mult)
                tt(oc[:, 768:1024], oc[:, 768:1024], ng[:, 768:1024], ALU.mult).then_inc(step("oc"), 1)

            def put_oT(t):
                done(dve, "oT_mm", t)
                cp(oT[:, 512:1024], bank[5][:, :]).then_inc(step("oT_b"), 1)

            def residual_a(t):
                done(dve, "wo_a", t)
                dve.wait_ge(step("x_in"), t * 16 + 16)
                tt(x2[:, 0:512], x2[:, 0:512], bank[6][:, :], ALU.add).then_inc(step("x2a"), 1)

            def residual_b(t):
                done(dve, "wo_b", t)
                tt(x2[:, 512:1024], x2[:, 512:1024], bank[0][:, :], ALU.add).then_inc(step("x2"), 1)

            def norm2(t):
                done(dve, "rs2", t, 2, 2)
                v.scalar_tensor_tensor(h2, x2, st2[:, 2:3], g2, ALU.mult, ALU.mult).then_inc(step("h2"), 1)

            def put_h2T(t):
                done(dve, "h2T_mm", t)
                cp(h2T[:, 512:1024], bank[2][:, :]).then_inc(step("h2T_b"), 1)

            def logits(t):
                done(dve, "rt_mm", t)
                tt(lg, bank[5][:, 0:36], rb, ALU.add).then_inc(step("lg"), 1)

            def tail(t):
                put_oT(t)
                residual_a(t)
                residual_b(t)
                norm2(t)
                put_h2T(t)
                logits(t)

            dve.wait_ge(setup, 6)
            tiles(dve, body, NT)
            prep(NT, 0)
            R8 = slice(0, NS)
            ts(tok[0][R8, GQ:GQ + 192], tok[0][R8, GQ:GQ + 192], DK_GLA ** -0.5, None, ALU.mult).then_inc(step("s_gq"), 1)
            dve.wait_ge(step("sconv_in"), 48)
            done(dve, "sso", NT - 1)
            n = [0]

            def then(ins):
                ins.then_inc(step("s_chain"), 1)
                n[0] += 1
                dve.wait_ge(step("s_chain"), n[0])

            def cw8(i):
                return cwb[:, i * CONV:(i + 1) * CONV]

            then(tt(cv[R8, :], sconv[:, 0:CONV], cw8(0), ALU.mult))
            for i in range(1, 4):
                src = sconv[:, i * CONV:(i + 1) * CONV] if i < 3 else qkv[R8, :]
                then(tt(ce[R8, :], src, cw8(i), ALU.mult))
                then(tt(cv[R8, :], cv[R8, :], ce[R8, :], ALU.add))
            ts(cv[R8, :], cv[R8, :], CLAMP, None, ALU.max).then_inc(step("s_conv"), 1)
            residual_a(NT - 1)
            residual_b(NT - 1)
            done(dve, "s_ce", 0, 3)
            tt(cv[R8, :], cv[R8, :], ce[R8, :], ALU.mult).then_inc(step("s_cs"), 1)
            norm2(NT - 1)
            done(dve, "s_sq", 0)
            v.tensor_reduce(ssd[R8, :], h3(ce[R8, 0:768]), AX, ALU.add).then_inc(step("s_ss"), 1)
            done(dve, "s_rs", 0, 2)
            tt(h3(cv[R8, 0:768]), h3(cv[R8, 0:768]), bl(rs[R8, :], 64), ALU.mult).then_inc(step("s_rows"), 1)
            put_h2T(NT - 1)
            logits(NT - 1)
            dve.wait_ge(step("rows_back"), 16 * 10)
            dve.wait_ge(step("late_back"), 16 * 3)
            dve.wait_ge(step("s_states_in"), 48)
            s3 = sstate.rearrange("p (k e) -> p k e", e=DV)
            tmp = big2[:, 0:64 * DV].rearrange("p (k e) -> p k e", e=DV)

            def over_v(ap):
                return ap.unsqueeze(2).to_broadcast([ap.shape[0], 64, DV])

            def over_k(ap):
                return ap.unsqueeze(1).to_broadcast([ap.shape[0], 64, DV])

            then(cp(s_dec[R_DN, :], s_decay.to_broadcast([48, 64])))
            then(tt(s3, s3, over_v(s_dec), ALU.mult))
            then(tt(tmp[R_DN], s3[R_DN], over_v(s_k[R_DN, :]), ALU.mult))
            then(v.tensor_reduce(ks, tmp[R_DN].rearrange("p k e -> p e k"), AX, ALU.add))
            then(tt(s_val[R_DN, :], s_val[R_DN, :], ks, ALU.subtract))
            then(ts(s_val[R_DN, :], s_val[R_DN, :], s_beta, None, ALU.mult))
            then(tt(tmp, over_v(s_k), over_k(s_val), ALU.mult))
            then(tt(s3, s3, tmp, ALU.add))
            then(tt(tmp, s3, over_v(s_q), ALU.mult))
            v.tensor_reduce(so, tmp.rearrange("p k e -> p e k"), AX, ALU.add).then_inc(step("s_out"), 1)
            dve.wait_ge(step("so_in"), 16)
            tt(oc[R8, 768:1024], oc[R8, 768:1024], ge[R8, 768:1024], ALU.mult).then_inc(step("oc_pre"), 1)
            head_sums(NT)
            head_scale(NT)
            tail(NT)

        @block.tensor
        def _(pe):
            mm, tr = nc.tensor.matmul, nc.tensor.transpose

            def per_head(out, lhs, rhs):
                for h in (0, 2, 4, 1, 3, 5):
                    b, c = out[h % 2], h // 2
                    ins = mm(b[:, c * P:(c + 1) * P], lhs(h), rhs(h), start=True, stop=True)
                return ins

            def blk(ap, h):
                return ap[:, slot(h) * P:slot(h) * P + P]

            def dn(ap, h):
                return ap[64 * (h % 2):64 * (h % 2) + 64, h // 2, :]

            def low_rank(t, u):
                loaded(pe, "tok_in", t, u)
                freed(pe, "oc_gla", t)
                tr(bank[0][0:16, 0:P], tok[u][:, GA:GA + 16], ident).then_inc(step("alT_mm"), 1)
                freed(pe, "s_dn0", t)
                done(pe, "alT", t)
                mm(bank[1][:, 0:192], alT[0:16, :], wa2[0:16, :], start=True, stop=True).then_inc(step("z_mm"), 1)

            def body(t, u):
                low_rank(t, u)
                late = not (isinstance(t, int) and t == 0)
                if late:
                    turn_o(t - 1)
                    project_a(t - 1)
                done(pe, "la", t)
                mm(bank[0][:, 0:LG_B], suf, la[:, 0:LG_B], start=True, stop=True)
                mm(bank[0][:, 454:460], cum, la[:, LG_D:LG_B], start=True, stop=True)
                mm(bank[0][:, 460:466], ones, la[:, LG_D:LG_B], start=True, stop=True).then_inc(step("sums_mm"), 1)
                done(pe, "hqs", t)
                done(pe, "hk", t)
                freed(pe, "s_dn", t)
                for b, base in ((1, GQ), (2, GK)):
                    tr(bank[b][:, 0:P], tok[u][:, base:base + P], ident)
                    tr(bank[b][0:64, P:2 * P], tok[u][:, base + P:base + 192], ident)
                    src = gc[:, 1024:1280] if b == 1 else hk
                    for c in range(2):
                        ins = tr(bank[b][:, (2 + c) * P:(3 + c) * P], src[:, c * P:(c + 1) * P], ident)
                ins.then_inc(step("linT_mm"), 1)
                done(pe, "cs", t)
                for c in range(CT):
                    ins = tr(bank[3 + c // 3][:, (c % 3) * P:(c % 3 + 1) * P], cv3[:, c, :], ident)
                ins.then_inc(step("cvT_mm"), 1)
                done(pe, "gl", t)
                freed(pe, "x2a", t)
                per_head(bank[6:8], lambda h: blk(gl, h), lambda h: cum).then_inc(step("gam_mm"), 1)
                if late:
                    done(pe, "ex", t)
                    project_b(t - 1)
                done(pe, "kb", t)
                for c in range(CT):
                    src = qkv[:, c * P:(c + 1) * P] if c < 6 else kb[:, (c - 6) * P:(c - 5) * P]
                    ins = tr(bank[3 + c // 3][:, (c % 3) * P:(c % 3 + 1) * P], src, ident)
                ins.then_inc(step("dqT_mm"), 1)
                done(pe, "dqT_out", t)
                done(pe, "gam_exp", t)
                qT, kT, kbT = dqT[:, 0:3, :], dqT[:, 3:6, :], dqT[:, 6:9, :]
                per_head(bank[6:8], lambda h: dn(kT, h), lambda h: dn(kbT, h)).then_inc(step("a_mm"), 1)
                per_head(bank[3:5], lambda h: dn(kT, h), lambda h: dn(qT, h)).then_inc(step("att_mm"), 1)
                if late:
                    done(pe, "q2", t)
                    done(pe, "k2", t)
                    turn_h2(t - 1)

                last_level, summed = [0], [0]

                def sums(dt):
                    done(pe, "ex", t)
                    done(pe, "q2", t)
                    done(pe, "k2", t)
                    freed(pe, "x2", t)
                    freed(pe, "h2T_a", t)
                    if dt:
                        done(pe, "e_exp", t, dt, 4)
                    if last_level[0]:
                        done(pe, "tU", t, last_level[0] + 1, 7)
                    summed[0] = dt + 1
                    R = DT_ROWS[dt]
                    for b in range(2):
                        ins = mm(bank[b][0:R, :], la[:, DT_COLS[dt]:DT_COLS[dt] + R], lv[:, 512 * b:512 * b + 512],
                                 start=True, stop=True)
                    ins.then_inc(step("cum_mm"), 1)

                sums(0)
                done(pe, "nm", t)
                done(pe, "atd", t)
                for what, n in order:
                    if what == "P":
                        done(pe, "tT", t, n, 6) if n else done(pe, "tu_init", t)
                        if n == 0:
                            freed(pe, "h2T_b", t)
                        per_head(bank[2:4], lambda h: blk(nm, h), lambda h: blk(T, h)).then_inc(step("p_mm"), 1)
                        if n == 0 and late:
                            route(t - 1)
                    elif what == "TU":
                        if not n:
                            continue
                        done(pe, "pm", t, n, 6)
                        if n == 1:
                            freed(pe, "lg", t)
                        done(pe, "tU", t, n, 7)
                        if n < 6:
                            per_head(bank[4:6], lambda h: blk(U, h), lambda h: blk(pm, h)).then_inc(step("tT_mm"), 1)
                            done(pe, "e_exp", t, summed[0], 4)
                        b = 0 if n < 6 else 2
                        per_head(bank[b:b + 2], lambda h: blk(pm, h), lambda h: blk(U, h)).then_inc(step("tU_mm"), 1)
                        last_level[0] = n
                    else:
                        dt, pair, half = LIN_STEPS[n]
                        if (pair, half) == (0, 0):
                            if dt < 3:
                                sums(dt + 1)
                            done(pe, "zs", t, dt + 1, 4)
                            done(pe, "zks", t, dt + 1, 4)
                        if n:
                            done(pe, "lin_put", t, 4 * n, 4 * LIN)
                        for m in range(2):
                            _, row, K, _ = head_place(DT_HEADS[dt][2 * pair + m])
                            R = slice(row, row + K)
                            for j in range(4):
                                lvl = 4 * half + j
                                if lvl < 7:
                                    lhs, rhs = zk[dt % 2][R, lvl * P:lvl * P + P], zq[dt % 2][R, lvl * P:lvl * P + P]
                                else:
                                    lhs, rhs = k_of(dt, R), q_of(dt, R)
                                ins = mm(bank[6 + m][:, j * P:j * P + P], lhs, rhs, start=True, stop=True)
                        ins.then_inc(step("lin_mm"), 1)
                freed(pe, "s_dn", t)
                for b, src in ((4, kbT), (5, qT)):
                    for c in range(3):
                        C = slice(c * P, c * P + P)
                        ins = mm(bank[b][:, C], src[:, c, :], s_dn[:, C], start=True, stop=True)
                ins.then_inc(step("ks_mm"), 1)
                done(pe, "e_exp", t, 4, 4)
                done(pe, "zs", t, 4, 4)
                done(pe, "lin_put", t, 4 * LIN, 4 * LIN)
                freed(pe, "s_lin", t)
                for dt in range(4):
                    w, c = DV * len(DT_HEADS[dt]), DT_VALS[dt]
                    b, c = (bank[0], c) if dt < 2 else (bank[1], c - 384)
                    R = slice(0, DT_ROWS[dt])
                    mm(b[:, c:c + w], qs[R, dt * P:dt * P + P], s_lin[R, DT_VALS[dt]:DT_VALS[dt] + w],
                       start=(dt % 2 == 0), stop=False, skip_group_check=True)
                    for m, head in enumerate(DT_HEADS[dt]):
                        vcol = head_place(head)[3]
                        ins = mm(b[:, c + DV * m:c + DV * m + DV], att[:, head * P:head * P + P],
                                 tok[u][:, vcol:vcol + DV], start=False,
                                 stop=(dt % 2 == 1 and m == 1), skip_group_check=True)
                ins.then_inc(step("olin_mm"), 1)
                done(pe, "r", t)
                done(pe, "tU", t, 7, 7)
                for h in range(6):
                    ins = mm(bank[2][:, DV * h:DV * h + DV], blk(U, h), r[:, DV * h:DV * h + DV],
                             start=True, stop=True)
                ins.then_inc(step("vn_mm"), 1)
                done(pe, "kdg", t)
                for dt in range(4):
                    R, w, vcol = DT_ROWS[dt], DV * len(DT_HEADS[dt]), head_place(DT_HEADS[dt][0])[3]
                    o = bank[6][0:R, DT_VALS[dt]:DT_VALS[dt] + w] if dt < 3 else bank[7][:, 0:w]
                    ins = mm(o, kdg[:, DT_COLS[dt]:DT_COLS[dt] + R], tok[u][:, vcol:vcol + w], start=True, stop=True)
                ins.then_inc(step("slin_mm"), 1)
                done(pe, "vn_out", t)
                for h in range(6):
                    ins = mm(bank[3][:, DV * h:DV * h + DV], blk(atd, h), vn[:, DV * h:DV * h + DV],
                             start=True, stop=True)
                ins.then_inc(step("o2_mm"), 1)
                done(pe, "kd", t)
                for c in range(3):
                    C = slice(c * P, c * P + P)
                    ins = mm(bank[2][:, C], kd[:, C], vn[:, C], start=True, stop=True)
                ins.then_inc(step("sdn_mm"), 1)

            def turn_o(t):
                done(pe, "oc", t)
                if isinstance(t, int) and t == NT:
                    freed(pe, "lg", t)
                v = oc.rearrange("p (t c) -> p c t", c=KC)
                for c in range(KC):
                    ins = tr(bank[4 + c // 4][:, (c % 4) * P:(c % 4 + 1) * P], v[:, c, :], ident)
                ins.then_inc(step("oT_mm"), 1)

            def project_a(t):
                done(pe, "oT_a", t)
                done(pe, "oT_b", t)
                freed(pe, "x2a", t)
                if isinstance(t, int) and t == 0:
                    pe.wait_ge(step("w_out_in"), 16)
                if not (isinstance(t, int) and t == NT):
                    done(pe, "s_lin", t)
                for c in range(KC):
                    ins = mm(bank[6][:, :], oT[:, c * P:c * P + P], w_out[:, c, 0:512],
                             start=(c == 0), stop=(c == KC - 1))
                ins.then_inc(step("wo_a"), 1)

            def project_b(t):
                for c in range(KC):
                    ins = mm(bank[0][:, :], oT[:, c * P:c * P + P], w_out[:, c, 512:1024],
                             start=(c == 0), stop=(c == KC - 1))
                ins.then_inc(step("wo_b"), 1)

            def turn_h2(t):
                done(pe, "h2", t)
                v = h2.rearrange("p (t c) -> p c t", c=KC)
                for c in range(KC):
                    ins = tr(bank[1 + c // 4][:, (c % 4) * P:(c % 4 + 1) * P], v[:, c, :], ident)
                ins.then_inc(step("h2T_mm"), 1)

            def route(t):
                done(pe, "h2T_a", t)
                done(pe, "h2T_b", t)
                for c in range(KC):
                    ins = mm(bank[5][:, 0:36], h2T[:, c * P:c * P + P], rw[:, c, :], start=(c == 0), stop=(c == KC - 1))
                ins.then_inc(step("rt_mm"), 1)

            def tail(t):
                turn_o(t)
                project_a(t)
                freed(pe, "x2", t)
                project_b(t)
                turn_h2(t)
                route(t)

            pe.wait_ge(params, params_all[0])
            pe.wait_ge(consts_in, 32)
            tiles(pe, body, NT)
            low_rank(NT, 0)
            turn_o(NT - 1)
            project_a(NT - 1)
            project_b(NT - 1)
            done(pe, "z", NT)
            done(pe, "s_dn", NT - 1)
            turn_h2(NT - 1)
            route(NT - 1)
            tail(NT)

def experts(nc, ctx, A, O, take, bank, const, masks, x2_d, h2_d, lg_d, y2_d):
    ident = const[:, C_ID:C_ID + P]
    cum = const[:, C_LV + 7 * P:C_LV + 8 * P]
    ones = const[:, C_ONES:C_ONES + P]
    nbefore = const[:, C_NST:C_NST + P]
    iota = const[:, C_IOTA:C_IOTA + P]
    dst_row = masks[:, M_DST:M_DST + 2 * NTT]
    sems = {}

    def step(name):
        if name not in sems:
            sems[name] = ctx.semaphore(name)
        return sems[name]

    held = {e: step(f"held2_{n}") for e, n in ((nc.vector.engine, "dve"), (nc.gpsimd.engine, "pool"),
                                               (nc.sync.engine, "sp"), (nc.scalar.engine, "act"))}

    def hold(eng):
        eng.sem_inc(held[eng.engine], 1)

    NW = 4
    w13 = [take(KC * 512).rearrange("p (c n) -> p c n", c=KC) for _ in range(NW)]
    w2 = [take(2 * D).rearrange("p (c n) -> p c n", c=2) for _ in range(NW)]
    X = [take(D) for _ in range(NW)]
    xT = [take(D).rearrange("p (c t) -> p c t", c=KC) for _ in range(2)]
    Y = [take(D) for _ in range(NW)]
    h1, sg, hT = take(256), take(256), [take(256) for _ in range(2)]
    idx = [[take(1).bitcast(I32) for _ in range(2)] for _ in range(NW)]
    T2 = 2 * NTT
    lg = take(NTT * 36).rearrange("p (t n) -> p t n", n=36)
    oh, S = take(T2 * 32), take((NTT + 1) * 32)
    tmp = take(T2 * 32)
    d4, e4, sel, cand = take(NTT * 4), take(NTT * 4), take(NTT * 8), take(NTT * 8)
    ohg, ohk = take(NTT * 4), [take(NTT * 8) for _ in range(2)]
    mx, mi, m1, m2, pgt = take(NTT), take(NTT), take(NTT), take(NTT), take(NTT)
    gate = take(T2)
    gate_v = gate.rearrange("p (t k) -> p t k", k=2)
    pos, ex_id, lvl, off, tile_of, addr, cmp = (take(T2) for _ in range(7))
    dst_f, multiples, table_f = take(T2), take(LEVEL_MAX), take(TILES)
    slot_hot, tile_hot = take(T2 * P), take(T2 * TILES)
    nT, ovT, cmpT = take(1), take(P), take(P)
    over, ovb = take(64), take(OVER * 32)
    ov_exp, ov_exp_i = take(OVER + 1), take(OVER + 1).bitcast(I32)
    table, tokens = take(TILES).bitcast(I32), take(TILES).bitcast(I32)
    x2 = [take(D) for _ in range(2)]
    y2 = [w2[n].rearrange("p c n -> p (c n)") for n in range(2)]
    fg, fo, fs = take(D), [take(D) for _ in range(2)], take(8)
    eps = take(1)

    def load_w(eng, e, buf, sem):
        eng.dma_start(w13[buf][:, :, 0:256], A["exp_w1"][0, e].rearrange("(p c) n -> p c n", c=KC)).then_inc(sem, 16)
        eng.dma_start(w13[buf][:, :, 256:512], A["exp_w3"][0, e].rearrange("(p c) n -> p c n", c=KC)).then_inc(sem, 16)
        eng.dma_start(w2[buf], A["exp_w2"][0, e].rearrange("(c p) n -> p c n", c=2)).then_inc(sem, 16)

    def weights_in(b):
        return step(f"weights_in{b}")

    def bcast(ap, n, dim=2):
        return ap.unsqueeze(dim).to_broadcast([P] + list(ap.shape[1:dim]) + [n] + list(ap.shape[dim:]))

    with nc.Block() as block:
        @block.sync
        def _(sp):
            sp.wait_ge(step("lg_zero"), 1)
            sp.dma_start(lg[:, 0:NT, :], lg_d[0:NT * P, :].rearrange("(t p) n -> p t n", p=P)).then_inc(step("lg_in"), 16)
            sp.dma_start(lg[0:NS, NT, :], lg_d[NT * P:NT * P + NS, :]).then_inc(step("lg_in"), 16)
            for e in range(NW):
                load_w(sp, e, e, weights_in(e))
            for u in range(2):
                sp.dma_start(x2[u], x2_d[u * P:u * P + P, :]).then_inc(step(f"f_in{u}"), 16)
            sp.dma_start(fg, A["final_norm_g"].partition_broadcast(P)).then_inc(step("fg_in"), 16)

        @block.gpsimd
        def _(pool):
            for b in range(NW):
                ins = nc.gpsimd.memset(X[b], 0.0)
            ins.then_inc(step("x_zero"), 1)
            pool.wait_ge(step("x_zero"), 1)

        @block.scalar
        def _(act):
            one_table(nc)
            act.wait_ge(step("d4"), 1)
            nc.scalar.activation(e4, d4, ACT.Exp).then_inc(step("e4"), 1)
            act.wait_ge(step("d12"), 1)
            nc.scalar.activation(m2, m2, ACT.Exp).then_inc(step("ed"), 1)

        @block.tensor
        def _(pe):
            mm = nc.tensor.matmul
            pe.wait_ge(step("S"), 1)
            mm(bank[0][:, 0:(NTT + 1) * 32], cum, S, start=True, stop=False, skip_group_check=True)
            for t in range(NTT):
                ins = mm(bank[0][:, (t + 1) * 32:(NTT + 1) * 32], ones,
                         S[:, t * 32:t * 32 + 32].unsqueeze(1).to_broadcast([P, NTT - t, 32]),
                         start=False, stop=(t == NTT - 1), skip_group_check=True)
            ins.then_inc(step("pos_mm"), 1)
            for t in range(NTT):
                ins = mm(bank[1][0:32, 0:P], S[:, t * 32:t * 32 + 32], ones, start=(t == 0), stop=(t == NTT - 1))
            ins.then_inc(step("n_mm"), 1)
            pe.wait_ge(step("ovT"), 1)
            mm(bank[2][:, 0:32], ovT[0:32, :], nbefore[0:32, 0:32], start=True, stop=True)
            mm(bank[2][:, 32:64], ovT[0:32, :], ident[0:32, 0:32], start=True, stop=True)
            mm(bank[2][:, 64:65], ovT[0:32, :], ones[0:32, 0:1], start=True, stop=True).then_inc(step("over_mm"), 1)
            for n in range(T2):
                pe.wait_ge(step("hot"), n // (T2 // 3) + 1)
                ins = mm(bank[3][:, 0:TILES], slot_hot[:, n * P:n * P + P], tile_hot[:, n * TILES:n * TILES + TILES],
                         start=(n == 0), stop=(n == T2 - 1))
            ins.then_inc(step("table_mm"), 1)

        @block.vector
        def _(dve):
            v = nc.vector
            tt, ts, red = v.tensor_tensor, v.tensor_scalar, v.tensor_reduce
            n = [0]

            def then(ins):
                ins.then_inc(step("r_chain"), 1)
                n[0] += 1
                dve.wait_ge(step("r_chain"), n[0])

            v.memset(lg[:, NT, :], 0.0).then_inc(step("lg_zero"), 1)
            v.memset(S[:, NTT * 32:], 0.0)
            v.memset(eps, EPS)
            then(v.tensor_copy(dst_f, dst_row))
            then(ts(dst_f, dst_f, -float(NONE), None, ALU.add))
            then(ts(multiples, iota[:, 0:LEVEL_MAX], float(CAP), float(CAP), ALU.mult, ALU.add))
            dve.wait_ge(step("lg_in"), 32)

            def t3(ap, k):
                return ap.rearrange("p (t k) -> p t k", k=k)

            def first_max(out, ap, k, mx):
                then(red(mx, ap, AX, ALU.max))
                then(tt(t3(cand[:, 0:NTT * k], k), ap, bcast(mx, k), ALU.is_ge))
                then(v.scalar_tensor_tensor(t3(cand[:, 0:NTT * k], k), t3(cand[:, 0:NTT * k], k), -64.0,
                                            bcast(iota[:, 0:k], NTT, 1), ALU.mult, ALU.add))
                then(red(mi, t3(cand[:, 0:NTT * k], k), AX, ALU.min))
                then(tt(t3(out, k), t3(cand[:, 0:NTT * k], k), bcast(mi, k), ALU.is_equal))

            first_max(ohg, lg[:, :, 0:4], 4, mx)
            then(tt(t3(d4, 4), lg[:, :, 0:4], bcast(mx, 4), ALU.subtract))
            dve.sem_inc(step("d4"), 1)
            for gi in range(4):
                o = t3(tmp[:, 0:NTT * 32], 32)[:, :, 8 * gi:8 * gi + 8]
                then(tt(o, lg[:, :, 4 + 8 * gi:12 + 8 * gi], bcast(ohg[:, gi::4], 8), ALU.mult))
            for gi in range(4):
                o = t3(tmp[:, 0:NTT * 32], 32)[:, :, 8 * gi:8 * gi + 8]
                if gi == 1:
                    then(tt(t3(sel, 8), t3(tmp[:, 0:NTT * 32], 32)[:, :, 0:8], o, ALU.add))
                elif gi:
                    then(tt(t3(sel, 8), t3(sel, 8), o, ALU.add))
            first_max(ohk[0], t3(sel, 8), 8, m1)
            then(v.scalar_tensor_tensor(sel, ohk[0], -1e30, sel, ALU.mult, ALU.add))
            first_max(ohk[1], t3(sel, 8), 8, m2)
            tt(m2, m2, m1, ALU.subtract).then_inc(step("d12"), 1)
            dve.wait_ge(step("e4"), 1)
            then(red(pgt, t3(e4, 4), AX, ALU.add))
            dve.wait_ge(step("ed"), 1)
            then(v.scalar_tensor_tensor(m1, m2, 1.0, pgt, ALU.add, ALU.mult))
            then(v.reciprocal(mx, m1))
            v.tensor_copy(gate_v[:, :, 0], mx)
            tt(gate_v[:, :, 1], mx, m2, ALU.mult)
            oh4 = oh.rearrange("p (t k e) -> p t k e", k=2, e=32)
            for k in range(2):
                for gi in range(4):
                    then(tt(oh4[:, :, k, 8 * gi:8 * gi + 8], t3(ohk[k], 8), bcast(ohg[:, gi::4], 8), ALU.mult))
            then(ts(oh4[:, NT, :, :], oh4[:, NT, :, :], cum[:, NS - 1:NS], None, ALU.mult))
            tt(t3(S[:, 0:NTT * 32], 32), oh4[:, :, 0, :], oh4[:, :, 1, :], ALU.add).then_inc(step("S"), 1)
            oh3, tmp3 = t3(oh, 32), t3(tmp, 32)
            then(tt(tmp3, oh3, bcast(iota[:, 0:32], T2, 1), ALU.mult))
            then(red(ex_id, tmp3, AX, ALU.add))
            dve.wait_ge(step("pos_mm"), 1)
            for k in range(2):
                then(tt(tmp.rearrange("p (t k e) -> p t k e", k=2, e=32)[:, :, k, :], oh4[:, :, k, :],
                        t3(bank[0][:, 0:NTT * 32], 32), ALU.mult))
            then(red(pos, tmp3, AX, ALU.add))

            def level(out, src, rows):
                w = src.shape[1]
                c3 = tmp[rows, 0:w * LEVEL_MAX].rearrange("p (n k) -> p n k", k=LEVEL_MAX)
                then(tt(c3, src.unsqueeze(2).to_broadcast([src.shape[0], w, LEVEL_MAX]),
                        multiples[rows, :].unsqueeze(1).to_broadcast([src.shape[0], w, LEVEL_MAX]), ALU.is_gt))
                return red(out, c3, AX, ALU.add)

            dve.wait_ge(step("n_mm"), 1)
            then(v.tensor_copy(cmpT[0:32, 0:1], bank[1][0:32, 0:1]))
            then(level(nT[0:32, :], cmpT[0:32, 0:1], slice(0, 32)))
            v.tensor_copy(ovT[0:32, :], nT[0:32, :].to_broadcast([32, P])).then_inc(step("ovT"), 1)
            then(level(lvl, pos, slice(0, P)))
            dve.wait_ge(step("over_mm"), 1)
            then(ts(over[:, 0:32], bank[2][:, 0:32], -1.0, None, ALU.mult))
            then(tt(tmp3, oh3, bcast(over[:, 0:32], T2, 1), ALU.mult))
            then(red(off, tmp3, AX, ALU.add))
            then(tt(off, off, lvl, ALU.add))
            then(tt(off, off, ex_id, ALU.subtract))
            then(ts(off, off, float(N_EXP - 1), None, ALU.add))
            then(ts(cmp, lvl, 0.0, None, ALU.is_gt))
            then(tt(off, off, cmp, ALU.mult))
            then(tt(tile_of, off, ex_id, ALU.add))
            then(ts(cmp, pos, 0.0, -1e6, ALU.is_le, ALU.mult))
            then(tt(tile_of, tile_of, cmp, ALU.add))
            tile3, slot3 = t3(tile_hot, TILES), t3(slot_hot, P)
            then(tt(tile3, bcast(iota[:, 0:TILES], T2, 1), bcast(tile_of, TILES), ALU.is_equal))
            then(v.scalar_tensor_tensor(addr, lvl, -float(CAP), pos, ALU.mult, ALU.add))
            then(ts(addr, addr, -1.0, None, ALU.add))
            tt(tile3, tile3, bcast(dst_f, TILES), ALU.mult)
            for third in range(3):
                N = slice(third * T2 // 3, (third + 1) * T2 // 3)
                tt(slot3[:, N, :], bcast(iota, T2 // 3, 1), bcast(addr[:, N], P), ALU.is_equal).then_inc(step("hot"), 1)
            then(tt(over[:, 32:64], over[:, 0:32], bank[2][:, 32:64], ALU.add))
            ov3 = ovb.rearrange("p (j e) -> p j e", e=32)
            then(tt(ov3, bcast(over[:, 32:64], OVER, 1), bcast(iota[:, 0:OVER], 32), ALU.is_le))
            then(red(ov_exp[:, 0:OVER], ov3, AX, ALU.add))
            then(v.tensor_copy(ov_exp[:, OVER:OVER + 1], bank[2][:, 64:65]))
            then(v.tensor_copy(ov_exp_i, ov_exp))
            dve.wait_ge(step("table_mm"), 1)
            then(ts(table_f, bank[3][:, 0:TILES], float(NONE), None, ALU.add))
            then(v.tensor_copy(table, table_f))
            then(ts(tokens, table, 1, None, ALU.logical_shift_right))

    with nc.Block() as block:
        def loop(eng, body, first=4, last=4):
            for e in range(first):
                body(e, e)
            with eng.Fori(1, N_EXP // NW - 1) as i:
                for u in range(NW):
                    body(i * NW + u, u)
            for e in range(N_EXP - last, N_EXP):
                body(e, e % NW)

        AHEAD = 3

        def after(eng, name, e, back=0, per=1, n=None):
            wait_earlier(eng, step(name), e, back, per, n)

        def in_buffer(eng, name, e, u):
            eng.wait_ge(step(f"{name}{u}"), (e - u) * (16 // NW) + 16)

        def out_of_buffer(eng, name, e, u):
            if not isinstance(e, int):
                eng.wait_ge(step(f"{name}{u}"), (e - u) * (16 // NW))
            elif e >= NW:
                eng.wait_ge(step(f"{name}{u}"), (e - u) * (16 // NW))

        @block.sync
        def _(sp):
            def body(e, u):
                after(sp, "mm2", e)
                hold(sp)
                load_w(sp, e + NW, u, weights_in(u))

            for e in range(NW):
                body(e, e)
            with sp.Fori(1, N_EXP // NW - 1) as i:
                for u in range(NW):
                    body(i * NW + u, u)

        @block.gpsimd
        def _(pool):
            g = nc.gpsimd

            def gather(e, u):
                after(pool, "idx", e)
                after(pool, "xT_mm", e, NW)
                hold(pool)
                pool.indirect_dma_start(X[u], None, h2_d, bass.IndirectOffsetOnAxis(ap=idx[u][0], axis=0),
                                        bounds_check=NT * P + NS - 1, oob_is_err=False
                                        ).then_inc(step(f"xg_in{u}"), 16)

            def scatter(e, u):
                after(pool, "odx", e)
                after(pool, "y_a", e)
                after(pool, "y_b", e)
                hold(pool)
                pool.indirect_dma_start(y2_d, bass.IndirectOffsetOnAxis(ap=idx[u][1], axis=0), Y[u], None,
                                        bounds_check=2 * (NT * P + NS) - 1, oob_is_err=False
                                        ).then_inc(step(f"y_out{u}"), 16)

            def body(e, u):
                if not (isinstance(e, int) and e >= N_EXP - AHEAD):
                    gather(e + AHEAD, (u + AHEAD) % NW)
                if not (isinstance(e, int) and e == 0):
                    scatter(e - 1, (u - 1) % NW)

            for e in range(AHEAD):
                gather(e, e)
            loop(pool, body)
            scatter(N_EXP - 1, NW - 1)
            for b in range(NW):
                pool.wait_ge(step(f"y_out{b}"), 16 * (N_EXP // NW))

        @block.scalar
        def _(act):
            one_table(nc)
            a = nc.scalar.activation

            def put_xT(e, u):
                after(act, "xT_mm", e)
                after(act, "mm1", e, 2)
                a(xT[u % 2][:, 0:4, :], bank[0][:, :].rearrange("p (c t) -> p c t", c=4), ACT.Copy
                  ).then_inc(step("xT_a"), 1)

            def put_y(e, u):
                after(act, "mm2", e)
                out_of_buffer(act, "y_out", e, u)
                a(Y[u][:, 0:512], bank[4 + 2 * (u % 2)][:, :], ACT.Copy).then_inc(step("y_a"), 1)

            def silu(e, u):
                after(act, "h_clamp", e)
                a(sg, h1, ACT.Exp, scale=-1.0).then_inc(step("sig"), 1)
                after(act, "sig", e, 0, 3, 1)
                a(sg, sg, ACT.Ln, bias=1.0).then_inc(step("sig"), 1)
                after(act, "sig", e, 0, 3, 2)
                a(sg, sg, ACT.Exp, scale=-1.0).then_inc(step("sig"), 1)

            def body(e, u):
                if not (isinstance(e, int) and e == N_EXP - 1):
                    put_xT(e + 1, u + 1)
                silu(e, u)
                if not (isinstance(e, int) and e == 0):
                    put_y(e - 1, u - 1 if u else NW - 1)

            put_xT(0, 0)
            loop(act, body)
            put_y(N_EXP - 1, NW - 1)

        @block.vector
        def _(dve):
            v = nc.vector

            def indices(e, u):
                out_of_buffer(dve, "xg_in", e, u)
                hold(dve)
                v.tensor_copy(idx[u][0], tokens[:, bass.ds(e, 1)]).then_inc(step("idx"), 1)

            def out_rows(e, u):
                out_of_buffer(dve, "y_out", e, u)
                hold(dve)
                v.tensor_copy(idx[u][1], table[:, bass.ds(e, 1)]).then_inc(step("odx"), 1)

            def put_xT(e, u):
                after(dve, "xT_mm", e)
                after(dve, "mm1", e, 2)
                v.tensor_copy(xT[u % 2][:, 4:8, :], bank[1][:, :].rearrange("p (c t) -> p c t", c=4)
                              ).then_inc(step("xT_b"), 1)

            def put_y(e, u):
                after(dve, "mm2", e)
                out_of_buffer(dve, "y_out", e, u)
                v.tensor_copy(Y[u][:, 512:1024], bank[5 + 2 * (u % 2)][:, :]).then_inc(step("y_b"), 1)

            def silu(e, u):
                h = bank[2 + u % 2]
                after(dve, "mm1", e)
                after(dve, "h", e, 1)
                v.tensor_scalar(h1, h[:, 0:256], CLAMP, None, ALU.max).then_inc(step("h_clamp"), 1)
                after(dve, "sig", e, 0, 3, 3)
                after(dve, "h_clamp", e)
                after(dve, "mm2", e, 2)
                v.tensor_tensor(h1, h1, h[:, 256:512], ALU.mult).then_inc(step("h13"), 1)
                after(dve, "h13", e)
                v.tensor_tensor(hT[u % 2], h1, sg, ALU.mult).then_inc(step("h"), 1)

            def body(e, u):
                if not (isinstance(e, int) and e >= N_EXP - AHEAD):
                    indices(e + AHEAD, (u + AHEAD) % NW)
                if not (isinstance(e, int) and e == N_EXP - 1):
                    put_xT(e + 1, u + 1)
                silu(e, u)
                out_rows(e, u)
                if not (isinstance(e, int) and e == 0):
                    put_y(e - 1, u - 1 if u else NW - 1)

            for e in range(AHEAD):
                indices(e, e)
            put_xT(0, 0)
            loop(dve, body)
            put_y(N_EXP - 1, NW - 1)

        @block.tensor
        def _(pe):
            mm, tr = nc.tensor.matmul, nc.tensor.transpose

            def transposes(e, u):
                in_buffer(pe, "xg_in", e, u % NW)
                after(pe, "xT_a", e, 1)
                after(pe, "xT_b", e, 1)
                x = X[u % NW].rearrange("p (t c) -> p c t", c=KC)
                for c in range(KC):
                    ins = tr(bank[c // 4][:, (c % 4) * P:(c % 4 + 1) * P], x[:, c, :], ident)
                ins.then_inc(step("xT_mm"), 1)

            def mm1(e, u):
                after(pe, "xT_a", e)
                after(pe, "xT_b", e)
                pe.wait_ge(weights_in(u % NW), (e - u) * (48 // NW) + 48)
                after(pe, "h13", e, 2)
                for j in range(4):
                    for c in range(KC):
                        ins = mm(bank[2 + u % 2][:, j * P:(j + 1) * P], w13[u][:, c, j * P:(j + 1) * P],
                                 xT[u % 2][:, c, :], start=(c == 0), stop=(c == KC - 1))
                ins.then_inc(step("mm1"), 1)

            def mm2(e, u):
                after(pe, "h", e)
                after(pe, "y_a", e, 2)
                after(pe, "y_b", e, 2)
                for b in range(2):
                    for c in range(2):
                        ins = mm(bank[4 + 2 * (u % 2) + b][:, :], hT[u % 2][:, c * P:(c + 1) * P],
                                 w2[u][:, c, 512 * b:512 * b + 512], start=(c == 0), stop=(c == 1))
                ins.then_inc(step("mm2"), 1)

            def body(e, u):
                if not (isinstance(e, int) and e == N_EXP - 1):
                    transposes(e + 1, u + 1)
                mm1(e, u)
                if not (isinstance(e, int) and e == 0):
                    mm2(e - 1, u - 1 if u else NW - 1)

            transposes(0, 0)
            loop(pe, body)
            mm2(N_EXP - 1, NW - 1)

    with nc.Block() as block:
        def further(eng, body):
            count = eng.value_load(ov_exp_i[0:1, OVER:OVER + 1], min_val=0, max_val=OVER)
            with eng.If(count > 0):
                with eng.Fori(0, count) as i:
                    body(i)

        @block.sync
        def _(sp):
            def body(i):
                sp.wait_ge(step("o_mm2"), i + 1)
                hold(sp)
                e = sp.value_load(ov_exp_i[0:1, bass.ds(i, 1)], min_val=0, max_val=N_EXP - 1)
                s = step("o_weights")
                w1v = A["exp_w1"][0].rearrange("e (p c) n -> e p c n", c=KC)
                w3v = A["exp_w3"][0].rearrange("e (p c) n -> e p c n", c=KC)
                w2v = A["exp_w2"][0].rearrange("e (c p) n -> e p c n", c=2)
                sp.dma_start(w13[0][:, :, 0:256], w1v[bass.ds(e, 1)]).then_inc(s, 16)
                sp.dma_start(w13[0][:, :, 256:512], w3v[bass.ds(e, 1)]).then_inc(s, 16)
                sp.dma_start(w2[0], w2v[bass.ds(e, 1)]).then_inc(s, 16)

            further(sp, body)

        @block.gpsimd
        def _(pool):
            def body(i):
                pool.wait_ge(step("o_idx"), i + 1)
                hold(pool)
                pool.indirect_dma_start(X[0], None, h2_d, bass.IndirectOffsetOnAxis(ap=idx[0][0], axis=0),
                                        bounds_check=NT * P + NS - 1, oob_is_err=False).then_inc(step("o_x"), 16)
                pool.wait_ge(step("o_y"), i + 1)
                hold(pool)
                pool.indirect_dma_start(y2_d, bass.IndirectOffsetOnAxis(ap=idx[0][1], axis=0), Y[0], None,
                                        bounds_check=2 * (NT * P + NS) - 1, oob_is_err=False
                                        ).then_inc(step("o_stored"), 16)
                pool.wait_ge(step("o_stored"), i * 16 + 16)
                pool.sem_inc(step("o_done"), 1)

            pool.sem_inc(step("o_done"), 1)
            further(pool, body)

        @block.scalar
        def _(act):
            one_table(nc)
            a = nc.scalar.activation

            def body(i):
                act.wait_ge(step("o_clamp"), i + 1)
                a(sg, h1, ACT.Exp, scale=-1.0).then_inc(step("o_sig"), 1)
                act.wait_ge(step("o_sig"), i * 3 + 1)
                a(sg, sg, ACT.Ln, bias=1.0).then_inc(step("o_sig"), 1)
                act.wait_ge(step("o_sig"), i * 3 + 2)
                a(sg, sg, ACT.Exp, scale=-1.0).then_inc(step("o_sig"), 1)

            further(act, body)

        @block.vector
        def _(dve):
            v = nc.vector

            def body(i):
                dve.wait_ge(step("o_done"), i + 1)
                hold(dve)
                v.tensor_copy(idx[0][0], tokens[:, bass.ds(i + N_EXP, 1)])
                v.tensor_copy(idx[0][1], table[:, bass.ds(i + N_EXP, 1)]).then_inc(step("o_idx"), 1)
                dve.wait_ge(step("o_xT_mm"), i + 1)
                for b in range(2):
                    ins = v.tensor_copy(xT[0][:, 4 * b:4 * b + 4, :], bank[b][:, :].rearrange("p (c t) -> p c t", c=4))
                ins.then_inc(step("o_xT"), 1)
                dve.wait_ge(step("o_mm1"), i + 1)
                v.tensor_scalar(h1, bank[2][:, 0:256], CLAMP, None, ALU.max).then_inc(step("o_clamp"), 1)
                dve.wait_ge(step("o_sig"), i * 3 + 3)
                v.tensor_tensor(h1, h1, bank[2][:, 256:512], ALU.mult).then_inc(step("o_h13"), 1)
                dve.wait_ge(step("o_h13"), i + 1)
                v.tensor_tensor(hT[0], h1, sg, ALU.mult).then_inc(step("o_h"), 1)
                dve.wait_ge(step("o_mm2"), i + 2)
                for b in range(2):
                    ins = v.tensor_copy(Y[0][:, 512 * b:512 * b + 512], bank[4 + b][:, :])
                ins.then_inc(step("o_y"), 1)

            further(dve, body)

        @block.tensor
        def _(pe):
            mm, tr = nc.tensor.matmul, nc.tensor.transpose

            def body(i):
                pe.wait_ge(step("o_x"), i * 16 + 16)
                x = X[0].rearrange("p (t c) -> p c t", c=KC)
                for c in range(KC):
                    ins = tr(bank[c // 4][:, (c % 4) * P:(c % 4 + 1) * P], x[:, c, :], ident)
                ins.then_inc(step("o_xT_mm"), 1)
                pe.wait_ge(step("o_xT"), i + 1)
                pe.wait_ge(step("o_weights"), i * 48 + 48)
                for j in range(4):
                    for c in range(KC):
                        ins = mm(bank[2][:, j * P:(j + 1) * P], w13[0][:, c, j * P:(j + 1) * P],
                                 xT[0][:, c, :], start=(c == 0), stop=(c == KC - 1))
                ins.then_inc(step("o_mm1"), 1)
                pe.wait_ge(step("o_h"), i + 1)
                for b in range(2):
                    for c in range(2):
                        ins = mm(bank[4 + b][:, :], hT[0][:, c * P:(c + 1) * P],
                                 w2[0][:, c, 512 * b:512 * b + 512], start=(c == 0), stop=(c == 1))
                ins.then_inc(step("o_mm2"), 1)

            pe.sem_inc(step("o_mm2"), 1)
            further(pe, body)

    with nc.Block() as block:
        out = O[0].rearrange("b s d -> (b s) d")
        out_s = O[1].rearrange("b s d -> (b s) d")

        @block.sync
        def _(sp):
            for t in range(NTT):
                u, rows = t % 2, slice(t * P, t * P + P) if t < NT else slice(NT * P, NT * P + NS)
                n = rows.stop - rows.start
                wait_earlier(sp, step("f_sum"), t, 2)
                if t >= 2:
                    sp.dma_start(x2[u][0:n, :], x2_d[rows, :]).then_inc(step(f"f_in{u}"), 16)
                sp.dma_start(y2[u][0:n, :], y2_d[2 * rows.start:2 * rows.stop, :].rearrange("(p k) d -> p (k d)", k=2)
                             ).then_inc(step(f"f_in{u}"), 16)

        @block.gpsimd
        def _(pool):
            for t in range(NTT):
                u = t % 2
                pool.wait_ge(step("f_out"), t + 1)
                if t < NT:
                    pool.dma_start(out[t * P:(t + 1) * P, :], fo[u]).then_inc(step(f"f_stored{u}"), 16)
                else:
                    pool.dma_start(out_s, fo[u][0:NS, :]).then_inc(step(f"f_stored{u}"), 16)
            pool.wait_ge(step("f_stored0"), 16 * (NT // 2 + 1))
            pool.wait_ge(step("f_stored1"), 16 * (NT // 2))

        @block.scalar
        def _(act):
            one_table(nc)
            a = nc.scalar.activation
            for t in range(NTT):
                R = slice(0, P if t < NT else NS)
                u = t % 2
                act.wait_ge(step("f_sum"), t + 1)
                if t:
                    act.wait_ge(step("f_rs"), 3 * t)
                    act.wait_ge(step("f_out"), t)
                a(X[0][R, :], Y[u][R, :], ACT.Square, accum_out=fs[R, 0:1]).then_inc(step("f_rs"), 1)
                act.wait_ge(step("f_rs"), 3 * t + 1)
                a(fs[R, 1:2], fs[R, 0:1], ACT.Ln, scale=1.0 / D, bias=eps[R, :]).then_inc(step("f_rs"), 1)
                act.wait_ge(step("f_rs"), 3 * t + 2)
                a(fs[R, 2:3], fs[R, 1:2], ACT.Exp, scale=-0.5).then_inc(step("f_rs"), 1)

        @block.vector
        def _(dve):
            v = nc.vector
            dve.wait_ge(step("fg_in"), 16)
            for t in range(NTT):
                R, u = slice(0, P if t < NT else NS), t % 2
                dve.wait_ge(step(f"f_in{u}"), 32 * (t // 2 + 1))
                if t >= 2:
                    dve.wait_ge(step("f_out"), t - 1)
                v.scalar_tensor_tensor(X[1][R, :], y2[u][R, 0:D], gate[R, 2 * t:2 * t + 1], x2[u][R, :],
                                       ALU.mult, ALU.add).then_inc(step("f_half"), 1)
                dve.wait_ge(step("f_half"), t + 1)
                v.scalar_tensor_tensor(Y[u][R, :], y2[u][R, D:2 * D], gate[R, 2 * t + 1:2 * t + 2], X[1][R, :],
                                       ALU.mult, ALU.add).then_inc(step("f_sum"), 1)
                dve.wait_ge(step("f_rs"), 3 * t + 3)
                dve.wait_ge(step("f_sum"), t + 1)
                if t >= 2:
                    dve.wait_ge(step(f"f_stored{u}"), 16 * (t // 2))
                v.scalar_tensor_tensor(fo[u][R, :], Y[u][R, :], fs[R, 2:3], fg[R, :], ALU.mult, ALU.mult
                                       ).then_inc(step("f_out"), 1)


_INS = ['x_prompt', 'x_sample', 'state_gla', 'state_dn', 'state_conv', 'state_hgrn', 'norm1_g', 'w_in', 'gla_wa2',
        'gla_ba', 'gla_norm_g', 'dn_conv_w', 'dn_a_log', 'dn_dt_bias', 'dn_norm_g', 'hg_lb_logits', 'hg_norm_g',
        'w_out', 'norm2_g', 'router_g_w', 'router_g_b', 'router_e_w', 'router_e_b', 'exp_w1', 'exp_w3', 'exp_w2',
        'final_norm_g']
_OUTS = [(1, SEQ, D), (NS, 1, D), (1, 1, H_GLA, DK_GLA, DV), (1, 1, H_DN, DK_DN, DV), (1, 1, 3, CONV),
         (1, 1, H_HG, DK_HG, DV), (1, NS, H_GLA, DK_GLA, DV), (1, NS, H_DN, DK_DN, DV), (1, NS, 3, CONV),
         (1, NS, H_HG, DK_HG, DV)]


def kernel(**inputs):
    import numpy as _np
    import concourse.bacc as _bacc
    from concourse.bass_utils import run_bass_kernel_spmd as _run

    nc = _bacc.Bacc("TRN2", target_bir_lowering=False, num_devices=1)
    arrays, ins = {}, {}
    given = {name: _np.ascontiguousarray(inputs[name]) for name in _INS}
    given["shape_consts"], given["shape_masks"] = shape_constants()
    for name, a in given.items():
        arrays[f"in_{name}"] = a
        ins[name] = nc.dram_tensor(f"in_{name}", a.shape, mybir.dt.from_np(a.dtype), kind="ExternalInput").ap()
    outs = [nc.dram_tensor(f"out_{i}", s, F32, kind="ExternalOutput").ap() for i, s in enumerate(_OUTS)]
    build(nc, ins, outs)
    r = _run(nc, [arrays], core_ids=[0])
    return tuple(r.results[0][f"out_{i}"] for i in range(len(_OUTS)))
```
